# Optimizing a Trainium2 kernel written in Bass

```python
import math
import jax, jax.numpy as jnp
from jax import lax
import numpy as np

D_MODEL = 1024
BATCH = 1
SEQ = 256
DEPTH = 4
DEC_BATCH = 1
DEC_SEQ = 512
PAST_LEN = 128

N_MIXERS = 3
N_A = (DEPTH + 2) // 3
N_B = (DEPTH + 1) // 3
N_C = DEPTH // 3
W_TOK = D_MODEL
N_MEM = 256
MEM_HEADS = 4
MEM_HEAD_DIM = 64
W_MEM = MEM_HEADS * MEM_HEAD_DIM
W_BRANCH = W_TOK + W_MEM
CONV_WIDTH = 31
RWKV_HEAD = 64
RWKV_HEADS = W_TOK // RWKV_HEAD
RANK_W = 64
RANK_A = 64
P_B = 3 * W_TOK + RANK_W + RANK_A
NA_HEAD_DIM = 64
NA_HEADS = W_TOK // NA_HEAD_DIM
GRID_W = 64
WIN_R = 8
WIN_C = 16
IN_A = 2 * W_TOK + W_MEM + W_BRANCH
IN_B = P_B + W_MEM + W_BRANCH
IN_C = 3 * W_TOK + W_MEM + W_BRANCH
RMS_EPS = 1e-6
LN_EPS = 1e-5
GN_EPS = 64e-5
DECAY_SCALE = math.exp(-0.5)
NEG_INF = -1e30

kernel_name = "hybrid_conv_rwkv7_natten_encoder"

def rms_norm(x, g):
    x32 = x.astype(jnp.float32)
    y = x32 * lax.rsqrt(jnp.mean(x32 * x32, -1, keepdims=True) + RMS_EPS)
    return (y * g.astype(jnp.float32)).astype(x.dtype)

def layer_norm(x, g, b):
    x32 = x.astype(jnp.float32)
    mean = jnp.mean(x32, -1, keepdims=True)
    var = jnp.mean(jnp.square(x32 - mean), -1, keepdims=True)
    y = (x32 - mean) * lax.rsqrt(var + LN_EPS) * g.astype(jnp.float32) + b.astype(jnp.float32)
    return y.astype(x.dtype)

def mixer_conv(h, conv_w, conv_b, ln_g, ln_b):
    z = h[..., :W_TOK] * jax.nn.sigmoid(h[..., W_TOK:])
    z = lax.conv_general_dilated(z, conv_w[:, None, :], (1,), [(CONV_WIDTH // 2, CONV_WIDTH // 2)],
                                 dimension_numbers=('NWC', 'WIO', 'NWC'), feature_group_count=W_TOK) + conv_b
    return jax.nn.silu(layer_norm(z, ln_g, ln_b))

def wkv_scan(r, w, kk, b, v, k, reverse):
    bsz, _, nh, n = r.shape
    xs = tuple(jnp.swapaxes(z, 0, 1) for z in (r, w, kk, b, v, k))

    def step(S, inp):
        r_t, w_t, kk_t, b_t, v_t, k_t = inp
        sa = jnp.einsum('bhvk,bhk->bhv', S, kk_t)
        S = S * w_t[:, :, None, :] - sa[..., None] * b_t[:, :, None, :] + v_t[..., None] * k_t[:, :, None, :]
        return S, jnp.einsum('bhvk,bhk->bhv', S, r_t)

    S0 = jnp.zeros((bsz, nh, n, n), jnp.float32)
    _, ys = lax.scan(step, S0, xs, reverse=reverse)
    return jnp.swapaxes(ys, 0, 1)

def mixer_rwkv(p, mu, w0, w_up, a0, a_up, k_k, k_a, r_k, ln_g, ln_b):
    f32 = jnp.float32
    bsz, t, _ = p.shape
    hs = (bsz, t, RWKV_HEADS, RWKV_HEAD)
    shifted = (jnp.pad(p, ((0, 0), (1, 0), (0, 0)))[:, :t],
               jnp.pad(p, ((0, 0), (0, 1), (0, 0)))[:, 1:])
    kg = k_k.astype(f32).reshape(RWKV_HEADS, RWKV_HEAD)
    ka = k_a.astype(f32).reshape(RWKV_HEADS, RWKV_HEAD)
    rk = r_k.astype(f32)
    wkv = []
    bonus = []
    for d in range(2):
        xd = p + mu[d] * (shifted[d] - p)
        r = xd[..., :W_TOK]
        k = xd[..., W_TOK:2 * W_TOK]
        v = xd[..., 2 * W_TOK:3 * W_TOK]
        wd = xd[..., 3 * W_TOK:3 * W_TOK + RANK_W]
        ad = xd[..., 3 * W_TOK + RANK_W:]
        decay = jnp.exp(-DECAY_SCALE * jax.nn.sigmoid((w0[d] + jnp.tanh(wd) @ w_up[d]).astype(f32)))
        a = jax.nn.sigmoid((a0[d] + ad @ a_up[d]).astype(f32))
        r, k, v, decay, a = (z.astype(f32).reshape(hs) for z in (r, k, v, decay, a))
        kk = k * kg
        kk = kk * lax.rsqrt(jnp.maximum(jnp.sum(kk * kk, -1, keepdims=True), 1e-24))
        k_eff = k * (1.0 + (a - 1.0) * ka)
        wkv.append(wkv_scan(r, decay, kk, kk * a, v, k_eff, d == 1))
        bonus.append(jnp.sum(r * k_eff * rk, -1, keepdims=True) * v)
    y = wkv[0] + wkv[1]
    mean = jnp.mean(y, -1, keepdims=True)
    var = jnp.mean(jnp.square(y - mean), -1, keepdims=True)
    y = (y - mean) * lax.rsqrt(var + GN_EPS)
    y = y.reshape(bsz, t, W_TOK) * ln_g.astype(f32) + ln_b.astype(f32) + (bonus[0] + bonus[1]).reshape(bsz, t, W_TOK)
    return y.astype(p.dtype)

def mixer_natten(qkv, rpb):
    f32 = jnp.float32
    bsz, t, _ = qkv.shape
    rows = t // GRID_W
    kr = min(WIN_R, rows)
    gs = (bsz, rows, GRID_W, NA_HEADS, NA_HEAD_DIM)
    q = (qkv[..., :W_TOK] * NA_HEAD_DIM ** -0.5).reshape(gs)
    k = qkv[..., W_TOK:2 * W_TOK].reshape(gs)
    v = qkv[..., 2 * W_TOK:].reshape(gs)
    cols = np.arange(GRID_W)
    col_start = np.clip(cols - WIN_C // 2, 0, GRID_W - WIN_C)
    col_mask = (cols[None, :] >= col_start[:, None]) & (cols[None, :] < col_start[:, None] + WIN_C)
    col_idx = np.clip(cols[None, :] - cols[:, None], -(WIN_C - 1), WIN_C - 1) + WIN_C - 1
    rpb_cols = rpb[:, :, col_idx]

    def row_block(r):
        s = jnp.clip(r - kr // 2, 0, rows - kr)
        qr = lax.dynamic_index_in_dim(q, r, axis=1, keepdims=False)
        kb = lax.dynamic_slice_in_dim(k, s, kr, axis=1)
        vb = lax.dynamic_slice_in_dim(v, s, kr, axis=1)
        sc = jnp.einsum('bqhd,bikhd->bhqik', qr, kb, preferred_element_type=f32)
        bias = jnp.take(rpb_cols, s - r + jnp.arange(kr) + WIN_R - 1, axis=1)
        sc = sc + jnp.transpose(bias, (0, 2, 1, 3)).astype(f32)[None]
        sc = jnp.where(col_mask[None, None, :, None, :], sc, NEG_INF)
        pr = jax.nn.softmax(sc.reshape(bsz, NA_HEADS, GRID_W, kr * GRID_W), -1).reshape(sc.shape)
        return jnp.einsum('bhqik,bikhd->bqhd', pr.astype(vb.dtype), vb)

    out = lax.map(row_block, jnp.arange(rows))
    return jnp.moveaxis(out, 0, 1).reshape(bsz, t, W_TOK)

def memory_attention(qm, mem, g, w_kv):
    bsz, t, _ = qm.shape
    m = mem.shape[1]
    kv = rms_norm(mem, g) @ w_kv
    mk = kv[..., :W_MEM].reshape(bsz, m, MEM_HEADS, MEM_HEAD_DIM)
    mv = kv[..., W_MEM:].reshape(bsz, m, MEM_HEADS, MEM_HEAD_DIM)
    q = (qm * MEM_HEAD_DIM ** -0.5).reshape(bsz, t, MEM_HEADS, MEM_HEAD_DIM)
    sc = jnp.einsum('bthd,bmhd->bhtm', q, mk, preferred_element_type=jnp.float32)
    pr = jax.nn.softmax(sc, -1).astype(mv.dtype)
    return jnp.einsum('bhtm,bmhd->bthd', pr, mv).reshape(bsz, t, W_MEM)

def trunk(x, mem, pre_norm, post_norm, mem_norm, w_mem_kv,
          a_w_in, a_conv_w, a_conv_b, a_ln_g, a_ln_b, a_w_out,
          b_w_in, b_mu, b_w0, b_w_up, b_a0, b_a_up, b_k_k, b_k_a, b_r_k, b_ln_g, b_ln_b, b_w_out,
          c_w_in, c_rpb, c_w_out):
    for l in range(DEPTH):
        kind, j = l % N_MIXERS, l // N_MIXERS
        hn = rms_norm(x, pre_norm[l])
        if kind == 0:
            h = hn @ a_w_in[j]
            nc = 2 * W_TOK
            tok = mixer_conv(h[..., :nc], a_conv_w[j], a_conv_b[j], a_ln_g[j], a_ln_b[j])
            w_out = a_w_out[j]
        elif kind == 1:
            h = hn @ b_w_in[j]
            nc = P_B
            tok = mixer_rwkv(h[..., :nc], b_mu[j], b_w0[j], b_w_up[j], b_a0[j], b_a_up[j],
                             b_k_k[j], b_k_a[j], b_r_k[j], b_ln_g[j], b_ln_b[j])
            w_out = b_w_out[j]
        else:
            h = hn @ c_w_in[j]
            nc = 3 * W_TOK
            tok = mixer_natten(h[..., :nc], c_rpb[j])
            w_out = c_w_out[j]
        mo = memory_attention(h[..., nc:nc + W_MEM], mem, mem_norm[l], w_mem_kv[l])
        gate = h[..., nc + W_MEM:]
        br = jnp.concatenate([tok.astype(h.dtype), mo], -1) * jax.nn.silu(gate)
        x = x + rms_norm(br @ w_out, post_norm[l])
    return x

def setup_inputs(seed: int = 0) -> dict:
    key = jax.random.key(seed)
    ks = jax.random.split(key, 32)
    f32 = jnp.float32

    def nrm(k, shape, scale):
        return jax.random.normal(k, shape, f32) * scale

    D = D_MODEL
    return {
        "x_prompt": nrm(ks[0], (BATCH, SEQ, D), 1.0),
        "x_sample": nrm(ks[1], (DEC_BATCH, DEC_SEQ, D), 1.0),
        "mem_prompt": nrm(ks[2], (BATCH, N_MEM, D), 1.0),
        "mem_sample": nrm(ks[3], (DEC_BATCH, N_MEM, D), 1.0),
        "pre_norm": 1.0 + nrm(ks[4], (DEPTH, D), 0.02),
        "post_norm": 1.0 + nrm(ks[5], (DEPTH, D), 0.02),
        "mem_norm": 1.0 + nrm(ks[6], (DEPTH, D), 0.02),
        "w_mem_kv": nrm(ks[7], (DEPTH, D, 2 * W_MEM), D ** -0.5),
        "a_w_in": nrm(ks[8], (N_A, D, IN_A), D ** -0.5),
        "a_conv_w": nrm(ks[9], (N_A, CONV_WIDTH, W_TOK), CONV_WIDTH ** -0.5),
        "a_conv_b": nrm(ks[10], (N_A, W_TOK), 0.02),
        "a_ln_g": 1.0 + nrm(ks[11], (N_A, W_TOK), 0.02),
        "a_ln_b": nrm(ks[12], (N_A, W_TOK), 0.02),
        "a_w_out": nrm(ks[13], (N_A, W_BRANCH, D), W_BRANCH ** -0.5),
        "b_w_in": nrm(ks[14], (N_B, D, IN_B), D ** -0.5),
        "b_mu": jax.random.uniform(ks[15], (N_B, 2, P_B), f32),
        "b_w0": nrm(ks[16], (N_B, 2, W_TOK), 0.5),
        "b_w_up": nrm(ks[17], (N_B, 2, RANK_W, W_TOK), 0.5 * RANK_W ** -0.5),
        "b_a0": nrm(ks[18], (N_B, 2, W_TOK), 0.3),
        "b_a_up": nrm(ks[19], (N_B, 2, RANK_A, W_TOK), 0.5 * RANK_A ** -0.5),
        "b_k_k": 0.85 + nrm(ks[20], (N_B, W_TOK), 0.05),
        "b_k_a": 1.0 + nrm(ks[21], (N_B, W_TOK), 0.05),
        "b_r_k": nrm(ks[22], (N_B, RWKV_HEADS, RWKV_HEAD), 0.1),
        "b_ln_g": 1.0 + nrm(ks[23], (N_B, W_TOK), 0.02),
        "b_ln_b": nrm(ks[24], (N_B, W_TOK), 0.02),
        "b_w_out": nrm(ks[25], (N_B, W_BRANCH, D), W_BRANCH ** -0.5),
        "c_w_in": nrm(ks[26], (N_C, D, IN_C), D ** -0.5),
        "c_rpb": nrm(ks[27], (N_C, NA_HEADS, 2 * WIN_R - 1, 2 * WIN_C - 1), 0.1),
        "c_w_out": nrm(ks[28], (N_C, W_BRANCH, D), W_BRANCH ** -0.5),
    }

def reference(x_prompt, x_sample, mem_prompt, mem_sample, pre_norm, post_norm, mem_norm, w_mem_kv,
              a_w_in, a_conv_w, a_conv_b, a_ln_g, a_ln_b, a_w_out,
              b_w_in, b_mu, b_w0, b_w_up, b_a0, b_a_up, b_k_k, b_k_a, b_r_k, b_ln_g, b_ln_b, b_w_out,
              c_w_in, c_rpb, c_w_out):
    weights = (pre_norm, post_norm, mem_norm, w_mem_kv,
               a_w_in, a_conv_w, a_conv_b, a_ln_g, a_ln_b, a_w_out,
               b_w_in, b_mu, b_w0, b_w_up, b_a0, b_a_up, b_k_k, b_k_a, b_r_k, b_ln_g, b_ln_b, b_w_out,
               c_w_in, c_rpb, c_w_out)
    y_prompt = trunk(x_prompt, mem_prompt, *weights)
    y_sample = trunk(x_sample, mem_sample, *weights)
    return (y_prompt, y_sample)


_drawn_inputs = setup_inputs


def setup_inputs(seed=0):
    import zlib

    import numpy as np

    out = dict(_drawn_inputs(seed))
    spreads = {}
    factors = {'mem_norm': 8.0,
     'b_k_k': 21.907,
     'b_ln_g': 3.752,
     'b_ln_b': 7.703,
     'a_ln_g': 3.343,
     'a_ln_b': 4.075,
     'c_rpb': 8.0}
    for name, (base, spread) in spreads.items():
        noise = np.random.default_rng([zlib.crc32(name.encode()), seed]).standard_normal(out[name].shape)
        drawn = base * np.exp(spread * noise) if base else spread * noise
        out[name] = __import__('jax').numpy.asarray(drawn.astype(out[name].dtype))
    for name, factor in factors.items():
        out[name] = (out[name] * factor).astype(out[name].dtype)
    return out
```

```python
import math
from contextlib import ExitStack

import concourse.bass as bass
import numpy as np
from concourse import mybir

F32 = mybir.dt.float32
ACT = mybir.ActivationFunctionType
ALU = mybir.AluOpType
AX_X = mybir.AxisListType.X

P = 128
D = 1024
KD = D // P
GROUPS = ((0, 256), (256, 512))
T = 768
MEM = 512
KB = (D + 256) // P
KINDS = (0, 1, 2, 0)
TAPS = 31
HALO = TAPS // 2
CONV_IN = T + 4 * HALO
CONV_OUT = CONV_IN - 2 * HALO
CONV_AT = (0, 256 + 2 * HALO)
RMS_EPS, LN_EPS, GN_EPS = 1e-6, 1e-5, 64e-5
DECAY = math.exp(-0.5)
HEAD_SCALE = 64 ** -0.5
C = 64
QUAD = 4
WT = T + 1
WKV_AT = (0, 257)
LEVELS = 6
BPAR = 15
MU, W0, A0, KG, KA, RK, LNG, LNB = 0, 6, 8, 10, 11, 12, 13, 14
APAR = TAPS + 3
NEG = -1e30
KEY_START = (0, 8, 24, 32)

PAIR_TILES = {0: 2, 1: 3, 2: 3}


def phases(kind):
    out = [("mem", 2, 2), ("qg", 6, 2)]
    if kind == 1:
        out.append(("lora", 1, 1))
    return out + [("pairs", 8, PAIR_TILES[kind]), ("out", 4, 2)]


def schedule():
    used, free, chunks, plan = [0, 0, 0], [0, 0, 0], 0, {}
    for l, kind in enumerate(KINDS):
        for name, n, tiles in phases(kind):
            per = tiles if name == "mem" else 2 * tiles
            plan[l, name] = (list(used), chunks, n, tiles, per, list(free))
            for s in range(tiles):
                used[s] += n
                free[s] = chunks + (n - 1) * per + (s + 1) * per // tiles
            chunks += n * per
    return plan


class Serial:

    def __init__(self, eng):
        self.eng, self.count, self.step, self.i = eng, {}, {}, 0

    def do(self, sem, ins):
        ins.then_inc(sem, 1)
        n = self.count.get(sem.name, 0) + 1
        self.count[sem.name] = n
        k = self.step.get(sem.name)
        self.eng.wait_ge(sem, n if k is None else self.i * k + n)

    def loop(self, n, steps, body):
        before = dict(self.count)
        self.step = {s.name: k for s, k in steps}
        with self.eng.Fori(0, n) as i:
            self.i = i
            body(i)
        for s, k in steps:
            assert self.count.get(s.name, 0) - before.get(s.name, 0) == k, (s.name, k, self.count.get(s.name, 0) - before.get(s.name, 0))
            self.count[s.name] = before.get(s.name, 0) + n * k
        changed = {s for s in self.count if self.count[s] != before.get(s, 0)} - set(self.step)
        assert not changed, changed
        self.step, self.i = {}, 0


def trunk_kernel(nc, x, mem, w_mem, w_a, w_b, w_c, w_out, gains, a_par, b_par, lora_up, bias,
                 square_c, scan_c, level_c, window_c, y, layers=4):
    plan = schedule()
    ctx = ExitStack()
    with ctx:
        def sem(name):
            return ctx.enter_context(nc.semaphore(name))

        def sb(name, *shape, stack=ctx):
            return stack.enter_context(nc.sbuf_tensor(name, [P, *shape], F32))

        ps = ctx.enter_context(nc.psum_tensor("ps", [P, 8, 512], F32))
        xT = sb("xT", KD, T)
        xn = sb("xn", KD, T)
        ring = sb("ring", 3, KB * P)
        br = sb("br", KB, T)
        gain = sb("gain", 12 * KD)
        square = sb("square", 3, P)
        ident, ones, bones = square[:, 0, :], square[:, 1, :], square[:, 2, :]

        region = ExitStack()
        sq = sb("sq", 2, 800, stack=region)
        rstd = sb("rstd", 800, stack=region)
        mk = sb("mk", 2, MEM, stack=region)
        mvf = sb("mvf", 2, MEM, stack=region)
        mv = sb("mv", 4, 256, stack=region)
        mq = sb("mq", 2, T, stack=region)
        attention = ExitStack()
        exps = sb("exps", 2, 512, stack=attention)
        probs_t = sb("probs_t", 2, 512, stack=attention)
        stat = sb("stat", 2, 8, stack=attention)
        scores = sb("scores", 2, 512, stack=attention)
        conv = ExitStack()
        z_in = sb("z_in", T, stack=conv)
        z_gate = sb("z_gate", T, stack=conv)
        z_pad = sb("z_pad", CONV_IN, stack=conv)
        z_out = sb("z_out", KD, CONV_OUT, stack=conv)
        apar = sb("apar", 8 * APAR, stack=conv)
        conv.close()
        na = ExitStack()
        na_q = sb("na_q", T, stack=na)
        na_k = sb("na_k", T, stack=na)
        na_v = sb("na_v", 5, 256, stack=na)
        na_vt = sb("na_vt", 10, P, stack=na)
        na_bias = sb("na_bias", 5, 2, 256, stack=na)
        na_bm = sb("na_bm", 5, 2, 256, stack=na)
        na_mask = sb("na_mask", 5, 256, stack=na)
        na.close()
        attention.close()
        region.close()
        wkv = ExitStack()
        tw = sb("tw", 2, WT, stack=wkv)
        bpar = sb("bpar", 8 * BPAR + 2, stack=wkv)
        one_minus_ka = sb("one_minus_ka", 8, stack=wkv)
        par_now = sb("par_now", BPAR, stack=wkv)
        up = sb("up", 2, P, stack=wkv)
        reset = sb("reset", 2, WT, stack=wkv)
        mask = sb("mask", 2, P, stack=wkv)
        level = sb("level", 2, LEVELS, C, stack=wkv)
        h_p = sb("h_p", 3, WT + 2, stack=wkv)
        lora = h_p[:, 0, :]
        xd = sb("xd", 3, WT, stack=wkv)
        sg = sb("sg", WT, stack=wkv)
        av = sb("av", WT, stack=wkv)
        cum = sb("cum", WT, stack=wkv)
        dx = sb("dx", WT, stack=wkv)
        dd = sb("dd", WT, stack=wkv)
        kk = sb("kk", WT, stack=wkv)
        ke = sb("ke", WT, stack=wkv)
        tmp = sb("tmp", WT, stack=wkv)
        ysum = sb("ysum", WT, stack=wkv)
        bonus = sb("bonus", WT, stack=wkv)
        ar = sb("ar", QUAD, P, stack=wkv)
        a_bd = sb("a_bd", QUAD, P, stack=wkv)
        b_bd = sb("b_bd", QUAD, P, stack=wkv)
        k_bd = sb("k_bd", QUAD, P, stack=wkv)
        v_bd = sb("v_bd", QUAD, P, stack=wkv)
        ab = sb("ab", QUAD, P, stack=wkv)
        ak = sb("ak", QUAD, P, stack=wkv)
        ak_bd = sb("ak_bd", QUAD, P, stack=wkv)
        bt = sb("bt", QUAD, P, stack=wkv)
        kt = sb("kt", QUAD, P, stack=wkv)
        vt = sb("vt", QUAD, P, stack=wkv)
        inv = sb("inv", QUAD, P, stack=wkv)
        inv_t = sb("inv_t", QUAD, P, stack=wkv)
        prod = sb("prod", QUAD, P, stack=wkv)
        lev = sb("lev", LEVELS, QUAD, P, stack=wkv)
        rhs = prod
        unew = sb("unew", QUAD, P, stack=wkv)
        state = sb("state", 2, P, stack=wkv)
        wkv.close()

        const_in, x_in, y_out = sem("const_in"), sem("x_in"), sem("y_out")
        mem_in, apar_in, bpar_in, up_in, bias_in, mask_in = (sem(n) for n in
            ("mem_in", "apar_in", "bpar_in", "up_in", "bias_in", "mask_in"))
        ring_in = [sem(f"ring_in{s}") for s in range(3)]
        cols_done, cols_taken = sem("cols_done"), sem("cols_taken")
        sq_ready, sq_used, ms_taken, root, inverse, scaled = (sem(n) for n in
            ("sq_ready", "sq_used", "ms_taken", "root", "inverse", "scaled"))
        normed = sem("normed")
        mv_turned, mv_taken = sem("mv_turned"), sem("mv_taken")
        sc_done, sc_biased, sc_max, ex_done, p_inv, p_done, tp_done, pt_done, av_done, gated = (
            [sem(f"{n}{a}") for a in range(2)] for n in
            ("sc_done", "sc_biased", "sc_max", "ex_done", "p_inv", "p_done", "tp_done", "pt_done", "av_done", "gated"))
        bm_ready, v_window, vt_turned, vt_taken = (sem(n) for n in ("bm_ready", "v_window", "vt_turned", "vt_taken"))
        glu_done, conv_done = sem("glu_done"), sem("conv_done")
        mean_done, centred, lsq_ready, lsq_used, l_ms, l_root, l_inv, l_scaled, l_silu, l_gated = (sem(n) for n in
            ("mean_done", "centred", "lsq_ready", "lsq_used", "l_ms", "l_root", "l_inv", "l_scaled", "l_silu", "l_gated"))
        w_zero, lora_mix, lora_shift, lora_act = sem("w_zero"), sem("lora_mix"), sem("lora_shift"), sem("lora_act")
        shifted, mixed, up_done, up_act, summed, less, decays = (sem(n) for n in
            ("shifted", "mixed", "up_done", "up_act", "summed", "less", "decays"))
        kk_raw, kk_sq, kk_ss, kk_max, kk_root, prepared, bon_in, bon_ps, bon_done = (sem(n) for n in
            ("kk_raw", "kk_sq", "kk_ss", "kk_max", "kk_root", "prepared", "bon_in", "bon_ps", "bon_done"))
        q_dve, q_pool, q_act, q_pairs, q_turn, q_masked, q_turned, q_akbd, q_levels = (sem(n) for n in
            ("q_dve", "q_pool", "q_act", "q_pairs", "q_turn", "q_masked", "q_turned", "q_akbd", "q_levels"))
        i_prod, i_taken, i_next, i_x = sem("i_prod"), sem("i_taken"), sem("i_next"), sem("i_x")
        c_r, c_rt, c_u, c_ut, c_s, c_st, c_y, c_yt = (sem(n) for n in
            ("c_r", "c_rt", "c_u", "c_ut", "c_s", "c_st", "c_y", "c_yt"))
        g_mean, g_centred, g_sq, g_var, g_eps, g_root, g_done = (sem(n) for n in
            ("g_mean", "g_centred", "g_sq", "g_var", "g_eps", "g_root", "g_done"))
        b_start, par_ready = sem("b_start"), sem("par_ready")
        block = ctx.enter_context(nc.Block())

        def tok(g, at=(0, 256)):
            return slice(at[g], at[g] + GROUPS[g][1])

        A_LAYERS = [l for l in range(layers) if KINDS[l] == 0]

        def quad_at(d, qn):
            return (0, WKV_AT[1], WKV_AT[1] + 256)[qn] if d == 0 else (0, WKV_AT[1] + 256, WKV_AT[1])[qn]

        @block.sync
        def _(sp):
            sp.dma_start(square[:, :, :], square_c).then_inc(const_in, 16)
            sp.dma_start(gain[:, :], gains).then_inc(const_in, 16)
            for l in range(layers):
                kind = KINDS[l]
                weights = {"mem": (w_mem, 4 * l), "out": (w_out, 8 * l)}
                body = {0: (w_a, 28 * (l // 3)), 1: (w_b, 0), 2: (w_c, 0)}[kind]
                weights["qg"] = body
                weights["lora"] = (body[0], 12)
                weights["pairs"] = (body[0], body[1] + (13 if kind == 1 else 12))
                if l:
                    sp.wait_ge(normed, 24 * l)
                sp.dma_start(xn[:, :, 0:MEM], mem).then_inc(mem_in, 16)
                if l == 0:
                    sp.dma_start(xT[:, :, :], x).then_inc(x_in, 16)
                for name, n, tiles in phases(kind):
                    used, chunks, n, tiles, per, free = plan[l, name]
                    src, first = weights[name]
                    width = (KB if name == "out" else KD) * P
                    if name == "pairs" and kind == 0:
                        sp.wait_ge(gated[0], 12 * (l + 1))
                        sp.dma_start(apar[:, :], a_par[l // 3]).then_inc(apar_in, 16)
                    if name == "lora":
                        sp.wait_ge(gated[0], 12 * (l + 1))
                        for dst, s in ((bpar[:, :], b_par), (reset[:, :, :], scan_c), (mask[:, :, :], window_c[1]),
                                       (level[:, :, :, :], level_c)):
                            sp.dma_start(dst, s).then_inc(bpar_in, 16)
                    if name == "pairs" and kind == 2:
                        sp.wait_ge(gated[0], 12 * (l + 1))
                        sp.dma_start(na_mask[:, :, :], window_c[0]).then_inc(mask_in, 16)

                    def load(i, first_free=False):
                        for s in range(tiles):
                            before = chunks - per + (s + 1) * per // tiles
                            sp.wait_ge(cols_done, free[s] if first_free else i * per + before)
                            sp.dma_start(ring[:, s, 0:width],
                                         src[bass.ds(first + i * tiles + s, 1), :, :].rearrange("a p c -> (a p) c"))\
                              .then_inc(ring_in[s], 16)
                        if name == "pairs" and kind == 1:
                            sp.wait_ge(up_done, 8 * i)
                            sp.dma_start(up[:, :, :], lora_up[bass.ds(i, 1), :, :, :].rearrange("a p d c -> (a p) d c"))\
                              .then_inc(up_in, 16)
                        if name == "pairs" and kind == 2:
                            sp.wait_ge(bm_ready, i)
                            sp.dma_start(na_bias[:, :, :, :].rearrange("p a h k -> p (a h k)"),
                                         bias[bass.ds(i, 1), :, :].rearrange("a p k -> (a p) k")).then_inc(bias_in, 16)

                    load(0, True)
                    if n > 1:
                        with sp.Fori(1, n) as i:
                            load(i)
            sp.wait_ge(normed, 24 * layers)
            sp.dma_start(y, xT[:, :, :]).then_inc(y_out, 16)
            sp.wait_ge(y_out, 16)

        @block.tensor
        def _(pe):
            mm = nc.tensor.matmul

            def project(l, name, i, s, c, src, token_chunks, kd=KD):
                used, chunks, n, tiles, per, _ = plan[l, name]
                pe.wait_ge(ring_in[s], (i + used[s] + 1) * 16)
                for j, (at, w) in enumerate(token_chunks):
                    if l or name != "mem" or i:
                        pe.wait_ge(cols_taken, i * per + chunks + c + j - 1)
                    for k in range(kd):
                        ins = mm(ps[:, (c + j) % 2, 0:w], ring[:, s, k * P:(k + 1) * P], src[:, k, at:at + w],
                                 start=k == 0, stop=k == kd - 1)
                    ins.then_inc(cols_done, 1)

            def sum_squares(q, widths):
                for k in range(KD):
                    pe.wait_ge(sq_ready, 8 * q + k + 1)
                    for j, (at, w) in enumerate(widths):
                        ins = mm(ps[:, j, 0:w], ones, sq[:, k % 2, at:at + w], start=k == 0, stop=k == KD - 1)
                    ins.then_inc(sq_used, 1)

            def attention_units(a, i, base, units, s_mm, v_of, per):
                n = len(units)

                def at(c):
                    return base + i * per + c

                def score(u):
                    if u >= 2:
                        pe.wait_ge(ex_done[a], 2 * at(u - 1))
                    s_mm(u).then_inc(sc_done[a], 1)

                score(0)
                for u in range(n):
                    if u + 1 < n:
                        score(u + 1)
                    pe.wait_ge(p_done[a], at(u + 1))
                    for h in range(2):
                        for c in range(2):
                            ins = nc.tensor.transpose(ps[:, 4 + u % 2, (2 * h + c) * P:(2 * h + c + 1) * P],
                                                      exps[:, u % 2, h * 256 + c * P:h * 256 + (c + 1) * P], ident)
                    ins.then_inc(tp_done[a], 1)
                    pe.wait_ge(pt_done[a], at(u + 1))
                    if u >= 2:
                        pe.wait_ge(gated[a], at(u - 1))
                    for h in range(2):
                        for c in range(2):
                            ins = mm(ps[64 * h:64 * h + 64, 6 + u % 2, 0:P], v_of(u, h, c),
                                     probs_t[:, u % 2, (2 * h + c) * P:(2 * h + c + 1) * P], start=c == 0, stop=c == 1)
                    ins.then_inc(av_done[a], 1)

            pe.wait_ge(const_in, 32)
            for l in range(layers):
                kind = KINDS[l]
                sum_squares(3 * l, [(0, MEM)])
                pe.wait_ge(normed, 24 * l + 8)
                for i in range(2):
                    for s in range(2):
                        project(l, "mem", i, s, s, xn, [(0, MEM)])
                pe.wait_ge(cols_taken, plan[l, "qg"][1])
                for m in range(4):
                    for c in range(2):
                        ins = nc.tensor.transpose(ps[:, 2 + m // 2, (m % 2) * 256 + c * P:(m % 2) * 256 + (c + 1) * P],
                                                  mvf[:, c, m * P:(m + 1) * P], ident)
                ins.then_inc(mv_turned, 1)
                sum_squares(3 * l + 1, GROUPS)
                pe.wait_ge(normed, 24 * l + 16)
                with pe.Fori(0, 6) as i:
                    for s in range(2):
                        project(l, "qg", i, s, 2 * s, xn, GROUPS)
                pe.wait_ge(cols_taken, plan[l, "qg"][1] + 24)
                pe.wait_ge(mv_taken, l + 1)

                def mem_scores(u):
                    hp, t = u // 6, u % 6
                    g = int(t >= 2)
                    for h in range(2):
                        r = slice(64 * h, 64 * h + 64)
                        ins = mm(ps[:, 2 * (u % 2) + h, 0:256], mq[r, hp, t * P:(t + 1) * P],
                                 mk[r, hp, g * 256:(g + 1) * 256], start=True, stop=True)
                    return ins

                def mem_v(u, h, c):
                    hp, t = u // 6, u % 6
                    return mv[:, 2 * int(t >= 2) + c, (2 * hp + h) * 64:(2 * hp + h + 1) * 64]

                attention_units(0, 0, 12 * l, range(12), mem_scores, mem_v, 0)
                pe.wait_ge(gated[0], 12 * (l + 1))

                if kind == 0:
                    with pe.Fori(0, 8) as i:
                        for s in range(2):
                            project(l, "pairs", i, s, 2 * s, xn, GROUPS)
                    la = l // 3
                    pe.wait_ge(conv_done, (TAPS + 1) * 8 * (la + 1))
                    half = CONV_OUT // 2
                    for k in range(KD):
                        for j in range(2):
                            ins = mm(ps[:, 2 + j, 0:half], ones, z_out[:, k, j * half:(j + 1) * half],
                                     start=k == 0, stop=k == KD - 1)
                    ins.then_inc(mean_done, 1)
                    for k in range(KD):
                        pe.wait_ge(lsq_ready, 8 * la + k + 1)
                        for j in range(2):
                            ins = mm(ps[:, 4 + j, 0:half], ones, sq[:, k % 2, j * half:(j + 1) * half],
                                     start=k == 0, stop=k == KD - 1)
                        ins.then_inc(lsq_used, 1)
                    pe.wait_ge(l_gated, 16 * (la + 1))
                elif kind == 2:
                    with pe.Fori(0, 8) as i:
                        for s in range(3):
                            project(l, "pairs", i, s, 2 * s, xn, GROUPS)
                        pe.wait_ge(cols_taken, plan[l, "pairs"][1] + i * 6 + 6)
                        for n in range(10):
                            ins = nc.tensor.transpose(ps[:, 2 + n // 4, (n % 4) * P:(n % 4 + 1) * P],
                                                      na_v[:, n // 2, (n % 2) * P:(n % 2 + 1) * P], ident)
                        ins.then_inc(vt_turned, 1)
                        pe.wait_ge(vt_taken, i * 3 + 3)

                        def keys(r, u):
                            if u >= 4:
                                return na_k[r, 0:256]
                            return na_k[r, 256:T].rearrange("p (r c) -> p r c", c=64)[:, :, KEY_START[u]:KEY_START[u] + 32]

                        def queries(r, u):
                            at = 256 + u * P if u < 4 else (u - 4) * P
                            return na_q[r, at:at + P]

                        def na_scores(u):
                            for h in range(2):
                                r = slice(64 * h, 64 * h + 64)
                                ins = mm(ps[:, 2 * (u % 2) + h, 0:256], queries(r, u), keys(r, u), start=True, stop=True)
                            return ins

                        def na_values(u, h, c):
                            return na_vt[:, 2 * min(u, 4) + c, h * 64:(h + 1) * 64]

                        attention_units(1, i, 0, range(6), na_scores, na_values, 6)
                        pe.wait_ge(gated[1], i * 12 + 12)
                else:
                    project(l, "lora", 0, 0, 0, xn, GROUPS)
                    parts = ((0, 257), (257, 512))
                    with pe.Fori(0, 8) as p:
                        for s in range(3):
                            project(l, "pairs", p, s, 2 * s, xn, GROUPS)
                        for d in range(2):
                            pe.wait_ge(up_in, p * 16 + 16)
                            if d == 0:
                                pe.wait_ge(lora_act, 4)
                            for j, (at, w) in enumerate(parts):
                                mm(ps[:, 2 + j, 0:w], up[0:64, d, :], tw[0:64, d, at:at + w], start=True, stop=True)\
                                    .then_inc(up_done, 1)
                                mm(ps[:, 4 + j, 0:w], up[64:128, d, :], tw[64:128, d, at:at + w], start=True, stop=True)\
                                    .then_inc(up_done, 1)
                            pe.wait_ge(kk_sq, p * 2 + d + 1)
                            for j, (at, w) in enumerate(parts):
                                ins = mm(ps[:, 6 + j, 0:w], bones, tmp[:, at:at + w], start=True, stop=True)
                            ins.then_inc(kk_ss, 1)
                            pe.wait_ge(bon_in, p * 2 + d + 1)
                            for j, (at, w) in enumerate(parts):
                                ins = mm(ps[:, 6 + j, 0:w], bones, tmp[:, at:at + w], start=True, stop=True)
                            ins.then_inc(bon_ps, 1)
                            for qn in range(3):
                                def n(c):
                                    return p * 6 + (3 * d + qn) + c
                                pe.wait_ge(q_dve, n(1) * 3)
                                pe.wait_ge(q_pool, n(1))
                                pe.wait_ge(q_act, n(1) * 6)
                                for c in range(QUAD):
                                    ins = mm(ps[:, 2, c * P:(c + 1) * P], b_bd[:, c, :], ar[:, c, :], start=True, stop=True)
                                ins.then_inc(q_pairs, 1)
                                for c in range(QUAD):
                                    ins = mm(ps[:, 3, c * P:(c + 1) * P], k_bd[:, c, :], ar[:, c, :], start=True, stop=True)
                                ins.then_inc(q_pairs, 1)
                                for b, src in ((4, b_bd), (5, k_bd), (6, v_bd)):
                                    for c in range(QUAD):
                                        ins = nc.tensor.transpose(ps[:, b, c * P:(c + 1) * P], src[:, c, :], ident)
                                    ins.then_inc(q_turn, 1)
                                pe.wait_ge(q_levels, n(1) * 12)
                                for c in range(QUAD):
                                    ins = mm(ps[:, 7, c * P:(c + 1) * P], lev[:, 0, c, :], ident, start=True, stop=True)
                                ins.then_inc(i_prod, 1)
                                pe.wait_ge(q_turned, n(1) * 3)
                                pe.wait_ge(q_masked, n(1) * 2)
                                for v in range(1, LEVELS):
                                    pe.wait_ge(i_x, (n(1) - 1) * 11 + 2 * v)
                                    for c in range(QUAD):
                                        ins = mm(ps[:, 2, c * P:(c + 1) * P], lev[:, v, c, :], inv[:, c, :], start=True, stop=True)
                                    ins.then_inc(i_prod, 1)
                                    pe.wait_ge(i_taken, (n(1) - 1) * 5 + v)
                                    for c in range(QUAD):
                                        ins = mm(ps[:, 3, c * P:(c + 1) * P], prod[:, c, :], inv_t[:, c, :], start=True, stop=True)
                                    if v < LEVELS - 1:
                                        for c in range(QUAD):
                                            ins = mm(ps[:, 4, c * P:(c + 1) * P], inv_t[:, c, :], prod[:, c, :], start=True, stop=True)
                                    ins.then_inc(i_next, 1)
                                pe.wait_ge(i_x, n(1) * 11)
                                pe.wait_ge(q_akbd, n(1) * 2)
                                order = range(QUAD) if d == 0 else range(QUAD - 1, -1, -1)
                                for m, c in enumerate(order):
                                    st = state[:, m % 2, :]
                                    cols = slice(c * P, (c + 1) * P)
                                    pe.wait_ge(c_st, p * 28 + (14 * d + (0, 5, 10)[qn]) + m + (0 if qn == 2 else 1))
                                    mm(ps[:, 5, cols], a_bd[:, c, :], st, start=True, stop=False)
                                    mm(ps[:, 5, cols], ak_bd[:, c, :], vt[:, c, :], start=False, stop=True).then_inc(c_r, 1)
                                    pe.wait_ge(c_rt, (n(1) - 1) * 4 + m + 1)
                                    mm(ps[:, 6, cols], inv_t[:, c, :], rhs[:, c, :], start=True, stop=True).then_inc(c_u, 1)
                                    pe.wait_ge(c_ut, (n(1) - 1) * 4 + m + 1)
                                    mm(ps[:, 7, cols], ident, st, start=True, stop=False)
                                    mm(ps[:, 7, cols], kt[:, c, :], vt[:, c, :], start=False, stop=False)
                                    mm(ps[:, 7, cols], bt[:, c, :], unew[:, c, :], start=False, stop=True).then_inc(c_s, 1)
                                    mm(ps[:, 2, cols], st, ar[:, c, :], start=True, stop=False)
                                    mm(ps[:, 2, cols], vt[:, c, :], ak[:, c, :], start=False, stop=False)
                                    mm(ps[:, 2, cols], unew[:, c, :], ab[:, c, :], start=False, stop=True).then_inc(c_y, 1)
                                pe.wait_ge(c_yt, n(1))
                        for j, (at, w) in enumerate(parts):
                            ins = mm(ps[:, 2 + j, 0:w], bones, ysum[:, at:at + w], start=True, stop=True)
                        ins.then_inc(g_mean, 1)
                        pe.wait_ge(g_sq, p + 1)
                        for j, (at, w) in enumerate(parts):
                            ins = mm(ps[:, 4 + j, 0:w], bones, tmp[:, at:at + w], start=True, stop=True)
                        ins.then_inc(g_var, 1)
                        pe.wait_ge(g_done, p * 5 + 5)

                pe.wait_ge(cols_taken, plan[l, "out"][1])
                with pe.Fori(0, 4) as i:
                    for s in range(2):
                        project(l, "out", i, s, 2 * s, br, GROUPS, KB)
                pe.wait_ge(cols_taken, plan[l, "out"][1] + 16)
                sum_squares(3 * l + 2, GROUPS)
                pe.wait_ge(normed, 24 * l + 24)

        @block.scalar
        def _(act):
            a_ = Serial(act)
            f = nc.scalar.activation

            def wait_cols(l, name, i, c):
                used, chunks, n, tiles, per, _ = plan[l, name]
                act.wait_ge(cols_done, i * per + chunks + c + 1)

            def take(l, name, i, c, dst, func, **kw):
                wait_cols(l, name, i, c)
                a_.do(cols_taken, f(dst, ps[:, c % 2, 0:dst.shape[-1]], func, **kw))

            def squares(q, src, w):
                for k in range(KD):
                    if 8 * q + k >= 2:
                        act.wait_ge(sq_used, 8 * q + k - 1)
                    a_.do(sq_ready, f(sq[:, k % 2, 0:w], src[:, k, 0:w], ACT.Square))
                act.wait_ge(ms_taken, q + 1)
                a_.do(root, f(rstd[:, 0:w], rstd[:, 0:w], ACT.Sqrt))

            def attention_units(a, i, base, n, per, src):
                def at(c):
                    return base + i * per + c

                def exp(u):
                    act.wait_ge(sc_max[a], at(u + 1))
                    for h in range(2):
                        a_.do(ex_done[a], f(exps[:, u % 2, h * 256:(h + 1) * 256], src(u, h), ACT.Exp,
                                            bias=stat[:, u % 2, h:h + 1], accum_out=stat[:, u % 2, 2 + h:3 + h]))

                exp(0)
                for u in range(n):
                    if u + 1 < n:
                        if u >= 1:
                            act.wait_ge(tp_done[a], at(u))
                        exp(u + 1)
                    act.wait_ge(tp_done[a], at(u + 1))
                    if u >= 2:
                        act.wait_ge(av_done[a], at(u - 1))
                    a_.do(pt_done[a], f(probs_t[:, u % 2, :], ps[:, 4 + u % 2, :], ACT.Copy))

            act.wait_ge(mem_in, 16)
            for l in range(layers):
                kind = KINDS[l]
                if l:
                    act.wait_ge(mem_in, 16 * (l + 1))
                squares(3 * l, xn, MEM)
                for c in range(2):
                    take(l, "mem", 0, c, mk[:, c, :], ACT.Copy)
                for c in range(2):
                    take(l, "mem", 1, c, mvf[:, c, :], ACT.Copy)
                act.wait_ge(mv_turned, l + 1)
                a_.do(mv_taken, f(mv[:, :, :].rearrange("p m c -> p (m c)"),
                                  ps[:, 2:4, :].rearrange("p b c -> p (b c)"), ACT.Copy))
                if l == 0:
                    act.wait_ge(x_in, 16)
                squares(3 * l + 1, xT, T)
                for s in range(2):
                    for g in range(2):
                        take(l, "qg", 0, 2 * s + g, mq[:, s, tok(g)], ACT.Copy, scale=HEAD_SCALE)

                def gates(i):
                    for s in range(2):
                        for g in range(2):
                            take(l, "qg", i + 1, 2 * s + g,
                                 br[:, 2 * i + s, tok(g)], ACT.Silu)
                for i in range(5):
                    gates(i)
                attention_units(0, 0, 12 * l, 12, 0, lambda u, h: ps[:, 2 * (u % 2) + h, 0:256])

                if kind == 0:
                    la = l // 3
                    act.wait_ge(gated[0], 12 * (l + 1))

                    def glu(i):
                        act.wait_ge(glu_done, 2 * i + (16 * la + la + 1))
                        for g in range(2):
                            take(l, "pairs", i, g, z_in[:, tok(g)], ACT.Copy)
                        for g in range(2):
                            take(l, "pairs", i, 2 + g, z_gate[:, tok(g)], ACT.Sigmoid)
                    a_.loop(8, [(cols_taken, 4)], glu)
                    for k in range(KD):
                        act.wait_ge(centred, 8 * la + k + 1)
                        if k >= 2:
                            act.wait_ge(lsq_used, 8 * la + k - 1)
                        a_.do(lsq_ready, f(sq[:, k % 2, 0:CONV_OUT], z_out[:, k, :], ACT.Square))
                    act.wait_ge(l_ms, la + 1)
                    a_.do(l_root, f(rstd[:, 0:CONV_OUT], rstd[:, 0:CONV_OUT], ACT.Sqrt))
                    for k in range(KD):
                        act.wait_ge(l_scaled, 8 * la + k + 1)
                        b = k * APAR + TAPS
                        a_.do(l_silu, f(z_out[:, k, :], z_out[:, k, :], ACT.Silu, scale=apar[:, b + 1:b + 2],
                                        bias=apar[:, b + 2:b + 3]))
                elif kind == 2:
                    act.wait_ge(gated[0], 12 * (l + 1))

                    def na(i):
                        for g, cols in ((0, 32), (1, 16)):
                            wait_cols(l, "pairs", i, g)
                            a_.do(cols_taken, f(
                                na_q[:, tok(g)].rearrange("p (i r c) -> p r i c", c=cols, i=64 // cols),
                                ps[:, g, 0:GROUPS[g][1]].rearrange("p (r i c) -> p r i c", c=cols, i=64 // cols),
                                ACT.Copy, scale=HEAD_SCALE))
                        for g in range(2):
                            take(l, "pairs", i, 2 + g, na_k[:, tok(g)], ACT.Copy)
                        take(l, "pairs", i, 4, na_v[:, 4, :], ACT.Copy)
                        wait_cols(l, "pairs", i, 5)
                        for w, start in enumerate(KEY_START):
                            a_.do(v_window if w < 3 else cols_taken, f(
                                na_v[:, w, :].rearrange("p (r c) -> p r c", c=32),
                                ps[:, 1, :].rearrange("p (r c) -> p r c", c=64)[:, :, start:start + 32], ACT.Copy))
                        act.wait_ge(vt_turned, i + 1)
                        flat = na_vt[:, :, :].rearrange("p w c -> p (w c)")
                        for b, w in ((0, 512), (1, 512), (2, 256)):
                            a_.do(vt_taken, f(flat[:, 512 * b:512 * b + w], ps[:, 2 + b, 0:w], ACT.Copy))
                        attention_units(1, i, 0, 6, 6, lambda u, h: scores[:, u % 2, h * 256:(h + 1) * 256])
                    a_.loop(8, [(cols_taken, 6), (v_window, 3), (vt_taken, 3), (ex_done[1], 12), (pt_done[1], 6)], na)
                else:
                    act.wait_ge(w_zero, 3)
                    for g in range(2):
                        take(l, "lora", 0, g, lora[:, 1 + WKV_AT[g]:1 + WKV_AT[g] + GROUPS[g][1]], ACT.Copy)
                    for d in range(2):
                        act.wait_ge(lora_mix, 2 * d + 2)
                        a_.do(lora_act, f(tw[0:64, d, :], tw[0:64, d, :], ACT.Tanh))
                        a_.do(lora_act, f(tw[64:128, d, :], tw[64:128, d, :], ACT.Copy))

                    act.wait_ge(lora_mix, 3)

                    def pair(p):
                        for n in range(3):
                            for g in range(2):
                                take(l, "pairs", p, 2 * n + g, h_p[:, n, 1 + WKV_AT[g]:1 + WKV_AT[g] + GROUPS[g][1]], ACT.Copy)
                        act.wait_ge(par_ready, p + 1)
                        for d in range(2):
                            if d:
                                act.wait_ge(c_yt, p * 6 + 3)
                            for j, (at, w) in enumerate(((0, 257), (257, 512))):
                                act.wait_ge(up_done, p * 8 + 4 * d + 2 * j + 1)
                                a_.do(up_act, f(sg[:, at:at + w], ps[:, 2 + j, 0:w], ACT.Sigmoid, bias=par_now[:, W0 + d:W0 + d + 1]))
                                act.wait_ge(up_done, p * 8 + 4 * d + 2 * j + 2)
                                a_.do(up_act, f(av[:, at:at + w], ps[:, 4 + j, 0:w], ACT.Sigmoid, bias=par_now[:, A0 + d:A0 + d + 1]))
                            act.wait_ge(kk_raw, p * 2 + d + 1)
                            a_.do(kk_sq, f(tmp[:, :], kk[:, :], ACT.Square))
                            act.wait_ge(kk_max, (p * 2 + d + 1) * 2)
                            a_.do(kk_root, f(tmp[:, :], tmp[:, :], ACT.Sqrt))
                            act.wait_ge(less, p * 2 + d + 1)
                            a_.do(decays, f(dd[:, :], cum[:, :], ACT.Exp, scale=-DECAY))
                            a_.do(decays, f(dx[:, :], dx[:, :], ACT.Exp, scale=-DECAY))
                            a_.do(decays, f(cum[:, :], cum[:, :], ACT.Exp, scale=DECAY))
                            act.wait_ge(bon_done, p * 3 + 2 * d + 1)
                            for qn in range(3):
                                first = quad_at(d, qn)
                                q = p * 6 + (3 * d + qn)
                                if d or qn:
                                    act.wait_ge(c_y, q * 4)
                                act.wait_ge(q_dve, q * 3 + 3)
                                for dst, src in ((k_bd, ke[:, first:first + 256].rearrange("p (c t) -> p c t", c=QUAD)),
                                                 (v_bd, xd[:, 2, first:first + 256].rearrange("p (c t) -> p c t", c=QUAD)),
                                                 (a_bd, ar[:, :, 0:C])):
                                    for h in range(2):
                                        r = slice(64 * h, 64 * h + 64)
                                        a_.do(q_act, f(dst[r, :, 64 * h:64 * h + 64], src[r], ACT.Copy))
                                for n, (b, dst) in enumerate(((4, bt), (5, kt), (6, vt))):
                                    act.wait_ge(q_turn, q * 3 + n + 1)
                                    a_.do(q_turned, f(dst[:, :, :].rearrange("p c t -> p (c t)"), ps[:, b, :], ACT.Copy))
                                act.wait_ge(q_masked, q * 2 + 2)
                                for h in range(2):
                                    r = slice(64 * h, 64 * h + 64)
                                    a_.do(q_akbd, f(ak_bd[r, :, 64 * h:64 * h + 64], ak[r, :, 0:C], ACT.Copy))
                                for v in range(1, LEVELS):
                                    act.wait_ge(i_prod, q * 6 + v + 1)
                                    a_.do(i_taken, f(prod[:, :, :].rearrange("p c t -> p (c t)"), ps[:, 2, :], ACT.Copy))
                                order = range(QUAD) if d == 0 else range(QUAD - 1, -1, -1)
                                for m, c in enumerate(order):
                                    cols = slice(c * P, (c + 1) * P)
                                    act.wait_ge(c_r, q * 4 + m + 1)
                                    a_.do(c_rt, f(rhs[:, c, :], ps[:, 5, cols], ACT.Copy))
                                    act.wait_ge(c_u, q * 4 + m + 1)
                                    a_.do(c_ut, f(unew[:, c, :], ps[:, 6, cols], ACT.Copy, scale=-1.0))
                        act.wait_ge(g_centred, p * 2 + 2)
                        a_.do(g_sq, f(tmp[:, :], ysum[:, :], ACT.Square))
                        act.wait_ge(g_eps, p * 2 + 2)
                        a_.do(g_root, f(tmp[:, :], tmp[:, :], ACT.Sqrt))
                    a_.loop(8, [(cols_taken, 6), (up_act, 8), (kk_sq, 2), (kk_root, 2), (decays, 6), (q_act, 36),
                                (q_turned, 18), (q_akbd, 12), (i_taken, 30), (c_rt, 24), (c_ut, 24), (g_sq, 1),
                                (g_root, 1)], pair)

                def outs(i):
                    for s in range(2):
                        for g in range(2):
                            take(l, "out", i, 2 * s + g, xn[:, 2 * i + s, tok(g)], ACT.Copy)
                for i in range(4):
                    outs(i)
                squares(3 * l + 2, xn, T)

        @block.gpsimd
        def _(pool):
            g_ = Serial(pool)
            for l in range(layers):
                if KINDS[l] == 2:
                    pool.wait_ge(mask_in, 16)

                    def add_mask(i):
                        pool.wait_ge(bias_in, i * 16 + 16)
                        pool.wait_ge(cols_taken, i * 6 + plan[l, "pairs"][1] + 1)
                        g_.do(bm_ready, nc.gpsimd.tensor_tensor(
                            na_bm[:, :, :, :], na_bias[:, :, :, :],
                            na_mask[:, :, :].unsqueeze(2).to_broadcast([P, 5, 2, 256]), ALU.add))
                    g_.loop(8, [(bm_ready, 1)], add_mask)
                elif KINDS[l] == 1:
                    pool.wait_ge(gated[0], 12 * (l + 1))
                    g_.do(w_zero, nc.gpsimd.memset(h_p[:, :, :], 0.0))
                    g_.do(w_zero, nc.gpsimd.memset(ysum[:, :], 0.0))
                    for dst in (a_bd, b_bd, k_bd, v_bd, ak_bd, lev):
                        ins = nc.gpsimd.memset(dst[tuple(slice(None) for _ in dst.shape)], 0.0)
                        if dst is lev:
                            g_.do(w_zero, ins)
                        else:
                            ins.then_inc(b_start, 1)
                    pool.wait_ge(b_start, 5)
                    pool.wait_ge(cols_taken, plan[l, "pairs"][1])
                    for d in range(2):
                        g_.do(lora_shift, nc.gpsimd.tensor_tensor(
                            tw[:, d, :], lora[:, 2 * d:2 * d + WT], lora[:, 1:1 + WT], ALU.subtract))

                    def pair(p):
                        for d in range(2):
                            pool.wait_ge(cols_taken, p * 6 + plan[l, "pairs"][1] + 6)
                            if d:
                                pool.wait_ge(c_yt, p * 6 + 3)
                            for n in range(3):
                                g_.do(shifted, nc.gpsimd.tensor_tensor(
                                    xd[:, n, :], h_p[:, n, 2 * d:2 * d + WT], h_p[:, n, 1:1 + WT], ALU.subtract))
                            pool.wait_ge(summed, p * 2 + d + 1)
                            g_.do(less, nc.gpsimd.tensor_tensor(dx[:, :], cum[:, :], sg[:, :], ALU.subtract))
                            pool.wait_ge(decays, p * 6 + 3 * d + 3)
                            for qn in range(3):
                                q = p * 6 + (3 * d + qn)
                                first = quad_at(d, qn)
                                pool.wait_ge(mixed, p * 6 + 3 * d + 3)
                                if d or qn:
                                    pool.wait_ge(c_y, q * 4)
                                g_.do(q_pool, nc.gpsimd.tensor_tensor(
                                    ar[:, :, C:P], xd[:, 0, first:first + 256].rearrange("p (c t) -> p c t", c=QUAD),
                                    dd[:, first:first + 256].rearrange("p (c t) -> p c t", c=QUAD), ALU.mult))
                                pool.wait_ge(q_masked, q * 2 + 1)
                                for v in range(LEVELS):
                                    for h in range(2):
                                        r = slice(64 * h, 64 * h + 64)
                                        g_.do(q_levels, nc.gpsimd.tensor_tensor(
                                            lev[r, v, :, 64 * h:64 * h + 64], ab[r, :, 0:C],
                                            level[r, d, v, :].unsqueeze(1).to_broadcast([64, QUAD, C]), ALU.mult))
                    g_.loop(8, [(shifted, 6), (less, 2), (q_pool, 6), (q_levels, 72)], pair)

        @block.vector
        def _(dve):
            v_ = Serial(dve)
            ve = nc.vector
            stt = ve.scalar_tensor_tensor

            def norm(q, widths, total, k_op):
                dve.wait_ge(sq_used, 8 * q + 8)
                for j, (at, w) in enumerate(widths):
                    ins = ve.tensor_scalar(rstd[:, at:at + w], ps[:, j, 0:w], 1.0 / D, RMS_EPS, ALU.mult, ALU.add)
                    if j < len(widths) - 1:
                        v_.do(scaled, ins)
                v_.do(ms_taken, ins)
                dve.wait_ge(root, q + 1)
                v_.do(inverse, ve.reciprocal(rstd[:, 0:total], rstd[:, 0:total]))
                for k in range(KD):
                    k_op(k)

            def attention_units(a, i, base, n, per, bias_of, gate):
                def at(c):
                    return base + i * per + c

                def top(u):
                    dve.wait_ge(sc_done[a], at(u + 1))
                    src = ps[:, 2 * (u % 2):2 * (u % 2) + 2, 0:256]
                    if bias_of:
                        out = scores[:, u % 2, :].rearrange("p (h k) -> p h k", h=2)
                        v_.do(sc_biased[a], ve.tensor_tensor(out, src, bias_of(u), ALU.add))
                        src = out
                    v_.do(sc_max[a], ve.tensor_reduce(out=stat[:, u % 2, 0:2], in_=src,
                                                      op=ALU.max, axis=AX_X, negate=True))

                top(0)
                for u in range(n):
                    if u + 1 < n:
                        top(u + 1)
                    dve.wait_ge(ex_done[a], 2 * at(u + 1))
                    v_.do(p_inv[a], ve.reciprocal(stat[:, u % 2, 4:6], stat[:, u % 2, 2:4]))
                    v_.do(p_done[a], ve.tensor_tensor(
                        exps[:, u % 2, :].rearrange("p (h k) -> p h k", h=2),
                        exps[:, u % 2, :].rearrange("p (h k) -> p h k", h=2),
                        stat[:, u % 2, 4:6].unsqueeze(2).to_broadcast([P, 2, 256]), ALU.mult))
                    dve.wait_ge(av_done[a], at(u + 1))
                    gate(u)

            dve.wait_ge(const_in, 32)
            for l in range(layers):
                kind = KINDS[l]

                def scale_by(row, src):
                    def k_op(k):
                        w = MEM if src is xn else T
                        v_.do(normed, stt(xn[:, k, 0:w], src[:, k, 0:w], gain[:, row * KD + k:row * KD + k + 1],
                                          rstd[:, 0:w], ALU.mult, ALU.mult))
                    return k_op

                norm(3 * l, [(0, MEM)], MEM, scale_by(8 + l, xn))
                dve.wait_ge(cols_done, plan[l, "qg"][1])
                norm(3 * l + 1, GROUPS, T, scale_by(l, xT))
                dve.wait_ge(cols_taken, plan[l, "qg"][1] + 24)

                def mem_gate(u):
                    hp, t = u // 6, u % 6
                    dst = br[:, KD + hp, t * P:(t + 1) * P]
                    v_.do(gated[0], ve.tensor_tensor(dst, dst, ps[:, 6 + u % 2, 0:P], ALU.mult))
                attention_units(0, 0, 12 * l, 12, 0, None, mem_gate)

                if kind == 0:
                    la = l // 3
                    dve.wait_ge(apar_in, 16 * (la + 1))
                    v_.do(glu_done, ve.memset(z_pad[:, :], 0.0))

                    def conv_pair(i):
                        dve.wait_ge(cols_taken, i * 4 + plan[l, "pairs"][1] + 4)
                        for g, (first, n) in enumerate(GROUPS):
                            at = HALO + CONV_AT[g]
                            v_.do(glu_done, ve.tensor_tensor(z_pad[:, at:at + n], z_in[:, first:first + n],
                                                             z_gate[:, first:first + n], ALU.mult))
                        dst = z_out[:, bass.ds(i, 1), :].rearrange("p a t -> p (a t)")

                        def w(c):
                            return apar[:, bass.ds(i * APAR + c, 1)]
                        v_.do(conv_done, ve.tensor_scalar(dst, z_pad[:, 0:CONV_OUT], w(0), w(TAPS), ALU.mult, ALU.add))
                        for c in range(1, TAPS):
                            v_.do(conv_done, stt(dst, z_pad[:, c:c + CONV_OUT], w(c), dst, ALU.mult, ALU.add))
                        v_.do(conv_done, ve.memset(stat[:, 0, 0:1], 0.0))
                    v_.loop(8, [(glu_done, 2), (conv_done, TAPS + 1)], conv_pair)
                    half = CONV_OUT // 2
                    dve.wait_ge(mean_done, la + 1)
                    for k in range(KD):
                        v = z_out[:, k, :].rearrange("p (j t) -> p j t", j=2)
                        v_.do(centred, stt(v, ps[:, 2:4, 0:half], -1.0 / D, v, ALU.mult, ALU.add))
                    dve.wait_ge(lsq_used, 8 * (la + 1))
                    v_.do(l_ms, ve.tensor_scalar(rstd[:, 0:CONV_OUT].rearrange("p (j t) -> p j t", j=2), ps[:, 4:6, 0:half],
                                                 1.0 / D, LN_EPS, ALU.mult, ALU.add))
                    dve.wait_ge(l_root, la + 1)
                    v_.do(l_inv, ve.reciprocal(rstd[:, 0:CONV_OUT], rstd[:, 0:CONV_OUT]))
                    for k in range(KD):
                        v_.do(l_scaled, ve.tensor_tensor(z_out[:, k, :], z_out[:, k, :], rstd[:, 0:CONV_OUT], ALU.mult))
                    for k in range(KD):
                        dve.wait_ge(l_silu, 8 * la + k + 1)
                        for g, (first, n) in enumerate(GROUPS):
                            dst = br[:, k, first:first + n]
                            v_.do(l_gated, ve.tensor_tensor(dst, dst, z_out[:, k, CONV_AT[g]:CONV_AT[g] + n], ALU.mult))
                elif kind == 2:
                    def na(i):
                        dve.wait_ge(bm_ready, i + 1)

                        def bias_of(u):
                            kind_of = (0, 1, 1, 2, 3, 4)[u]
                            return na_bm[:, kind_of, :, :]

                        def gate(u):
                            for h in range(2):
                                r = slice(64 * h, 64 * h + 64)
                                row = br[r, bass.ds(i, 1), :].rearrange("p a t -> p (a t)")
                                o = ps[r, 6 + u % 2, 0:P]
                                if u >= 4:
                                    dst = row[:, 0:256].rearrange("p (r c) -> p r c", c=64)[:, :, 32 * (u - 4):32 * (u - 4) + 32]
                                    o = o.rearrange("p (r c) -> p r c", c=32)
                                else:
                                    dst = row[:, 256:T].rearrange("p (r c) -> p r c", c=64)[:, :, 16 * u:16 * u + 16]
                                    o = o.rearrange("p (r c) -> p r c", c=16)
                                v_.do(gated[1], ve.tensor_tensor(dst, dst, o, ALU.mult))
                        attention_units(1, i, 0, 6, 6, bias_of, gate)
                    v_.loop(8, [(sc_biased[1], 6), (sc_max[1], 6), (p_inv[1], 6), (p_done[1], 6), (gated[1], 12)], na)
                else:
                    dve.wait_ge(bpar_in, 64)
                    v_.do(lora_mix, ve.tensor_scalar(
                        one_minus_ka[:, :].unsqueeze(2), bpar[:, 0:8 * BPAR].rearrange("p (k c) -> p k c", c=BPAR)[:, :, KA:KA + 1],
                        -1.0, 1.0, ALU.mult, ALU.add))
                    for d in range(2):
                        dve.wait_ge(lora_shift, d + 1)
                        v_.do(lora_mix, stt(tw[:, d, :], tw[:, d, :], bpar[:, 8 * BPAR + d:8 * BPAR + d + 1],
                                            lora[:, 1:1 + WT], ALU.mult, ALU.add))
                    v_.do(lora_mix, ve.memset(bonus[:, :], 0.0))

                    def par(p, c):
                        return bpar[:, bass.ds(p * BPAR + c, 1)]

                    def pair(p):
                        v_.do(par_ready, ve.tensor_copy(par_now[:, :], bpar[:, bass.ds(p * BPAR, BPAR)]))
                        for d in range(2):
                            for n in range(3):
                                dve.wait_ge(shifted, p * 6 + 3 * d + n + 1)
                                v_.do(mixed, stt(xd[:, n, :], xd[:, n, :], par(p, MU + 3 * d + n), h_p[:, n, 1:1 + WT],
                                                 ALU.mult, ALU.add))
                            dve.wait_ge(up_act, p * 8 + 4 * d + 4)
                            at = slice(None) if d == 0 else slice(None, None, -1)
                            v_.do(summed, ve.tensor_tensor_scan(out=cum[:, at], data0=reset[:, d, at], data1=sg[:, at],
                                                                initial=0.0, op0=ALU.mult, op1=ALU.add))
                            v_.do(kk_raw, ve.tensor_scalar(kk[:, :], xd[:, 1, :], par(p, KG), None, ALU.mult))
                            dve.wait_ge(kk_ss, p * 2 + d + 1)
                            for j, (at_, w) in enumerate(((0, 257), (257, 512))):
                                v_.do(kk_max, ve.tensor_scalar(tmp[:, at_:at_ + w], ps[:, 6 + j, 0:w], 1e-24, None, ALU.max))
                            dve.wait_ge(kk_root, p * 2 + d + 1)
                            v_.do(prepared, ve.reciprocal(tmp[:, :], tmp[:, :]))
                            v_.do(prepared, ve.tensor_tensor(kk[:, :], kk[:, :], tmp[:, :], ALU.mult))
                            v_.do(prepared, ve.tensor_scalar(ke[:, :], av[:, :], par(p, KA), one_minus_ka[:, bass.ds(p, 1)],
                                                             ALU.mult, ALU.add))
                            v_.do(prepared, ve.tensor_tensor(ke[:, :], ke[:, :], xd[:, 1, :], ALU.mult))
                            v_.do(bon_in, stt(tmp[:, :], xd[:, 0, :], par(p, RK), ke[:, :], ALU.mult, ALU.mult))
                            dve.wait_ge(decays, p * 6 + 3 * d + 3)
                            v_.do(prepared, ve.tensor_tensor(av[:, :], av[:, :], cum[:, :], ALU.mult))
                            v_.do(prepared, ve.tensor_tensor(ke[:, :], ke[:, :], cum[:, :], ALU.mult))
                            v_.do(prepared, ve.tensor_tensor(dx[:, :], dx[:, :], kk[:, :], ALU.mult))
                            v_.do(prepared, ve.tensor_tensor(av[:, :], av[:, :], kk[:, :], ALU.mult))
                            dve.wait_ge(bon_ps, p * 2 + d + 1)
                            dst = bonus if d == 0 else tmp
                            for j, (at_, w) in enumerate(((0, 257), (257, 512))):
                                ins = ve.tensor_tensor(dst[:, at_:at_ + w], xd[:, 2, at_:at_ + w], ps[:, 6 + j, 0:w], ALU.mult)
                                v_.do(prepared if j == 0 or d == 1 else bon_done, ins)
                            if d == 1:
                                v_.do(bon_done, ve.tensor_tensor(bonus[:, :], bonus[:, :], tmp[:, :], ALU.add))
                                v_.do(bon_done, ve.memset(tmp[:, 0:1], 0.0))
                            for qn in range(3):
                                first = quad_at(d, qn)
                                q = p * 6 + (3 * d + qn)

                                def quad(buf):
                                    return buf[:, first:first + 256].rearrange("p (c t) -> p c t", c=QUAD)
                                if d or qn:
                                    dve.wait_ge(c_y, q * 4)
                                v_.do(q_dve, ve.tensor_copy(ar[:, :, 0:C], quad(dx)))
                                for h in range(2):
                                    r = slice(64 * h, 64 * h + 64)
                                    v_.do(q_dve, ve.tensor_copy(b_bd[r, :, 64 * h:64 * h + 64], quad(av)[r]))
                                for n, dst in enumerate((ab, ak)):
                                    dve.wait_ge(q_pairs, q * 2 + n + 1)
                                    v_.do(q_masked, ve.tensor_tensor(
                                        dst[:, :, :], ps[:, 2 + n, :].rearrange("p (c t) -> p c t", c=QUAD),
                                        mask[:, d, :].unsqueeze(1).to_broadcast([P, QUAD, P]), ALU.mult))
                                dve.wait_ge(q_levels, q * 12 + 12)
                                eye = ident.unsqueeze(1).to_broadcast([P, QUAD, P])
                                v_.do(i_x, ve.tensor_tensor(inv_t[:, :, :], eye, lev[:, 0, :, :], ALU.subtract))
                                dve.wait_ge(i_prod, q * 6 + 1)
                                v_.do(i_x, ve.tensor_tensor(inv[:, :, :], eye, ps[:, 7, :].rearrange("p (c t) -> p c t", c=QUAD),
                                                            ALU.subtract))
                                for v in range(1, LEVELS):
                                    dve.wait_ge(i_next, q * 5 + v)
                                    for b, dst in ((3, inv_t), (4, inv)):
                                        if b == 3 or v < LEVELS - 1:
                                            flat = dst[:, :, :].rearrange("p c t -> p (c t)")
                                            v_.do(i_x, ve.tensor_tensor(flat, flat, ps[:, b, :], ALU.subtract))
                                if qn < 2:
                                    v_.do(c_st, ve.memset(state[:, 0, :], 0.0))
                                order = range(QUAD) if d == 0 else range(QUAD - 1, -1, -1)
                                for m, c in enumerate(order):
                                    dve.wait_ge(c_s, q * 4 + m + 1)
                                    last = first + c * C + (C - 1 if d == 0 else 0)
                                    v_.do(c_st, ve.tensor_scalar(state[:, (m + 1) % 2, :], ps[:, 7, c * P:(c + 1) * P],
                                                                 dd[:, last:last + 1], None, ALU.mult))
                                dve.wait_ge(c_y, q * 4 + 4)
                                out = ps[:, 2, :].rearrange("p (c t) -> p c t", c=QUAD)[:, :, C:P]
                                if d == 0:
                                    v_.do(c_yt, ve.tensor_copy(quad(ysum), out))
                                else:
                                    v_.do(c_yt, ve.tensor_tensor(quad(ysum), quad(ysum), out, ALU.add))
                        dve.wait_ge(g_mean, p + 1)
                        for j, (at_, w) in enumerate(((0, 257), (257, 512))):
                            v_.do(g_centred, stt(ysum[:, at_:at_ + w], ps[:, 2 + j, 0:w], -1.0 / 64, ysum[:, at_:at_ + w],
                                                 ALU.mult, ALU.add))
                        dve.wait_ge(g_var, p + 1)
                        for j, (at_, w) in enumerate(((0, 257), (257, 512))):
                            v_.do(g_eps, ve.tensor_scalar(tmp[:, at_:at_ + w], ps[:, 4 + j, 0:w], 1.0 / 64, GN_EPS,
                                                          ALU.mult, ALU.add))
                        dve.wait_ge(g_root, p + 1)
                        v_.do(g_done, ve.reciprocal(tmp[:, :], tmp[:, :]))
                        v_.do(g_done, stt(ysum[:, :], ysum[:, :], par(p, LNG), tmp[:, :], ALU.mult, ALU.mult))
                        v_.do(g_done, stt(ysum[:, :], ysum[:, :], par(p, LNB), bonus[:, :], ALU.add, ALU.add))
                        for g, (first, n) in enumerate(GROUPS):
                            dst = br[:, bass.ds(p, 1), first:first + n].rearrange("p a t -> p (a t)")
                            v_.do(g_done, ve.tensor_tensor(dst, dst, ysum[:, WKV_AT[g]:WKV_AT[g] + n], ALU.mult))
                    v_.loop(8, [(par_ready, 1), (mixed, 6), (summed, 2), (kk_raw, 2), (kk_max, 4), (prepared, 19), (bon_in, 2), (bon_done, 3),
                                (q_dve, 18), (q_masked, 12), (i_x, 66), (c_st, 28), (c_yt, 6), (g_centred, 2), (g_eps, 2),
                                (g_done, 5)], pair)

                def residual(k):
                    v_.do(scaled, stt(xn[:, k, :], xn[:, k, :], gain[:, (4 + l) * KD + k:(4 + l) * KD + k + 1], rstd[:, 0:T],
                                      ALU.mult, ALU.mult))
                    v_.do(normed, ve.tensor_tensor(xT[:, k, :], xT[:, k, :], xn[:, k, :], ALU.add))
                norm(3 * l + 2, GROUPS, T, residual)


def _tiles(w):
    k, n = w.shape
    return np.ascontiguousarray(w.reshape(k // P, P, n // P, P).transpose(2, 1, 0, 3).reshape(n // P, P, k))


def _features(v):
    return np.ascontiguousarray(v.reshape(-1, KD, P).transpose(2, 0, 1).reshape(P, -1))


def _acts(a, b):
    both = np.concatenate([a[0], b[0]], 0)
    return np.ascontiguousarray(both.T.reshape(KD, P, -1).transpose(1, 0, 2))


def _pairs(w, skip, names):
    t = _tiles(w)
    body = 8 * names
    rest = t[body + skip:]
    mixer = [t[n * 8 + p] for p in range(8) for n in range(names)]
    return np.ascontiguousarray(np.concatenate([rest, t[body:body + skip], np.stack(mixer)], 0))


def _constants():
    square = np.zeros((P, 3, P), np.float32)
    square[:, 0] = np.eye(P)
    square[:, 1] = 1
    square[:64, 2, :64] = 1
    square[64:, 2, 64:] = 1
    reset = np.ones((P, 2, WT), np.float32)
    for g, at in enumerate(WKV_AT):
        for c in range(GROUPS[g][1] // C):
            reset[:, 0, at + c * C] = 0
            reset[:, 1, at + c * C + C - 1] = 0
    reset[:, :, 256] = 0
    j, t = np.arange(C)[:, None], np.arange(C)[None, :]
    mask = np.zeros((P, 2, P), np.float32)
    level = np.zeros((P, 2, LEVELS, C), np.float32)
    for d in range(2):
        a, b = (j, t) if d == 0 else (t, j)
        m = np.concatenate([a < b, a <= b], 1)
        mask[:, d] = np.concatenate([m, m], 0)
        for v in range(LEVELS):
            s = 1 << v
            m = (a // (2 * s) == b // (2 * s)) & ((a // s) % 2 == 0) & ((b // s) % 2 == 1)
            level[:, d, v] = np.concatenate([m, m], 0)
    return square, reset, mask, level


def _windows():
    out = []
    for cols, keys in ((range(0, 16), range(0, 32)), (range(16, 32), range(8, 40)), (range(48, 64), range(32, 64))):
        out.append((np.array([(r, c) for r in range(8) for c in cols]), np.array([(r, c) for r in range(8) for c in keys])))
    for i in range(2):
        out.append((np.array([(r, c) for r in range(4) for c in range(32 * i, 32 * i + 32)]),
                    np.array([(r, c) for r in range(4) for c in range(64)])))
    return out


def _bias(rpb):
    bias = np.zeros((8, P, 5, 2, 256), np.float32)
    mask = np.zeros((P, 5, 256), np.float32)
    for n, (q, k) in enumerate(_windows()):
        dr = k[None, :, 0] - q[:, None, 0] + 7
        dc = np.clip(k[None, :, 1] - q[:, None, 1], -15, 15) + 15
        bias[:, :, n] = rpb.reshape(8, 2, 15, 31)[:, :, dr, dc].transpose(0, 2, 1, 3)
        start = np.clip(q[:, 1] - 8, 0, 48)[:, None]
        mask[:, n] = np.where((k[None, :, 1] >= start) & (k[None, :, 1] < start + 16), 0.0, NEG)
    return bias.reshape(8, P, -1), mask


def _inputs(i):
    a = {k: np.asarray(v) for k, v in i.items()}
    out = {"x": _acts(a["x_prompt"], a["x_sample"]), "mem": _acts(a["mem_prompt"], a["mem_sample"])}
    out["w_mem"] = np.concatenate([_tiles(w) for w in a["w_mem_kv"]], 0)
    out["w_a"] = np.concatenate([_pairs(w, 0, 2) for w in a["a_w_in"]], 0)
    out["w_b"] = _pairs(a["b_w_in"][0], 1, 3)
    out["w_c"] = _pairs(a["c_w_in"][0], 0, 3)
    out["w_out"] = np.concatenate([_tiles(w) for w in (a["a_w_out"][0], a["b_w_out"][0], a["c_w_out"][0], a["a_w_out"][1])], 0)
    out["gains"] = np.concatenate([_features(a[n]) for n in ("pre_norm", "post_norm", "mem_norm")], 1)
    par = []
    for j in range(2):
        rows = np.concatenate([a["a_conv_w"][j], a["a_conv_b"][j:j + 1], a["a_ln_g"][j:j + 1], a["a_ln_b"][j:j + 1]], 0)
        par.append(rows.reshape(APAR, KD, P).transpose(2, 1, 0).reshape(P, -1))
    out["a_par"] = np.stack(par)
    mu = a["b_mu"][0]
    rows = [mu[d, n * D:(n + 1) * D] for d in range(2) for n in range(3)]
    rows += [a["b_w0"][0, 0], a["b_w0"][0, 1], a["b_a0"][0, 0], a["b_a0"][0, 1], a["b_k_k"][0], a["b_k_a"][0],
             a["b_r_k"][0].reshape(-1), a["b_ln_g"][0], a["b_ln_b"][0]]
    rows = np.stack(rows).reshape(BPAR, KD, P).transpose(2, 1, 0).reshape(P, -1)
    out["b_par"] = np.concatenate([rows, mu[:, 3 * D:].T], 1)
    up = np.concatenate([a["b_w_up"][0], a["b_a_up"][0]], 1)
    out["lora_up"] = up.reshape(2, P, 8, P).transpose(2, 1, 0, 3)
    square, reset, mask, level = _constants()
    out["bias"], window = _bias(a["c_rpb"][0])
    out["square_c"], out["scan_c"], out["level_c"], out["window_c0"], out["window_c1"] = square, reset, level, window, mask
    return {k: np.ascontiguousarray(v) for k, v in out.items()}


def _declare(nc, arrays, layers=4):
    ap = {n: nc.dram_tensor(f"in_{n}", v.shape, mybir.dt.from_np(v.dtype), kind="ExternalInput").ap()
          for n, v in arrays.items()}
    y = nc.dram_tensor("out_y", (P, KD, T), F32, kind="ExternalOutput").ap()
    trunk_kernel(nc, ap["x"], ap["mem"], ap["w_mem"], ap["w_a"], ap["w_b"], ap["w_c"], ap["w_out"], ap["gains"], ap["a_par"],
                 ap["b_par"], ap["lora_up"], ap["bias"], ap["square_c"], ap["scan_c"], ap["level_c"],
                 (ap["window_c0"], ap["window_c1"]), y, layers)


def _outputs(y):
    out = y.transpose(1, 0, 2).reshape(D, T).T
    return np.ascontiguousarray(out[None, 0:256]), np.ascontiguousarray(out[None, 256:T])


def kernel(**inputs):
    import concourse.bacc as bacc
    from concourse.bass_utils import run_bass_kernel_spmd as run

    arrays = _inputs(inputs)
    nc = bacc.Bacc("TRN2", target_bir_lowering=False, num_devices=1)
    _declare(nc, arrays)
    r = run(nc, [{f"in_{k}": v for k, v in arrays.items()}], core_ids=[0])
    return _outputs(r.results[0]["out_y"])
```

```python
import math
from contextlib import ExitStack

import concourse.bass as bass
import numpy as np
from concourse import mybir

F32 = mybir.dt.float32
ACT = mybir.ActivationFunctionType
ALU = mybir.AluOpType
AX_X = mybir.AxisListType.X

P = 128
D = 1024
KD = D // P
GROUPS = ((0, 256), (256, 512))
T = 768
MEM = 512
KB = (D + 256) // P
KINDS = (0, 1, 2, 0)
TAPS = 31
HALO = TAPS // 2
CONV_IN = T + 4 * HALO
CONV_OUT = CONV_IN - 2 * HALO
CONV_AT = (0, 256 + 2 * HALO)
RMS_EPS, LN_EPS, GN_EPS = 1e-6, 1e-5, 64e-5
DECAY = math.exp(-0.5)
HEAD_SCALE = 64 ** -0.5
C = 64
QUAD = 4
WT = T + 1
WKV_AT = (0, 257)
LEVELS = 6
BPAR = 15
MU, W0, A0, KG, KA, RK, LNG, LNB = 0, 6, 8, 10, 11, 12, 13, 14
APAR = TAPS + 3
NEG = -1e30
PREPARED = 26
KEY_START = (0, 8, 24, 32)

PAIR_TILES = {0: 2, 1: 3, 2: 3}


def phases(kind):
    out = [("mem", 2, 2), ("qg", 6, 2)]
    if kind == 1:
        out.append(("lora", 1, 1))
    return out + [("pairs", 8, PAIR_TILES[kind]), ("out", 4, 2)]


def schedule():
    used, free, chunks, plan = [0, 0, 0], [0, 0, 0], 0, {}
    for l, kind in enumerate(KINDS):
        for name, n, tiles in phases(kind):
            per = tiles if name == "mem" else 2 * tiles
            plan[l, name] = (list(used), chunks, n, tiles, per, list(free))
            for s in range(tiles):
                used[s] += n
                free[s] = chunks + (n - 1) * per + (s + 1) * per // tiles
            chunks += n * per
    return plan


class Serial:

    def __init__(self, eng):
        self.eng, self.count, self.step, self.i = eng, {}, {}, 0

    def go(self, sem, ins):
        ins.then_inc(sem, 1)
        self.count[sem.name] = self.count.get(sem.name, 0) + 1

    def do(self, sem, ins):
        self.go(sem, ins)
        n, k = self.count[sem.name], self.step.get(sem.name)
        self.eng.wait_ge(sem, n if k is None else self.i * k + n)

    def loop(self, n, steps, body):
        before = dict(self.count)
        self.step = {s.name: k for s, k in steps}
        with self.eng.Fori(0, n) as i:
            self.i = i
            body(i)
        for s, k in steps:
            assert self.count.get(s.name, 0) - before.get(s.name, 0) == k, (s.name, k, self.count.get(s.name, 0) - before.get(s.name, 0))
            self.count[s.name] = before.get(s.name, 0) + n * k
        changed = {s for s in self.count if self.count[s] != before.get(s, 0)} - set(self.step)
        assert not changed, changed
        self.step, self.i = {}, 0


def trunk_kernel(nc, x, mem, w_mem, w_a, w_b, w_c, w_out, gains, a_par, b_par, lora_up, bias,
                 square_c, scan_c, level_c, window_c, y, layers=4):
    plan = schedule()
    ctx = ExitStack()
    with ctx:
        def sem(name):
            return ctx.enter_context(nc.semaphore(name))

        def sb(name, *shape, stack=ctx):
            return stack.enter_context(nc.sbuf_tensor(name, [P, *shape], F32))

        ps = ctx.enter_context(nc.psum_tensor("ps", [P, 8, 512], F32))
        xn = sb("xn", KD, T)
        ring = sb("ring", 3, KB * P)
        br = sb("br", KB, T)
        gain = sb("gain", 12 * KD)
        square = sb("square", 3, P)
        ident, ones, bones = square[:, 0, :], square[:, 1, :], square[:, 2, :]

        region = ExitStack()
        xT = sb("xT", KD, T, stack=region)
        sq = sb("sq", 2, 800, stack=region)
        rstd = sb("rstd", 800, stack=region)
        mk = sb("mk", 2, MEM, stack=region)
        mvf = sb("mvf", 2, MEM, stack=region)
        mv = sb("mv", 4, 256, stack=region)
        mq = sb("mq", 2, T, stack=region)
        attention = ExitStack()
        exps = sb("exps", 2, 512, stack=attention)
        probs_t = sb("probs_t", 2, 512, stack=attention)
        stat = sb("stat", 2, 8, stack=attention)
        scores = sb("scores", 2, 512, stack=attention)
        conv = ExitStack()
        z_in = sb("z_in", T, stack=conv)
        z_gate = sb("z_gate", T, stack=conv)
        z_pad = sb("z_pad", CONV_IN, stack=conv)
        z_out = sb("z_out", KD, CONV_OUT, stack=conv)
        apar = sb("apar", 8 * APAR, stack=conv)
        conv.close()
        na = ExitStack()
        na_q = sb("na_q", T, stack=na)
        na_k = sb("na_k", T, stack=na)
        na_v = sb("na_v", 5, 256, stack=na)
        na_vt = sb("na_vt", 10, P, stack=na)
        na_bias = sb("na_bias", 5, 2, 256, stack=na)
        na_bm = sb("na_bm", 5, 2, 256, stack=na)
        na_mask = sb("na_mask", 5, 256, stack=na)
        na.close()
        attention.close()
        region.close()
        wkv = ExitStack()
        tw = sb("tw", 2, WT, stack=wkv)
        bpar = sb("bpar", 8 * BPAR + 2, stack=wkv)
        one_minus_ka = sb("one_minus_ka", 8, stack=wkv)
        par_now = sb("par_now", BPAR, stack=wkv)
        up = sb("up", 2, P, stack=wkv)
        reset = sb("reset", 2, WT, stack=wkv)
        mask = sb("mask", 2, P, stack=wkv)
        level = sb("level", 2, LEVELS, C, stack=wkv)
        h_p = sb("h_p", 3, WT + 2, stack=wkv)
        lora = h_p[:, 0, :]
        xr = sb("xr", 2, WT, stack=wkv)
        xv = sb("xv", 2, WT, stack=wkv)
        av = sb("av", 2, WT, stack=wkv)
        ke = sb("ke", 2, WT, stack=wkv)
        dx = sb("dx", 2, WT, stack=wkv)
        dend = sb("dend", 2, 12, stack=wkv)
        xk = sb("xk", WT, stack=wkv)
        sg = sb("sg", WT, stack=wkv)
        tmp = sg
        cum = sb("cum", WT, stack=wkv)
        dd = sb("dd", WT, stack=wkv)
        kk = sb("kk", WT, stack=wkv)
        ysum = sb("ysum", WT, stack=wkv)
        bonus = sb("bonus", WT, stack=wkv)
        ar = sb("ar", 2, QUAD, P, stack=wkv)
        a_bd = sb("a_bd", 2, QUAD, P, stack=wkv)
        b_bd = sb("b_bd", 2, QUAD, P, stack=wkv)
        k_bd = sb("k_bd", 2, QUAD, P, stack=wkv)
        v_bd = sb("v_bd", 2, QUAD, P, stack=wkv)
        ab = sb("ab", 2, QUAD, P, stack=wkv)
        ak = sb("ak", 2, QUAD, P, stack=wkv)
        ak_bd = sb("ak_bd", 2, QUAD, P, stack=wkv)
        bt = sb("bt", 2, QUAD, P, stack=wkv)
        kt = sb("kt", 2, QUAD, P, stack=wkv)
        vt = sb("vt", 2, QUAD, P, stack=wkv)
        inv_t = sb("inv_t", 2, QUAD, P, stack=wkv)
        lev = sb("lev", 2, 2, QUAD, P, stack=wkv)
        inv, prod, unew = b_bd, v_bd, k_bd
        rhs = prod
        state = sb("state", 2, 2, P, stack=wkv)
        wkv.close()

        spill = nc.dram_tensor("spill", (P, KD, T), F32, kind="Internal").ap()
        const_in, x_in, y_out = sem("const_in"), sem("x_in"), sem("y_out")
        x_spilled, x_back = sem("x_spilled"), sem("x_back")
        mem_in, apar_in, bpar_in, up_in, bias_in, mask_in = (sem(n) for n in
            ("mem_in", "apar_in", "bpar_in", "up_in", "bias_in", "mask_in"))
        ring_in = [sem(f"ring_in{s}") for s in range(3)]
        cols_done, cols_taken = sem("cols_done"), sem("cols_taken")
        sq_ready, sq_used, ms_taken, root, inverse, scaled = (sem(n) for n in
            ("sq_ready", "sq_used", "ms_taken", "root", "inverse", "scaled"))
        normed = sem("normed")
        mv_turned, mv_taken = sem("mv_turned"), sem("mv_taken")
        sc_done, sc_biased, sc_max, ex_done, p_inv, p_done, tp_done, pt_done, av_done, gated = (
            [sem(f"{n}{a}") for a in range(2)] for n in
            ("sc_done", "sc_biased", "sc_max", "ex_done", "p_inv", "p_done", "tp_done", "pt_done", "av_done", "gated"))
        bm_ready, v_window, vt_turned, vt_taken = (sem(n) for n in ("bm_ready", "v_window", "vt_turned", "vt_taken"))
        glu_done, conv_done = sem("glu_done"), sem("conv_done")
        mean_done, centred, lsq_ready, lsq_used, l_ms, l_root, l_inv, l_scaled, l_silu, l_gated = (sem(n) for n in
            ("mean_done", "centred", "lsq_ready", "lsq_used", "l_ms", "l_root", "l_inv", "l_scaled", "l_silu", "l_gated"))
        w_zero, lora_mix, lora_shift, lora_act = sem("w_zero"), sem("lora_mix"), sem("lora_shift"), sem("lora_act")
        shifted, mixed, up_done, up_act, summed, less, decays = (sem(n) for n in
            ("shifted", "mixed", "up_done", "up_act", "summed", "less", "decays"))
        kk_raw, kk_sq, kk_ss, kk_max, kk_root, prepared, bon_in, bon_ps, bon_done = (sem(n) for n in
            ("kk_raw", "kk_sq", "kk_ss", "kk_max", "kk_root", "prepared", "bon_in", "bon_ps", "bon_done"))
        q_dve, q_act, q_pairs, q_turn, q_masked, q_turned, q_akbd, q_levels = (sem(n) for n in
            ("q_dve", "q_act", "q_pairs", "q_turn", "q_masked", "q_turned", "q_akbd", "q_levels"))
        i_prod, i_taken, i_next, i_x = sem("i_prod"), sem("i_taken"), sem("i_next"), sem("i_x")
        c_r, c_rt, c_u, c_ut, c_s, c_st, c_y, c_yt = (sem(n) for n in
            ("c_r", "c_rt", "c_u", "c_ut", "c_s", "c_st", "c_y", "c_yt"))
        g_mean, g_centred, g_sq, g_var, g_eps, g_root, g_done = (sem(n) for n in
            ("g_mean", "g_centred", "g_sq", "g_var", "g_eps", "g_root", "g_done"))
        b_start, par_ready, y_zero = sem("b_start"), sem("par_ready"), sem("y_zero")
        block = ctx.enter_context(nc.Block())

        def tok(g, at=(0, 256)):
            return slice(at[g], at[g] + GROUPS[g][1])

        A_LAYERS = [l for l in range(layers) if KINDS[l] == 0]

        def quad_at(d, qn):
            return (0, WKV_AT[1], WKV_AT[1] + 256)[qn] if d == 0 else (0, WKV_AT[1] + 256, WKV_AT[1])[qn]

        @block.sync
        def _(sp):
            sp.dma_start(square[:, :, :], square_c).then_inc(const_in, 16)
            sp.dma_start(gain[:, :], gains).then_inc(const_in, 16)
            for l in range(layers):
                kind = KINDS[l]
                weights = {"mem": (w_mem, 4 * l), "out": (w_out, 8 * l)}
                body = {0: (w_a, 28 * (l // 3)), 1: (w_b, 0), 2: (w_c, 0)}[kind]
                weights["qg"] = body
                weights["lora"] = (body[0], 12)
                weights["pairs"] = (body[0], body[1] + (13 if kind == 1 else 12))
                if l:
                    sp.wait_ge(normed, 24 * l)
                sp.dma_start(xn[:, :, 0:MEM], mem).then_inc(mem_in, 16)
                if l == 0:
                    sp.dma_start(xT[:, :, :], x).then_inc(x_in, 16)
                for name, n, tiles in phases(kind):
                    used, chunks, n, tiles, per, free = plan[l, name]
                    src, first = weights[name]
                    width = (KB if name == "out" else KD) * P
                    if name == "pairs" and kind == 0:
                        sp.wait_ge(gated[0], 12 * (l + 1))
                        sp.dma_start(apar[:, :], a_par[l // 3]).then_inc(apar_in, 16)
                    if name == "lora":
                        sp.wait_ge(normed, 24 * l + 16)
                        sp.dma_start(spill, xT[:, :, :]).then_inc(x_spilled, 16)
                        sp.wait_ge(gated[0], 12 * (l + 1))
                        sp.wait_ge(x_spilled, 16)
                        for dst, s in ((bpar[:, :], b_par), (reset[:, :, :], scan_c), (mask[:, :, :], window_c[1]),
                                       (level[:, :, :, :], level_c)):
                            sp.dma_start(dst, s).then_inc(bpar_in, 16)
                    if name == "pairs" and kind == 2:
                        sp.wait_ge(gated[0], 12 * (l + 1))
                        sp.dma_start(na_mask[:, :, :], window_c[0]).then_inc(mask_in, 16)

                    def load(i, first_free=False):
                        for s in range(tiles):
                            before = chunks - per + (s + 1) * per // tiles
                            sp.wait_ge(cols_done, free[s] if first_free else i * per + before)
                            sp.dma_start(ring[:, s, 0:width],
                                         src[bass.ds(first + i * tiles + s, 1), :, :].rearrange("a p c -> (a p) c"))\
                              .then_inc(ring_in[s], 16)
                        if name == "pairs" and kind == 1:
                            sp.wait_ge(up_done, 8 * i)
                            sp.dma_start(up[:, :, :], lora_up[bass.ds(i, 1), :, :, :].rearrange("a p d c -> (a p) d c"))\
                              .then_inc(up_in, 16)
                        if name == "pairs" and kind == 2:
                            sp.wait_ge(bm_ready, i)
                            sp.dma_start(na_bias[:, :, :, :].rearrange("p a h k -> p (a h k)"),
                                         bias[bass.ds(i, 1), :, :].rearrange("a p k -> (a p) k")).then_inc(bias_in, 16)

                    load(0, True)
                    if name == "out" and kind == 1:
                        sp.wait_ge(g_done, 40)
                        sp.dma_start(xT[:, :, :], spill).then_inc(x_back, 16)
                    if n > 1:
                        with sp.Fori(1, n) as i:
                            load(i)
            sp.wait_ge(normed, 24 * layers)
            sp.dma_start(y, xT[:, :, :]).then_inc(y_out, 16)
            sp.wait_ge(y_out, 16)

        @block.tensor
        def _(pe):
            mm = nc.tensor.matmul

            def project(l, name, i, s, c, src, token_chunks, kd=KD):
                used, chunks, n, tiles, per, _ = plan[l, name]
                pe.wait_ge(ring_in[s], (i + used[s] + 1) * 16)
                for j, (at, w) in enumerate(token_chunks):
                    if l or name != "mem" or i:
                        pe.wait_ge(cols_taken, i * per + chunks + c + j - 1)
                    for k in range(kd):
                        ins = mm(ps[:, (c + j) % 2, 0:w], ring[:, s, k * P:(k + 1) * P], src[:, k, at:at + w],
                                 start=k == 0, stop=k == kd - 1)
                    ins.then_inc(cols_done, 1)

            def project_steps(l, name, i, tiles):
                used, chunks, n, _, per, _ = plan[l, name]
                for s in range(tiles):
                    for j, (at, w) in enumerate(GROUPS):
                        for k in range(KD):
                            if k == 0:
                                if j == 0:
                                    pe.wait_ge(ring_in[s], i * 16 + (used[s] + 1) * 16)
                                pe.wait_ge(cols_taken, i * per + (chunks + 2 * s + j - 1))
                            ins = mm(ps[:, j, 0:w], ring[:, s, k * P:(k + 1) * P], xn[:, k, at:at + w],
                                     start=k == 0, stop=k == KD - 1)
                            if k == KD - 1:
                                ins.then_inc(cols_done, 1)
                            yield

            def sum_squares(q, widths):
                for k in range(KD):
                    pe.wait_ge(sq_ready, 8 * q + k + 1)
                    for j, (at, w) in enumerate(widths):
                        ins = mm(ps[:, j, 0:w], ones, sq[:, k % 2, at:at + w], start=k == 0, stop=k == KD - 1)
                    ins.then_inc(sq_used, 1)

            def attention_units(a, i, base, units, s_mm, v_of, per):
                n = len(units)

                def at(c):
                    return base + i * per + c

                def score(u):
                    if u >= 2:
                        pe.wait_ge(ex_done[a], 2 * at(u - 1))
                    s_mm(u).then_inc(sc_done[a], 1)

                score(0)
                for u in range(n):
                    if u + 1 < n:
                        score(u + 1)
                    pe.wait_ge(p_done[a], at(u + 1))
                    for h in range(2):
                        for c in range(2):
                            ins = nc.tensor.transpose(ps[:, 4 + u % 2, (2 * h + c) * P:(2 * h + c + 1) * P],
                                                      exps[:, u % 2, h * 256 + c * P:h * 256 + (c + 1) * P], ident)
                    ins.then_inc(tp_done[a], 1)
                    pe.wait_ge(pt_done[a], at(u + 1))
                    if u >= 2:
                        pe.wait_ge(gated[a], at(u - 1))
                    for h in range(2):
                        for c in range(2):
                            ins = mm(ps[64 * h:64 * h + 64, 6 + u % 2, 0:P], v_of(u, h, c),
                                     probs_t[:, u % 2, (2 * h + c) * P:(2 * h + c + 1) * P], start=c == 0, stop=c == 1)
                    ins.then_inc(av_done[a], 1)

            pe.wait_ge(const_in, 32)
            for l in range(layers):
                kind = KINDS[l]
                sum_squares(3 * l, [(0, MEM)])
                pe.wait_ge(normed, 24 * l + 8)
                for i in range(2):
                    for s in range(2):
                        project(l, "mem", i, s, s, xn, [(0, MEM)])
                pe.wait_ge(cols_taken, plan[l, "qg"][1])
                for m in range(4):
                    for c in range(2):
                        ins = nc.tensor.transpose(ps[:, 2 + m // 2, (m % 2) * 256 + c * P:(m % 2) * 256 + (c + 1) * P],
                                                  mvf[:, c, m * P:(m + 1) * P], ident)
                ins.then_inc(mv_turned, 1)
                sum_squares(3 * l + 1, GROUPS)
                pe.wait_ge(normed, 24 * l + 16)
                with pe.Fori(0, 6) as i:
                    for s in range(2):
                        project(l, "qg", i, s, 2 * s, xn, GROUPS)
                pe.wait_ge(cols_taken, plan[l, "qg"][1] + 24)
                pe.wait_ge(mv_taken, l + 1)

                def mem_scores(u):
                    hp, t = u // 6, u % 6
                    g = int(t >= 2)
                    for h in range(2):
                        r = slice(64 * h, 64 * h + 64)
                        ins = mm(ps[:, 2 * (u % 2) + h, 0:256], mq[r, hp, t * P:(t + 1) * P],
                                 mk[r, hp, g * 256:(g + 1) * 256], start=True, stop=True)
                    return ins

                def mem_v(u, h, c):
                    hp, t = u // 6, u % 6
                    return mv[:, 2 * int(t >= 2) + c, (2 * hp + h) * 64:(2 * hp + h + 1) * 64]

                attention_units(0, 0, 12 * l, range(12), mem_scores, mem_v, 0)
                pe.wait_ge(gated[0], 12 * (l + 1))

                if kind == 0:
                    with pe.Fori(0, 8) as i:
                        for s in range(2):
                            project(l, "pairs", i, s, 2 * s, xn, GROUPS)
                    la = l // 3
                    pe.wait_ge(conv_done, (TAPS + 1) * 8 * (la + 1))
                    half = CONV_OUT // 2
                    for k in range(KD):
                        for j in range(2):
                            ins = mm(ps[:, 2 + j, 0:half], ones, z_out[:, k, j * half:(j + 1) * half],
                                     start=k == 0, stop=k == KD - 1)
                    ins.then_inc(mean_done, 1)
                    for k in range(KD):
                        pe.wait_ge(lsq_ready, 8 * la + k + 1)
                        for j in range(2):
                            ins = mm(ps[:, 4 + j, 0:half], ones, sq[:, k % 2, j * half:(j + 1) * half],
                                     start=k == 0, stop=k == KD - 1)
                        ins.then_inc(lsq_used, 1)
                    pe.wait_ge(l_gated, 16 * (la + 1))
                elif kind == 2:
                    with pe.Fori(0, 8) as i:
                        for s in range(3):
                            project(l, "pairs", i, s, 2 * s, xn, GROUPS)
                        pe.wait_ge(cols_taken, plan[l, "pairs"][1] + i * 6 + 6)
                        for n in range(10):
                            ins = nc.tensor.transpose(ps[:, 2 + n // 4, (n % 4) * P:(n % 4 + 1) * P],
                                                      na_v[:, n // 2, (n % 2) * P:(n % 2 + 1) * P], ident)
                        ins.then_inc(vt_turned, 1)
                        pe.wait_ge(vt_taken, i * 3 + 3)

                        def keys(r, u):
                            if u >= 4:
                                return na_k[r, 0:256]
                            return na_k[r, 256:T].rearrange("p (r c) -> p r c", c=64)[:, :, KEY_START[u]:KEY_START[u] + 32]

                        def queries(r, u):
                            at = 256 + u * P if u < 4 else (u - 4) * P
                            return na_q[r, at:at + P]

                        def na_scores(u):
                            for h in range(2):
                                r = slice(64 * h, 64 * h + 64)
                                ins = mm(ps[:, 2 * (u % 2) + h, 0:256], queries(r, u), keys(r, u), start=True, stop=True)
                            return ins

                        def na_values(u, h, c):
                            return na_vt[:, 2 * min(u, 4) + c, h * 64:(h + 1) * 64]

                        attention_units(1, i, 0, range(6), na_scores, na_values, 6)
                        pe.wait_ge(gated[1], i * 12 + 12)
                else:
                    project(l, "lora", 0, 0, 0, xn, GROUPS)
                    parts = ((0, 257), (257, 512))

                    def bank(d, n):
                        return 2 + 3 * d + n

                    def pair(p, filler):
                        for d in range(2):
                            pe.wait_ge(up_in, p * 16 + 16)
                            if d == 0:
                                pe.wait_ge(lora_act, 4)
                            for j, (at, w) in enumerate(parts):
                                mm(ps[:, 2 + j, 0:w], up[0:64, d, :], tw[0:64, d, at:at + w], start=True, stop=True)\
                                    .then_inc(up_done, 1)
                                mm(ps[:, 4 + j, 0:w], up[64:128, d, :], tw[64:128, d, at:at + w], start=True, stop=True)\
                                    .then_inc(up_done, 1)
                            pe.wait_ge(kk_sq, p * 2 + d + 1)
                            for j, (at, w) in enumerate(parts):
                                ins = mm(ps[:, 6 + j, 0:w], bones, tmp[:, at:at + w], start=True, stop=True)
                            ins.then_inc(kk_ss, 1)
                            pe.wait_ge(bon_in, p * 2 + d + 1)
                            for j, (at, w) in enumerate(parts):
                                ins = mm(ps[:, 6 + j, 0:w], bones, tmp[:, at:at + w], start=True, stop=True)
                            ins.then_inc(bon_ps, 1)
                        queue = iter(project_steps(l, "pairs", p + 1, 3) if filler else ())

                        def fill():
                            next(queue, None)

                        for qn in range(3):
                            def at(per, n):
                                return p * (3 * per) + (qn * per + n)

                            def each(b, d, lhs, rhs_, sem_):
                                for c in range(QUAD):
                                    ins = mm(ps[:, bank(d, b), c * P:(c + 1) * P], lhs(c), rhs_(c), start=True, stop=True)
                                if sem_ is not None:
                                    ins.then_inc(sem_, 1)

                            def turn(b, d, src):
                                for c in range(QUAD):
                                    ins = nc.tensor.transpose(ps[:, bank(d, b), c * P:(c + 1) * P], src[:, d, c, :], ident)
                                ins.then_inc(q_turn, 1)

                            for d in range(2):
                                pe.wait_ge(q_dve, at(4, 2 * d + 2))
                                pe.wait_ge(q_act, at(16, 8 * d + 8))
                                if qn:
                                    pe.wait_ge(c_yt, at(2, -1 + d))
                                each(0, d, lambda c: b_bd[:, d, c, :], lambda c: ar[:, d, c, :], q_pairs)
                                each(1, d, lambda c: k_bd[:, d, c, :], lambda c: ar[:, d, c, :], q_pairs)
                                turn(2, d, b_bd)
                            fill()
                            for d in range(2):
                                pe.wait_ge(q_masked, at(4, 2 * d + 1))
                                turn(0, d, k_bd)
                                pe.wait_ge(q_masked, at(4, 2 * d + 2))
                                turn(1, d, v_bd)
                            fill()
                            for d in range(2):
                                pe.wait_ge(q_levels, at(24, 2 * d + 2))
                                pe.wait_ge(q_turned, at(6, d + 1))
                                each(2, d, lambda c: lev[:, d, 0, c, :], lambda c: ident, i_prod)
                            fill()
                            pe.wait_ge(q_turned, at(6, 6))
                            for v in range(1, LEVELS):
                                for d in range(2):
                                    pe.wait_ge(q_levels, at(24, 4 * v + 2 * d + 2))
                                    pe.wait_ge(i_x, at(22, 3 + d if v == 1 else 4 * (v - 1) + 2 * d + 2))
                                    each(0, d, lambda c: lev[:, d, v % 2, c, :], lambda c: inv[:, d, c, :], i_prod)
                                fill()
                                for d in range(2):
                                    pe.wait_ge(i_taken, at(10, 2 * (v - 1) + d + 1))
                                    last = v == LEVELS - 1
                                    each(1, d, lambda c: prod[:, d, c, :], lambda c: inv_t[:, d, c, :], i_next if last else None)
                                    if not last:
                                        each(2, d, lambda c: inv_t[:, d, c, :], lambda c: prod[:, d, c, :], i_next)
                            for m in range(QUAD):
                                def parts_of(d):
                                    c = m if d == 0 else QUAD - 1 - m
                                    return c, state[:, d, m % 2, :]
                                for d in range(2):
                                    c, st = parts_of(d)
                                    if m == 0:
                                        pe.wait_ge(i_x, at(22, 20 + d + 1))
                                        pe.wait_ge(q_akbd, at(4, 2 * d + 2))
                                        ready = d + 1 if qn < 2 else 0
                                    else:
                                        ready = (2 if qn < 2 else 0) + 2 * (m - 1) + d + 1
                                    pe.wait_ge(c_st, p * 28 + (10 * qn + ready))
                                    mm(ps[:, bank(d, 0), 0:P], a_bd[:, d, c, :], st, start=True, stop=False)
                                    mm(ps[:, bank(d, 0), 0:P], ak_bd[:, d, c, :], vt[:, d, c, :], start=False, stop=True)\
                                        .then_inc(c_r, 1)
                                fill()
                                for d in range(2):
                                    c, st = parts_of(d)
                                    pe.wait_ge(c_rt, at(8, 2 * m + d + 1))
                                    mm(ps[:, bank(d, 0), P:2 * P], inv_t[:, d, c, :], rhs[:, d, c, :], start=True, stop=True)\
                                        .then_inc(c_u, 1)
                                fill()
                                for d in range(2):
                                    c, st = parts_of(d)
                                    out = ps[:, bank(d, 0), 2 * P:3 * P]
                                    pe.wait_ge(c_ut, at(8, 2 * m + d + 1))
                                    mm(out, ident, st, start=True, stop=False)
                                    mm(out, kt[:, d, c, :], vt[:, d, c, :], start=False, stop=False)
                                    mm(out, bt[:, d, c, :], unew[:, d, c, :], start=False, stop=True).then_inc(c_s, 1)
                                for d in range(2):
                                    c, st = parts_of(d)
                                    out = ps[:, bank(d, 1), c * P:(c + 1) * P]
                                    mm(out, st, ar[:, d, c, :], start=True, stop=False)
                                    mm(out, vt[:, d, c, :], ak[:, d, c, :], start=False, stop=False)
                                    mm(out, unew[:, d, c, :], ab[:, d, c, :], start=False, stop=True).then_inc(c_y, 1)
                        pe.wait_ge(c_yt, p * 6 + 6)
                        for j, (at_, w) in enumerate(parts):
                            ins = mm(ps[:, 2 + j, 0:w], bones, ysum[:, at_:at_ + w], start=True, stop=True)
                        ins.then_inc(g_mean, 1)
                        pe.wait_ge(g_sq, p + 1)
                        for j, (at_, w) in enumerate(parts):
                            ins = mm(ps[:, 4 + j, 0:w], bones, tmp[:, at_:at_ + w], start=True, stop=True)
                        ins.then_inc(g_var, 1)
                        pe.wait_ge(g_done, p * 5 + 5)

                    for s in range(3):
                        project(l, "pairs", 0, s, 2 * s, xn, GROUPS)
                    with pe.Fori(0, 7) as p:
                        pair(p, True)
                    pair(7, False)

                pe.wait_ge(cols_taken, plan[l, "out"][1])
                with pe.Fori(0, 4) as i:
                    for s in range(2):
                        project(l, "out", i, s, 2 * s, br, GROUPS, KB)
                pe.wait_ge(cols_taken, plan[l, "out"][1] + 16)
                sum_squares(3 * l + 2, GROUPS)
                pe.wait_ge(normed, 24 * l + 24)

        @block.scalar
        def _(act):
            a_ = Serial(act)
            f = nc.scalar.activation

            def wait_cols(l, name, i, c):
                used, chunks, n, tiles, per, _ = plan[l, name]
                act.wait_ge(cols_done, i * per + chunks + c + 1)

            def take(l, name, i, c, dst, func, **kw):
                wait_cols(l, name, i, c)
                a_.do(cols_taken, f(dst, ps[:, c % 2, 0:dst.shape[-1]], func, **kw))

            def squares(q, src, w):
                for k in range(KD):
                    if 8 * q + k >= 2:
                        act.wait_ge(sq_used, 8 * q + k - 1)
                    a_.do(sq_ready, f(sq[:, k % 2, 0:w], src[:, k, 0:w], ACT.Square))
                act.wait_ge(ms_taken, q + 1)
                a_.do(root, f(rstd[:, 0:w], rstd[:, 0:w], ACT.Sqrt))

            def attention_units(a, i, base, n, per, src):
                def at(c):
                    return base + i * per + c

                def exp(u):
                    act.wait_ge(sc_max[a], at(u + 1))
                    for h in range(2):
                        a_.do(ex_done[a], f(exps[:, u % 2, h * 256:(h + 1) * 256], src(u, h), ACT.Exp,
                                            bias=stat[:, u % 2, h:h + 1], accum_out=stat[:, u % 2, 2 + h:3 + h]))

                exp(0)
                for u in range(n):
                    if u + 1 < n:
                        if u >= 1:
                            act.wait_ge(tp_done[a], at(u))
                        exp(u + 1)
                    act.wait_ge(tp_done[a], at(u + 1))
                    if u >= 2:
                        act.wait_ge(av_done[a], at(u - 1))
                    a_.do(pt_done[a], f(probs_t[:, u % 2, :], ps[:, 4 + u % 2, :], ACT.Copy))

            act.wait_ge(mem_in, 16)
            for l in range(layers):
                kind = KINDS[l]
                if l:
                    act.wait_ge(mem_in, 16 * (l + 1))
                squares(3 * l, xn, MEM)
                for c in range(2):
                    take(l, "mem", 0, c, mk[:, c, :], ACT.Copy)
                for c in range(2):
                    take(l, "mem", 1, c, mvf[:, c, :], ACT.Copy)
                act.wait_ge(mv_turned, l + 1)
                a_.do(mv_taken, f(mv[:, :, :].rearrange("p m c -> p (m c)"),
                                  ps[:, 2:4, :].rearrange("p b c -> p (b c)"), ACT.Copy))
                if l == 0:
                    act.wait_ge(x_in, 16)
                squares(3 * l + 1, xT, T)
                for s in range(2):
                    for g in range(2):
                        take(l, "qg", 0, 2 * s + g, mq[:, s, tok(g)], ACT.Copy, scale=HEAD_SCALE)

                def gates(i):
                    for s in range(2):
                        for g in range(2):
                            take(l, "qg", i + 1, 2 * s + g,
                                 br[:, 2 * i + s, tok(g)], ACT.Silu)
                for i in range(5):
                    gates(i)
                attention_units(0, 0, 12 * l, 12, 0, lambda u, h: ps[:, 2 * (u % 2) + h, 0:256])

                if kind == 0:
                    la = l // 3
                    act.wait_ge(gated[0], 12 * (l + 1))

                    def glu(i):
                        act.wait_ge(glu_done, 2 * i + (16 * la + la + 1))
                        for g in range(2):
                            take(l, "pairs", i, g, z_in[:, tok(g)], ACT.Copy)
                        for g in range(2):
                            take(l, "pairs", i, 2 + g, z_gate[:, tok(g)], ACT.Sigmoid)
                    a_.loop(8, [(cols_taken, 4)], glu)
                    for k in range(KD):
                        act.wait_ge(centred, 8 * la + k + 1)
                        if k >= 2:
                            act.wait_ge(lsq_used, 8 * la + k - 1)
                        a_.do(lsq_ready, f(sq[:, k % 2, 0:CONV_OUT], z_out[:, k, :], ACT.Square))
                    act.wait_ge(l_ms, la + 1)
                    a_.do(l_root, f(rstd[:, 0:CONV_OUT], rstd[:, 0:CONV_OUT], ACT.Sqrt))
                    for k in range(KD):
                        act.wait_ge(l_scaled, 8 * la + k + 1)
                        b = k * APAR + TAPS
                        a_.do(l_silu, f(z_out[:, k, :], z_out[:, k, :], ACT.Silu, scale=apar[:, b + 1:b + 2],
                                        bias=apar[:, b + 2:b + 3]))
                elif kind == 2:
                    act.wait_ge(gated[0], 12 * (l + 1))

                    def na(i):
                        for g, cols in ((0, 32), (1, 16)):
                            wait_cols(l, "pairs", i, g)
                            a_.do(cols_taken, f(
                                na_q[:, tok(g)].rearrange("p (i r c) -> p r i c", c=cols, i=64 // cols),
                                ps[:, g, 0:GROUPS[g][1]].rearrange("p (r i c) -> p r i c", c=cols, i=64 // cols),
                                ACT.Copy, scale=HEAD_SCALE))
                        for g in range(2):
                            take(l, "pairs", i, 2 + g, na_k[:, tok(g)], ACT.Copy)
                        take(l, "pairs", i, 4, na_v[:, 4, :], ACT.Copy)
                        wait_cols(l, "pairs", i, 5)
                        for w, start in enumerate(KEY_START):
                            a_.do(v_window if w < 3 else cols_taken, f(
                                na_v[:, w, :].rearrange("p (r c) -> p r c", c=32),
                                ps[:, 1, :].rearrange("p (r c) -> p r c", c=64)[:, :, start:start + 32], ACT.Copy))
                        act.wait_ge(vt_turned, i + 1)
                        flat = na_vt[:, :, :].rearrange("p w c -> p (w c)")
                        for b, w in ((0, 512), (1, 512), (2, 256)):
                            a_.do(vt_taken, f(flat[:, 512 * b:512 * b + w], ps[:, 2 + b, 0:w], ACT.Copy))
                        attention_units(1, i, 0, 6, 6, lambda u, h: scores[:, u % 2, h * 256:(h + 1) * 256])
                    a_.loop(8, [(cols_taken, 6), (v_window, 3), (vt_taken, 3), (ex_done[1], 12), (pt_done[1], 6)], na)
                else:
                    act.wait_ge(w_zero, 2)
                    for g in range(2):
                        take(l, "lora", 0, g, lora[:, 1 + WKV_AT[g]:1 + WKV_AT[g] + GROUPS[g][1]], ACT.Copy)
                    for d in range(2):
                        act.wait_ge(lora_mix, 2 * d + 2)
                        a_.do(lora_act, f(tw[0:64, d, :], tw[0:64, d, :], ACT.Tanh))
                        a_.do(lora_act, f(tw[64:128, d, :], tw[64:128, d, :], ACT.Copy))

                    act.wait_ge(lora_mix, 3)

                    def take_pair(p, c):
                        n, g = c // 2, c % 2
                        take(l, "pairs", p, c, h_p[:, n, 1 + WKV_AT[g]:1 + WKV_AT[g] + GROUPS[g][1]], ACT.Copy)

                    def pair(p, filler):
                        act.wait_ge(par_ready, p + 1)
                        for d in range(2):
                            if d:
                                act.wait_ge(bon_done, p * 2 + 1)
                            for j, (at, w) in enumerate(((0, 257), (257, 512))):
                                act.wait_ge(up_done, p * 8 + 4 * d + 2 * j + 1)
                                a_.go(up_act, f(sg[:, at:at + w], ps[:, 2 + j, 0:w], ACT.Sigmoid,
                                                bias=par_now[:, W0 + d:W0 + d + 1]))
                                act.wait_ge(up_done, p * 8 + 4 * d + 2 * j + 2)
                                a_.go(up_act, f(av[:, d, at:at + w], ps[:, 4 + j, 0:w], ACT.Sigmoid,
                                                bias=par_now[:, A0 + d:A0 + d + 1]))
                            act.wait_ge(less, p * 2 + d + 1)
                            act.wait_ge(kk_raw, p * 2 + d + 1)
                            a_.go(kk_sq, f(tmp[:, :], kk[:, :], ACT.Square))
                            a_.go(decays, f(dd[:, :], cum[:, :], ACT.Exp, scale=-DECAY))
                            a_.go(decays, f(dx[:, d, :], dx[:, d, :], ACT.Exp, scale=-DECAY))
                            a_.do(decays, f(cum[:, :], cum[:, :], ACT.Exp, scale=DECAY))
                            act.wait_ge(kk_max, (p * 2 + d + 1) * 2)
                            a_.do(kk_root, f(tmp[:, :], tmp[:, :], ACT.Sqrt))
                        for qn in range(3):
                            def at(per, n):
                                return p * (3 * per) + (qn * per + n)

                            for d in range(2):
                                first = quad_at(d, qn)

                                def quad(buf):
                                    return buf[:, d, first:first + 256].rearrange("p (c t) -> p c t", c=QUAD)
                                if qn == 0:
                                    act.wait_ge(prepared, p * PREPARED + PREPARED)
                                else:
                                    act.wait_ge(c_y, at(8, -2 + d + 1))
                                for dst, src in ((b_bd, av), (k_bd, ke), (v_bd, xv), (a_bd, dx)):
                                    for h in range(2):
                                        r = slice(64 * h, 64 * h + 64)
                                        a_.go(q_act, f(dst[r, d, :, 64 * h:64 * h + 64], quad(src)[r], ACT.Copy))

                            def turned(n, b, d, dst):
                                act.wait_ge(q_turn, at(6, n))
                                a_.go(q_turned, f(dst[:, d, :, :].rearrange("p c t -> p (c t)"), ps[:, 2 + 3 * d + b, :], ACT.Copy))

                            turned(1, 2, 0, bt)
                            turned(2, 2, 1, bt)
                            for d in range(2):
                                turned(3 + 2 * d, 0, d, kt)
                                turned(4 + 2 * d, 1, d, vt)
                            for d in range(2):
                                act.wait_ge(q_masked, at(4, 2 * d + 2))
                                for h in range(2):
                                    r = slice(64 * h, 64 * h + 64)
                                    a_.go(q_akbd, f(ak_bd[r, d, :, 64 * h:64 * h + 64], ak[r, d, :, 0:C], ACT.Copy))
                            for v in range(1, LEVELS):
                                for d in range(2):
                                    act.wait_ge(i_prod, at(12, 2 * v + d + 1))
                                    a_.go(i_taken, f(prod[:, d, :, :].rearrange("p c t -> p (c t)"), ps[:, 2 + 3 * d, :], ACT.Copy))
                            if filler:
                                take_pair(p + 1, 2 * qn)
                            for m in range(QUAD):
                                for d in range(2):
                                    c = m if d == 0 else QUAD - 1 - m
                                    act.wait_ge(c_r, at(8, 2 * m + d + 1))
                                    a_.go(c_rt, f(rhs[:, d, c, :], ps[:, 2 + 3 * d, 0:P], ACT.Copy))
                                for d in range(2):
                                    c = m if d == 0 else QUAD - 1 - m
                                    act.wait_ge(c_u, at(8, 2 * m + d + 1))
                                    a_.go(c_ut, f(unew[:, d, c, :], ps[:, 2 + 3 * d, P:2 * P], ACT.Copy, scale=-1.0))
                            if filler:
                                take_pair(p + 1, 2 * qn + 1)
                        act.wait_ge(g_centred, p * 2 + 2)
                        a_.do(g_sq, f(tmp[:, :], ysum[:, :], ACT.Square))
                        act.wait_ge(g_eps, p * 2 + 2)
                        a_.do(g_root, f(tmp[:, :], tmp[:, :], ACT.Sqrt))

                    for c in range(6):
                        take_pair(0, c)
                    counts = [(cols_taken, 6), (up_act, 8), (kk_sq, 2), (kk_root, 2), (decays, 6), (q_act, 48),
                              (q_turned, 18), (q_akbd, 12), (i_taken, 30), (c_rt, 24), (c_ut, 24), (g_sq, 1), (g_root, 1)]
                    a_.loop(7, counts, lambda p: pair(p, True))
                    pair(7, False)

                def outs(i):
                    for s in range(2):
                        for g in range(2):
                            take(l, "out", i, 2 * s + g, xn[:, 2 * i + s, tok(g)], ACT.Copy)
                for i in range(4):
                    outs(i)
                squares(3 * l + 2, xn, T)

        @block.gpsimd
        def _(pool):
            g_ = Serial(pool)
            for l in range(layers):
                if KINDS[l] == 2:
                    pool.wait_ge(mask_in, 16)

                    def add_mask(i):
                        pool.wait_ge(bias_in, i * 16 + 16)
                        pool.wait_ge(cols_taken, i * 6 + plan[l, "pairs"][1] + 1)
                        g_.do(bm_ready, nc.gpsimd.tensor_tensor(
                            na_bm[:, :, :, :], na_bias[:, :, :, :],
                            na_mask[:, :, :].unsqueeze(2).to_broadcast([P, 5, 2, 256]), ALU.add))
                    g_.loop(8, [(bm_ready, 1)], add_mask)
                elif KINDS[l] == 1:
                    pool.wait_ge(gated[0], 12 * (l + 1))
                    pool.wait_ge(x_spilled, 16)
                    g_.do(w_zero, nc.gpsimd.memset(h_p[:, :, :], 0.0))
                    for dst in (a_bd, b_bd, k_bd, v_bd, ak_bd, lev):
                        ins = nc.gpsimd.memset(dst[tuple(slice(None) for _ in dst.shape)], 0.0)
                        if dst is lev:
                            g_.do(w_zero, ins)
                        else:
                            ins.then_inc(b_start, 1)
                    pool.wait_ge(b_start, 5)
                    pool.wait_ge(cols_taken, plan[l, "pairs"][1])
                    for d in range(2):
                        g_.do(lora_shift, nc.gpsimd.tensor_tensor(
                            tw[:, d, :], lora[:, 2 * d:2 * d + WT], lora[:, 1:1 + WT], ALU.subtract))

                    def pair(p):
                        for d in range(2):
                            pool.wait_ge(cols_taken, p * 6 + plan[l, "pairs"][1] + 6)
                            if d:
                                pool.wait_ge(bon_done, p * 2 + 1)
                            for n, dst in enumerate((xr[:, d, :], xk[:, :], xv[:, d, :])):
                                g_.do(shifted, nc.gpsimd.tensor_tensor(
                                    dst, h_p[:, n, 2 * d:2 * d + WT], h_p[:, n, 1:1 + WT], ALU.subtract))
                            pool.wait_ge(summed, p * 2 + d + 1)
                            g_.do(less, nc.gpsimd.tensor_tensor(dx[:, d, :], cum[:, :], sg[:, :], ALU.subtract))
                        for qn in range(3):
                            def at(per, n):
                                return p * (3 * per) + (qn * per + n)

                            for v in range(LEVELS):
                                for d in range(2):
                                    if v == 0:
                                        pool.wait_ge(q_masked, at(4, 2 * d + 1))
                                    if v >= 2:
                                        pool.wait_ge(i_prod, at(12, 2 * (v - 2) + d + 1))
                                        pool.wait_ge(i_x, at(22, d + 1))
                                    for h in range(2):
                                        r = slice(64 * h, 64 * h + 64)
                                        g_.do(q_levels, nc.gpsimd.tensor_tensor(
                                            lev[r, d, v % 2, :, 64 * h:64 * h + 64], ab[r, d, :, 0:C],
                                            level[r, d, v, :].unsqueeze(1).to_broadcast([64, QUAD, C]), ALU.mult))
                    g_.loop(8, [(shifted, 6), (less, 2), (q_levels, 72)], pair)

        @block.vector
        def _(dve):
            v_ = Serial(dve)
            ve = nc.vector
            stt = ve.scalar_tensor_tensor

            def norm(q, widths, total, k_op):
                dve.wait_ge(sq_used, 8 * q + 8)
                for j, (at, w) in enumerate(widths):
                    ins = ve.tensor_scalar(rstd[:, at:at + w], ps[:, j, 0:w], 1.0 / D, RMS_EPS, ALU.mult, ALU.add)
                    if j < len(widths) - 1:
                        v_.do(scaled, ins)
                v_.do(ms_taken, ins)
                dve.wait_ge(root, q + 1)
                v_.do(inverse, ve.reciprocal(rstd[:, 0:total], rstd[:, 0:total]))
                for k in range(KD):
                    k_op(k)

            def attention_units(a, i, base, n, per, bias_of, gate):
                def at(c):
                    return base + i * per + c

                def top(u):
                    dve.wait_ge(sc_done[a], at(u + 1))
                    src = ps[:, 2 * (u % 2):2 * (u % 2) + 2, 0:256]
                    if bias_of:
                        out = scores[:, u % 2, :].rearrange("p (h k) -> p h k", h=2)
                        v_.do(sc_biased[a], ve.tensor_tensor(out, src, bias_of(u), ALU.add))
                        src = out
                    v_.do(sc_max[a], ve.tensor_reduce(out=stat[:, u % 2, 0:2], in_=src,
                                                      op=ALU.max, axis=AX_X, negate=True))

                top(0)
                for u in range(n):
                    if u + 1 < n:
                        top(u + 1)
                    dve.wait_ge(ex_done[a], 2 * at(u + 1))
                    v_.do(p_inv[a], ve.reciprocal(stat[:, u % 2, 4:6], stat[:, u % 2, 2:4]))
                    v_.do(p_done[a], ve.tensor_tensor(
                        exps[:, u % 2, :].rearrange("p (h k) -> p h k", h=2),
                        exps[:, u % 2, :].rearrange("p (h k) -> p h k", h=2),
                        stat[:, u % 2, 4:6].unsqueeze(2).to_broadcast([P, 2, 256]), ALU.mult))
                    dve.wait_ge(av_done[a], at(u + 1))
                    gate(u)

            dve.wait_ge(const_in, 32)
            for l in range(layers):
                kind = KINDS[l]

                def scale_by(row, src):
                    def k_op(k):
                        w = MEM if src is xn else T
                        v_.do(normed, stt(xn[:, k, 0:w], src[:, k, 0:w], gain[:, row * KD + k:row * KD + k + 1],
                                          rstd[:, 0:w], ALU.mult, ALU.mult))
                    return k_op

                norm(3 * l, [(0, MEM)], MEM, scale_by(8 + l, xn))
                dve.wait_ge(cols_done, plan[l, "qg"][1])
                norm(3 * l + 1, GROUPS, T, scale_by(l, xT))
                dve.wait_ge(cols_taken, plan[l, "qg"][1] + 24)

                def mem_gate(u):
                    hp, t = u // 6, u % 6
                    dst = br[:, KD + hp, t * P:(t + 1) * P]
                    v_.do(gated[0], ve.tensor_tensor(dst, dst, ps[:, 6 + u % 2, 0:P], ALU.mult))
                attention_units(0, 0, 12 * l, 12, 0, None, mem_gate)

                if kind == 0:
                    la = l // 3
                    dve.wait_ge(apar_in, 16 * (la + 1))
                    v_.do(glu_done, ve.memset(z_pad[:, :], 0.0))

                    def conv_pair(i):
                        dve.wait_ge(cols_taken, i * 4 + plan[l, "pairs"][1] + 4)
                        for g, (first, n) in enumerate(GROUPS):
                            at = HALO + CONV_AT[g]
                            v_.do(glu_done, ve.tensor_tensor(z_pad[:, at:at + n], z_in[:, first:first + n],
                                                             z_gate[:, first:first + n], ALU.mult))
                        dst = z_out[:, bass.ds(i, 1), :].rearrange("p a t -> p (a t)")

                        def w(c):
                            return apar[:, bass.ds(i * APAR + c, 1)]
                        v_.do(conv_done, ve.tensor_scalar(dst, z_pad[:, 0:CONV_OUT], w(0), w(TAPS), ALU.mult, ALU.add))
                        for c in range(1, TAPS):
                            v_.do(conv_done, stt(dst, z_pad[:, c:c + CONV_OUT], w(c), dst, ALU.mult, ALU.add))
                        v_.do(conv_done, ve.memset(stat[:, 0, 0:1], 0.0))
                    v_.loop(8, [(glu_done, 2), (conv_done, TAPS + 1)], conv_pair)
                    half = CONV_OUT // 2
                    dve.wait_ge(mean_done, la + 1)
                    for k in range(KD):
                        v = z_out[:, k, :].rearrange("p (j t) -> p j t", j=2)
                        v_.do(centred, stt(v, ps[:, 2:4, 0:half], -1.0 / D, v, ALU.mult, ALU.add))
                    dve.wait_ge(lsq_used, 8 * (la + 1))
                    v_.do(l_ms, ve.tensor_scalar(rstd[:, 0:CONV_OUT].rearrange("p (j t) -> p j t", j=2), ps[:, 4:6, 0:half],
                                                 1.0 / D, LN_EPS, ALU.mult, ALU.add))
                    dve.wait_ge(l_root, la + 1)
                    v_.do(l_inv, ve.reciprocal(rstd[:, 0:CONV_OUT], rstd[:, 0:CONV_OUT]))
                    for k in range(KD):
                        v_.do(l_scaled, ve.tensor_tensor(z_out[:, k, :], z_out[:, k, :], rstd[:, 0:CONV_OUT], ALU.mult))
                    for k in range(KD):
                        dve.wait_ge(l_silu, 8 * la + k + 1)
                        for g, (first, n) in enumerate(GROUPS):
                            dst = br[:, k, first:first + n]
                            v_.do(l_gated, ve.tensor_tensor(dst, dst, z_out[:, k, CONV_AT[g]:CONV_AT[g] + n], ALU.mult))
                elif kind == 2:
                    def na(i):
                        dve.wait_ge(bm_ready, i + 1)

                        def bias_of(u):
                            kind_of = (0, 1, 1, 2, 3, 4)[u]
                            return na_bm[:, kind_of, :, :]

                        def gate(u):
                            for h in range(2):
                                r = slice(64 * h, 64 * h + 64)
                                row = br[r, bass.ds(i, 1), :].rearrange("p a t -> p (a t)")
                                o = ps[r, 6 + u % 2, 0:P]
                                if u >= 4:
                                    dst = row[:, 0:256].rearrange("p (r c) -> p r c", c=64)[:, :, 32 * (u - 4):32 * (u - 4) + 32]
                                    o = o.rearrange("p (r c) -> p r c", c=32)
                                else:
                                    dst = row[:, 256:T].rearrange("p (r c) -> p r c", c=64)[:, :, 16 * u:16 * u + 16]
                                    o = o.rearrange("p (r c) -> p r c", c=16)
                                v_.do(gated[1], ve.tensor_tensor(dst, dst, o, ALU.mult))
                        attention_units(1, i, 0, 6, 6, bias_of, gate)
                    v_.loop(8, [(sc_biased[1], 6), (sc_max[1], 6), (p_inv[1], 6), (p_done[1], 6), (gated[1], 12)], na)
                else:
                    dve.wait_ge(bpar_in, 64)
                    v_.do(lora_mix, ve.tensor_scalar(
                        one_minus_ka[:, :].unsqueeze(2), bpar[:, 0:8 * BPAR].rearrange("p (k c) -> p k c", c=BPAR)[:, :, KA:KA + 1],
                        -1.0, 1.0, ALU.mult, ALU.add))
                    for d in range(2):
                        dve.wait_ge(lora_shift, d + 1)
                        v_.do(lora_mix, stt(tw[:, d, :], tw[:, d, :], bpar[:, 8 * BPAR + d:8 * BPAR + d + 1],
                                            lora[:, 1:1 + WT], ALU.mult, ALU.add))
                    v_.do(lora_mix, ve.memset(bonus[:, :], 0.0))

                    def par(p, c):
                        return bpar[:, bass.ds(p * BPAR + c, 1)]

                    def pair(p):
                        v_.go(par_ready, ve.tensor_copy(par_now[:, :], bpar[:, bass.ds(p * BPAR, BPAR)]))
                        v_.go(y_zero, ve.memset(ysum[:, :], 0.0))
                        for d in range(2):
                            for n, dst in enumerate((xr[:, d, :], xk[:, :], xv[:, d, :])):
                                dve.wait_ge(shifted, p * 6 + 3 * d + n + 1)
                                v_.do(mixed, stt(dst, dst, par(p, MU + 3 * d + n), h_p[:, n, 1:1 + WT], ALU.mult, ALU.add))
                            v_.go(kk_raw, ve.tensor_scalar(kk[:, :], xk[:, :], par(p, KG), None, ALU.mult))
                            dve.wait_ge(up_act, p * 8 + 4 * d + 4)
                            at_ = slice(None) if d == 0 else slice(None, None, -1)
                            v_.go(summed, ve.tensor_tensor_scan(out=cum[:, at_], data0=reset[:, d, at_], data1=sg[:, at_],
                                                                initial=0.0, op0=ALU.mult, op1=ALU.add))
                            v_.do(prepared, ve.tensor_scalar(ke[:, d, :], av[:, d, :], par(p, KA), one_minus_ka[:, bass.ds(p, 1)],
                                                             ALU.mult, ALU.add))
                            v_.do(prepared, ve.tensor_tensor(ke[:, d, :], ke[:, d, :], xk[:, :], ALU.mult))
                            dve.wait_ge(kk_ss, p * 2 + d + 1)
                            for j, (at_, w) in enumerate(((0, 257), (257, 512))):
                                v_.go(kk_max, ve.tensor_scalar(tmp[:, at_:at_ + w], ps[:, 6 + j, 0:w], 1e-24, None, ALU.max))
                            dve.wait_ge(kk_root, p * 2 + d + 1)
                            v_.do(prepared, ve.reciprocal(tmp[:, :], tmp[:, :]))
                            v_.do(prepared, ve.tensor_tensor(kk[:, :], kk[:, :], tmp[:, :], ALU.mult))
                            v_.go(bon_in, stt(tmp[:, :], xr[:, d, :], par(p, RK), ke[:, d, :], ALU.mult, ALU.mult))
                            dve.wait_ge(decays, p * 6 + 3 * d + 3)
                            v_.go(prepared, ve.tensor_tensor(av[:, d, :], av[:, d, :], cum[:, :], ALU.mult))
                            v_.go(prepared, ve.tensor_tensor(dx[:, d, :], dx[:, d, :], kk[:, :], ALU.mult))
                            v_.go(prepared, ve.tensor_tensor(ke[:, d, :], ke[:, d, :], cum[:, :], ALU.mult))
                            v_.do(prepared, ve.tensor_tensor(xr[:, d, :], xr[:, d, :], dd[:, :], ALU.mult))
                            v_.go(prepared, ve.tensor_tensor(av[:, d, :], av[:, d, :], kk[:, :], ALU.mult))
                            e = C - 1 if d == 0 else 0
                            v_.go(prepared, ve.tensor_copy(dend[:, d, 0:4], dd[:, e:e + 3 * C + 1:C]))
                            v_.go(prepared, ve.tensor_copy(dend[:, d, 4:12], dd[:, 257 + e:257 + e + 7 * C + 1:C]))
                            dve.wait_ge(bon_ps, p * 2 + d + 1)
                            dst = bonus if d == 0 else tmp
                            for j, (at_, w) in enumerate(((0, 257), (257, 512))):
                                v_.do(prepared, ve.tensor_tensor(dst[:, at_:at_ + w], xv[:, d, at_:at_ + w], ps[:, 6 + j, 0:w],
                                                                 ALU.mult))
                            if d == 0:
                                v_.do(bon_done, ve.memset(tmp[:, 0:1], 0.0))
                            else:
                                v_.do(bon_done, ve.tensor_tensor(bonus[:, :], bonus[:, :], tmp[:, :], ALU.add))
                        for qn in range(3):
                            def at(per, n):
                                return p * (3 * per) + (qn * per + n)

                            def quad(buf, d):
                                first = quad_at(d, qn)
                                return buf[:, first:first + 256].rearrange("p (c t) -> p c t", c=QUAD)

                            def four(bank):
                                return ps[:, bank, :].rearrange("p (c t) -> p c t", c=QUAD)

                            for d in range(2):
                                v_.go(q_dve, ve.tensor_copy(ar[:, d, :, 0:C], quad(dx[:, d, :], d)))
                                v_.go(q_dve, ve.tensor_copy(ar[:, d, :, C:P], quad(xr[:, d, :], d)))
                            for d in range(2):
                                for n, dst in enumerate((ab, ak)):
                                    dve.wait_ge(q_pairs, at(4, 2 * d + n + 1))
                                    v_.go(q_masked, ve.tensor_tensor(dst[:, d, :, :], four(2 + 3 * d + n),
                                                                     mask[:, d, :].unsqueeze(1).to_broadcast([P, QUAD, P]),
                                                                     ALU.mult))
                            eye = ident.unsqueeze(1).to_broadcast([P, QUAD, P])
                            for d in range(2):
                                dve.wait_ge(q_levels, at(24, 2 * d + 2))
                                v_.go(i_x, ve.tensor_tensor(inv_t[:, d, :, :], eye, lev[:, d, 0, :, :], ALU.subtract))
                            for d in range(2):
                                dve.wait_ge(i_prod, at(12, d + 1))
                                v_.go(i_x, ve.tensor_tensor(inv[:, d, :, :], eye, four(4 + 3 * d), ALU.subtract))
                            for v in range(1, LEVELS):
                                for d in range(2):
                                    dve.wait_ge(i_next, at(10, 2 * (v - 1) + d + 1))
                                    for b, dst in ((1, inv_t), (2, inv)):
                                        if b == 1 or v < LEVELS - 1:
                                            flat = dst[:, d, :, :].rearrange("p c t -> p (c t)")
                                            v_.go(i_x, ve.tensor_tensor(flat, flat, ps[:, 2 + 3 * d + b, :], ALU.subtract))
                            if qn < 2:
                                for d in range(2):
                                    v_.go(c_st, ve.memset(state[:, d, 0, :], 0.0))
                            for m in range(QUAD):
                                for d in range(2):
                                    c = m if d == 0 else QUAD - 1 - m
                                    dve.wait_ge(c_s, at(8, 2 * m + d + 1))
                                    n = c + {0: 0, 257: 4, 513: 8}[quad_at(d, qn)]
                                    v_.go(c_st, ve.tensor_scalar(state[:, d, (m + 1) % 2, :], ps[:, 2 + 3 * d, 2 * P:3 * P],
                                                                 dend[:, d, n:n + 1], None, ALU.mult))
                            for d in range(2):
                                dve.wait_ge(c_y, at(8, 6 + d + 1))
                                v_.do(c_yt, ve.tensor_tensor(quad(ysum, d), quad(ysum, d), four(3 + 3 * d)[:, :, C:P], ALU.add))
                        dve.wait_ge(g_mean, p + 1)
                        for j, (at_, w) in enumerate(((0, 257), (257, 512))):
                            v_.go(g_centred, stt(ysum[:, at_:at_ + w], ps[:, 2 + j, 0:w], -1.0 / 64, ysum[:, at_:at_ + w],
                                                 ALU.mult, ALU.add))
                        dve.wait_ge(g_var, p + 1)
                        for j, (at_, w) in enumerate(((0, 257), (257, 512))):
                            v_.go(g_eps, ve.tensor_scalar(tmp[:, at_:at_ + w], ps[:, 4 + j, 0:w], 1.0 / 64, GN_EPS,
                                                          ALU.mult, ALU.add))
                        dve.wait_ge(g_root, p + 1)
                        v_.do(g_done, ve.reciprocal(tmp[:, :], tmp[:, :]))
                        v_.do(g_done, stt(ysum[:, :], ysum[:, :], par(p, LNG), tmp[:, :], ALU.mult, ALU.mult))
                        v_.do(g_done, stt(ysum[:, :], ysum[:, :], par(p, LNB), bonus[:, :], ALU.add, ALU.add))
                        for g, (first, n) in enumerate(GROUPS):
                            dst = br[:, bass.ds(p, 1), first:first + n].rearrange("p a t -> p (a t)")
                            v_.do(g_done, ve.tensor_tensor(dst, dst, ysum[:, WKV_AT[g]:WKV_AT[g] + n], ALU.mult))
                    v_.loop(8, [(par_ready, 1), (y_zero, 1), (mixed, 6), (summed, 2), (kk_raw, 2), (kk_max, 4),
                                (prepared, PREPARED), (bon_in, 2), (bon_done, 2), (q_dve, 12), (q_masked, 12), (i_x, 66),
                                (c_st, 28), (c_yt, 6), (g_centred, 2), (g_eps, 2), (g_done, 5)], pair)
                    dve.wait_ge(x_back, 16)

                def residual(k):
                    v_.do(scaled, stt(xn[:, k, :], xn[:, k, :], gain[:, (4 + l) * KD + k:(4 + l) * KD + k + 1], rstd[:, 0:T],
                                      ALU.mult, ALU.mult))
                    v_.do(normed, ve.tensor_tensor(xT[:, k, :], xT[:, k, :], xn[:, k, :], ALU.add))
                norm(3 * l + 2, GROUPS, T, residual)


def _tiles(w):
    k, n = w.shape
    return np.ascontiguousarray(w.reshape(k // P, P, n // P, P).transpose(2, 1, 0, 3).reshape(n // P, P, k))


def _features(v):
    return np.ascontiguousarray(v.reshape(-1, KD, P).transpose(2, 0, 1).reshape(P, -1))


def _acts(a, b):
    both = np.concatenate([a[0], b[0]], 0)
    return np.ascontiguousarray(both.T.reshape(KD, P, -1).transpose(1, 0, 2))


def _pairs(w, skip, names):
    t = _tiles(w)
    body = 8 * names
    rest = t[body + skip:]
    mixer = [t[n * 8 + p] for p in range(8) for n in range(names)]
    return np.ascontiguousarray(np.concatenate([rest, t[body:body + skip], np.stack(mixer)], 0))


def _constants():
    square = np.zeros((P, 3, P), np.float32)
    square[:, 0] = np.eye(P)
    square[:, 1] = 1
    square[:64, 2, :64] = 1
    square[64:, 2, 64:] = 1
    reset = np.ones((P, 2, WT), np.float32)
    for g, at in enumerate(WKV_AT):
        for c in range(GROUPS[g][1] // C):
            reset[:, 0, at + c * C] = 0
            reset[:, 1, at + c * C + C - 1] = 0
    reset[:, :, 256] = 0
    j, t = np.arange(C)[:, None], np.arange(C)[None, :]
    mask = np.zeros((P, 2, P), np.float32)
    level = np.zeros((P, 2, LEVELS, C), np.float32)
    for d in range(2):
        a, b = (j, t) if d == 0 else (t, j)
        m = np.concatenate([a < b, a <= b], 1)
        mask[:, d] = np.concatenate([m, m], 0)
        for v in range(LEVELS):
            s = 1 << v
            m = (a // (2 * s) == b // (2 * s)) & ((a // s) % 2 == 0) & ((b // s) % 2 == 1)
            level[:, d, v] = np.concatenate([m, m], 0)
    return square, reset, mask, level


def _windows():
    out = []
    for cols, keys in ((range(0, 16), range(0, 32)), (range(16, 32), range(8, 40)), (range(48, 64), range(32, 64))):
        out.append((np.array([(r, c) for r in range(8) for c in cols]), np.array([(r, c) for r in range(8) for c in keys])))
    for i in range(2):
        out.append((np.array([(r, c) for r in range(4) for c in range(32 * i, 32 * i + 32)]),
                    np.array([(r, c) for r in range(4) for c in range(64)])))
    return out


def _bias(rpb):
    bias = np.zeros((8, P, 5, 2, 256), np.float32)
    mask = np.zeros((P, 5, 256), np.float32)
    for n, (q, k) in enumerate(_windows()):
        dr = k[None, :, 0] - q[:, None, 0] + 7
        dc = np.clip(k[None, :, 1] - q[:, None, 1], -15, 15) + 15
        bias[:, :, n] = rpb.reshape(8, 2, 15, 31)[:, :, dr, dc].transpose(0, 2, 1, 3)
        start = np.clip(q[:, 1] - 8, 0, 48)[:, None]
        mask[:, n] = np.where((k[None, :, 1] >= start) & (k[None, :, 1] < start + 16), 0.0, NEG)
    return bias.reshape(8, P, -1), mask


def _inputs(i):
    a = {k: np.asarray(v) for k, v in i.items()}
    out = {"x": _acts(a["x_prompt"], a["x_sample"]), "mem": _acts(a["mem_prompt"], a["mem_sample"])}
    out["w_mem"] = np.concatenate([_tiles(w) for w in a["w_mem_kv"]], 0)
    out["w_a"] = np.concatenate([_pairs(w, 0, 2) for w in a["a_w_in"]], 0)
    out["w_b"] = _pairs(a["b_w_in"][0], 1, 3)
    out["w_c"] = _pairs(a["c_w_in"][0], 0, 3)
    out["w_out"] = np.concatenate([_tiles(w) for w in (a["a_w_out"][0], a["b_w_out"][0], a["c_w_out"][0], a["a_w_out"][1])], 0)
    out["gains"] = np.concatenate([_features(a[n]) for n in ("pre_norm", "post_norm", "mem_norm")], 1)
    par = []
    for j in range(2):
        rows = np.concatenate([a["a_conv_w"][j], a["a_conv_b"][j:j + 1], a["a_ln_g"][j:j + 1], a["a_ln_b"][j:j + 1]], 0)
        par.append(rows.reshape(APAR, KD, P).transpose(2, 1, 0).reshape(P, -1))
    out["a_par"] = np.stack(par)
    mu = a["b_mu"][0]
    rows = [mu[d, n * D:(n + 1) * D] for d in range(2) for n in range(3)]
    rows += [a["b_w0"][0, 0], a["b_w0"][0, 1], a["b_a0"][0, 0], a["b_a0"][0, 1], a["b_k_k"][0], a["b_k_a"][0],
             a["b_r_k"][0].reshape(-1), a["b_ln_g"][0], a["b_ln_b"][0]]
    rows = np.stack(rows).reshape(BPAR, KD, P).transpose(2, 1, 0).reshape(P, -1)
    out["b_par"] = np.concatenate([rows, mu[:, 3 * D:].T], 1)
    up = np.concatenate([a["b_w_up"][0], a["b_a_up"][0]], 1)
    out["lora_up"] = up.reshape(2, P, 8, P).transpose(2, 1, 0, 3)
    square, reset, mask, level = _constants()
    out["bias"], window = _bias(a["c_rpb"][0])
    out["square_c"], out["scan_c"], out["level_c"], out["window_c0"], out["window_c1"] = square, reset, level, window, mask
    return {k: np.ascontiguousarray(v) for k, v in out.items()}


def _declare(nc, arrays, layers=4):
    ap = {n: nc.dram_tensor(f"in_{n}", v.shape, mybir.dt.from_np(v.dtype), kind="ExternalInput").ap()
          for n, v in arrays.items()}
    y = nc.dram_tensor("out_y", (P, KD, T), F32, kind="ExternalOutput").ap()
    trunk_kernel(nc, ap["x"], ap["mem"], ap["w_mem"], ap["w_a"], ap["w_b"], ap["w_c"], ap["w_out"], ap["gains"], ap["a_par"],
                 ap["b_par"], ap["lora_up"], ap["bias"], ap["square_c"], ap["scan_c"], ap["level_c"],
                 (ap["window_c0"], ap["window_c1"]), y, layers)


def _outputs(y):
    out = y.transpose(1, 0, 2).reshape(D, T).T
    return np.ascontiguousarray(out[None, 0:256]), np.ascontiguousarray(out[None, 256:T])


def kernel(**inputs):
    import concourse.bacc as bacc
    from concourse.bass_utils import run_bass_kernel_spmd as run

    arrays = _inputs(inputs)
    nc = bacc.Bacc("TRN2", target_bir_lowering=False, num_devices=1)
    _declare(nc, arrays)
    r = run(nc, [{f"in_{k}": v for k, v in arrays.items()}], core_ids=[0])
    return _outputs(r.results[0]["out_y"])
```

```python
import math
from contextlib import ExitStack

import concourse.bass as bass
import numpy as np
from concourse import mybir

F32 = mybir.dt.float32
ACT = mybir.ActivationFunctionType
ALU = mybir.AluOpType
AX_X = mybir.AxisListType.X

P = 128
D = 1024
KD = D // P
GROUPS = ((0, 256), (256, 512))
T = 768
MEM = 512
KB = (D + 256) // P
KINDS = (0, 1, 2, 0)
TAPS = 31
HALO = TAPS // 2
PE_TAPS = 5
CONV_IN = T + 4 * HALO
CONV_OUT = CONV_IN - 2 * HALO
CONV_AT = (0, 256 + 2 * HALO)
RMS_EPS, LN_EPS, GN_EPS = 1e-6, 1e-5, 64e-5
DECAY = math.exp(-0.5)
HEAD_SCALE = 64 ** -0.5
C = 64
QUAD = 4
WT = T + 1
WKV_AT = (0, 257)
LEVELS = 6
BPAR = 15
MU, W0, A0, KG, KA, RK, LNG, LNB = 0, 6, 8, 10, 11, 12, 13, 14
APAR = TAPS + 3
NEG = -1e30
def share(total, parts):
    return [total * (n + 1) // parts - total * n // parts for n in range(parts)]


PROJECTION_GAPS = share(3 * KD, 16)
PREPARE_GAPS = [1, 1, 0] + [0, 0, 1, 1, 0] + [1, 0, 1, 0, 0, 0, 0, 0]
PREPARED = 24
KEY_START = (0, 8, 24, 32)

PAIR_TILES = {0: 2, 1: 3, 2: 3}


def phases(kind):
    mixer = ("pairs", 8, PAIR_TILES[kind])
    gates = ("gates", 4, 2)
    middle = {0: [mixer, gates], 1: [gates, ("lora", 1, 1), mixer], 2: [gates, mixer]}[kind]
    return [("mem", 2, 2), ("q", 2, 2)] + middle + [("out", 4, 2)]


GATE_STEPS = 8 * 2 * KD
GATES_AHEAD = {0: 64, 1: 0, 2: 0}
GATE_GAPS = {k: share(GATE_STEPS - n, 24) for k, n in GATES_AHEAD.items()}
NA_GAPS = share(6 * KD, 12)


def schedule():
    used, free, chunks, plan = [0, 0, 0], [0, 0, 0], 0, {}
    for l, kind in enumerate(KINDS):
        for name, n, tiles in phases(kind):
            per = tiles if name == "mem" else 2 * tiles
            plan[l, name] = (list(used), chunks, n, tiles, per, list(free))
            for s in range(tiles):
                used[s] += n
                free[s] = chunks + (n - 1) * per + (s + 1) * per // tiles
            chunks += n * per
    return plan


class Serial:

    def __init__(self, eng):
        self.eng, self.count, self.step, self.i = eng, {}, {}, 0

    def go(self, sem, ins):
        ins.then_inc(sem, 1)
        self.count[sem.name] = self.count.get(sem.name, 0) + 1

    def do(self, sem, ins):
        self.go(sem, ins)
        self.settle(sem)

    def settle(self, sem):
        n, k = self.count[sem.name], self.step.get(sem.name)
        self.eng.wait_ge(sem, n if k is None else self.i * k + n)

    def loop(self, n, steps, body):
        before = dict(self.count)
        self.step = {s.name: k for s, k in steps}
        with self.eng.Fori(0, n) as i:
            self.i = i
            body(i)
        for s, k in steps:
            assert self.count.get(s.name, 0) - before.get(s.name, 0) == k, (s.name, k, self.count.get(s.name, 0) - before.get(s.name, 0))
            self.count[s.name] = before.get(s.name, 0) + n * k
        changed = {s for s in self.count if self.count[s] != before.get(s, 0)} - set(self.step)
        assert not changed, changed
        self.step, self.i = {}, 0


def trunk_kernel(nc, x, mem, w_mem, w_a, w_b, w_c, w_out, gains, a_par, b_par, lora_up, bias,
                 square_c, scan_c, level_c, window_c, y, layers=4):
    plan = schedule()
    ctx = ExitStack()
    with ctx:
        def sem(name):
            return ctx.enter_context(nc.semaphore(name))

        def sb(name, *shape, stack=ctx):
            return stack.enter_context(nc.sbuf_tensor(name, [P, *shape], F32))

        ps = ctx.enter_context(nc.psum_tensor("ps", [P, 8, 512], F32))
        xn = sb("xn", KD, T)
        ring = sb("ring", 3, KB * P)
        br = sb("br", KB, T)
        gain = sb("gain", 12 * KD)
        square = sb("square", 3, P)
        ident, ones, bones = square[:, 0, :], square[:, 1, :], square[:, 2, :]

        region = ExitStack()
        xT = sb("xT", KD, T, stack=region)
        sq = sb("sq", 2, 800, stack=region)
        rstd = sb("rstd", 800, stack=region)
        mk = sb("mk", 2, MEM, stack=region)
        mvf = sb("mvf", 2, MEM, stack=region)
        mv = sb("mv", 4, 256, stack=region)
        mq = sb("mq", 2, T, stack=region)
        memn = sb("memn", KD, MEM, stack=region)
        attention = ExitStack()
        exps = sb("exps", 2, 512, stack=attention)
        probs_t = sb("probs_t", 512, stack=attention)
        stat = sb("stat", 2, 8, stack=attention)
        scores = sb("scores", 2, 512, stack=attention)
        conv = ExitStack()
        z_in = sb("z_in", T, stack=conv)
        z_gate = sb("z_gate", T, stack=conv)
        z_pad = sb("z_pad", CONV_IN, stack=conv)
        z_out = sb("z_out", KD, CONV_OUT, stack=conv)
        z_odd = sb("z_odd", CONV_OUT, stack=conv)
        diag = sb("diag", PE_TAPS, P, stack=conv)
        apar = sb("apar", 8 * APAR, stack=conv)
        conv.close()
        na = ExitStack()
        na_q = sb("na_q", 2, T, stack=na)
        na_k = sb("na_k", 2, T, stack=na)
        na_v = sb("na_v", 2, 5, 256, stack=na)
        na_vt = sb("na_vt", 10, P, stack=na)
        na_bias = sb("na_bias", 5, 2, 256, stack=na)
        na_bm = sb("na_bm", 5, 2, 256, stack=na)
        na_mask = sb("na_mask", 5, 256, stack=na)
        na.close()
        attention.close()
        region.close()
        wkv = ExitStack()
        tw = sb("tw", 2, WT, stack=wkv)
        bpar = sb("bpar", 8 * BPAR + 2, stack=wkv)
        one_minus_ka = sb("one_minus_ka", 8, stack=wkv)
        par_now = sb("par_now", BPAR, stack=wkv)
        up = sb("up", 2, P, stack=wkv)
        reset = sb("reset", WT + 1, stack=wkv)
        mask = sb("mask", 2, P, stack=wkv)
        level = sb("level", 2, LEVELS, C, stack=wkv)
        h_p = sb("h_p", 3, WT + 2, stack=wkv)
        lora = h_p[:, 0, :]
        xr = sb("xr", 2, WT, stack=wkv)
        xv = sb("xv", 2, WT, stack=wkv)
        av = sb("av", 2, WT, stack=wkv)
        ke = sb("ke", 2, WT, stack=wkv)
        dx = sb("dx", 2, WT, stack=wkv)
        dend = sb("dend", 2, 12, stack=wkv)
        dend_now = sb("dend_now", 2, 12, stack=wkv)
        bonus_now = sb("bonus_now", WT, stack=wkv)
        xk = sb("xk", WT, stack=wkv)
        sg = sb("sg", WT, stack=wkv)
        tmp = sg
        cum = sb("cum", WT, stack=wkv)
        dd = sb("dd", WT, stack=wkv)
        kk = sb("kk", WT, stack=wkv)
        ysum = sb("ysum", WT, stack=wkv)
        bonus = sb("bonus", WT, stack=wkv)
        ar = sb("ar", 2, QUAD, P, stack=wkv)
        a_bd = sb("a_bd", 2, QUAD, P, stack=wkv)
        b_bd = sb("b_bd", 2, QUAD, P, stack=wkv)
        k_bd = sb("k_bd", 2, QUAD, P, stack=wkv)
        v_bd = sb("v_bd", 2, QUAD, P, stack=wkv)
        ab = sb("ab", 2, QUAD, P, stack=wkv)
        ak = sb("ak", 2, QUAD, P, stack=wkv)
        ak_bd = sb("ak_bd", 2, QUAD, P, stack=wkv)
        bt = sb("bt", 2, QUAD, P, stack=wkv)
        kt = sb("kt", 2, QUAD, P, stack=wkv)
        vt = sb("vt", 2, QUAD, P, stack=wkv)
        inv_t = sb("inv_t", 2, QUAD, P, stack=wkv)
        lev = sb("lev", 2, 2, QUAD, P, stack=wkv)
        inv, prod, unew = b_bd, v_bd, k_bd
        rhs = prod
        state = sb("state", 2, 2, P, stack=wkv)
        gn = ar[:, :, :, :].rearrange("p d c t -> p (d c t)")[:, 0:WT]
        ends = ring[:, :, KD * P:KB * P]
        halves = ((0, 256, ends[:, 0, :]), (257, 512, ends[:, 1:3, :]))
        wkv.close()

        spill = nc.dram_tensor("spill", (P, KD, T), F32, kind="Internal").ap()
        const_in, x_in, y_out = sem("const_in"), sem("x_in"), sem("y_out")
        x_spilled, x_back = sem("x_spilled"), sem("x_back")
        mem_in, apar_in, bpar_in, up_in, bias_in, mask_in = (sem(n) for n in
            ("mem_in", "apar_in", "bpar_in", "up_in", "bias_in", "mask_in"))
        ring_in = [sem(f"ring_in{s}") for s in range(3)]
        cols_done, cols_taken = sem("cols_done"), sem("cols_taken")
        sq_ready, sq_used, ms_taken, root, inverse, scaled = (sem(n) for n in
            ("sq_ready", "sq_used", "ms_taken", "root", "inverse", "scaled"))
        normed = sem("normed")
        mv_turned, mv_taken = sem("mv_turned"), sem("mv_taken")
        sc_done, sc_biased, sc_max, ex_done, p_inv, p_done, tp_done, pt_done, av_done, gated = (
            [sem(f"{n}{a}") for a in range(2)] for n in
            ("sc_done", "sc_biased", "sc_max", "ex_done", "p_inv", "p_done", "tp_done", "pt_done", "av_done", "gated"))
        bm_ready, v_window, vt_turned, vt_taken = (sem(n) for n in ("bm_ready", "v_window", "vt_turned", "vt_taken"))
        glu_done, conv_done, diag_done, conv_ps = sem("glu_done"), sem("conv_done"), sem("diag_done"), sem("conv_ps")
        conv_taps = [sem("conv_even"), sem("conv_odd")]
        mean_done, centred, lsq_ready, lsq_used, l_ms, l_root, l_inv, l_scaled, l_silu, l_gated = (sem(n) for n in
            ("mean_done", "centred", "lsq_ready", "lsq_used", "l_ms", "l_root", "l_inv", "l_scaled", "l_silu", "l_gated"))
        w_zero, lora_mix, lora_shift, lora_act = sem("w_zero"), sem("lora_mix"), sem("lora_shift"), sem("lora_act")
        shifted, mixed, up_done, up_act, summed, less, decays = (sem(n) for n in
            ("shifted", "mixed", "up_done", "up_act", "summed", "less", "decays"))
        kk_raw, kk_sq, kk_ss, kk_max, kk_root, kk_done, prepared, bon_in, bon_ps, bon_done = (sem(n) for n in
            ("kk_raw", "kk_sq", "kk_ss", "kk_max", "kk_root", "kk_done", "prepared", "bon_in", "bon_ps", "bon_done"))
        q_dve, q_act, q_pairs, q_turn, q_masked, q_turned, q_akbd, q_levels = (sem(n) for n in
            ("q_dve", "q_act", "q_pairs", "q_turn", "q_masked", "q_turned", "q_akbd", "q_levels"))
        i_prod, i_taken, i_next, i_x = sem("i_prod"), sem("i_taken"), sem("i_next"), sem("i_x")
        c_r, c_rt, c_u, c_ut, c_s, c_st, c_y, c_yt = (sem(n) for n in
            ("c_r", "c_rt", "c_u", "c_ut", "c_s", "c_st", "c_y", "c_yt"))
        g_mean, g_centred, g_sq, g_var, g_eps, g_root, g_done = (sem(n) for n in
            ("g_mean", "g_centred", "g_sq", "g_var", "g_eps", "g_root", "g_done"))
        b_start, par_ready, y_zero = sem("b_start"), sem("par_ready"), sem("y_zero")
        block = ctx.enter_context(nc.Block())

        def score_bank(u):
            return 2 if u % 2 == 0 else 6

        def mem_norm(l):
            return 3 * l - 1 if l else 0

        def in_norm(l):
            return 3 * l + 1

        def out_norm(l):
            return 3 * l + 3 if l < layers - 1 else 3 * l + 2

        def tok(g, at=(0, 256)):
            return slice(at[g], at[g] + GROUPS[g][1])

        A_LAYERS = [l for l in range(layers) if KINDS[l] == 0]

        def quad_at(d, qn):
            return (0, WKV_AT[1], WKV_AT[1] + 256)[qn] if d == 0 else (0, WKV_AT[1] + 256, WKV_AT[1])[qn]

        @block.sync
        def _(sp):
            sp.dma_start(square[:, :, :], square_c).then_inc(const_in, 16)
            sp.dma_start(gain[:, :], gains).then_inc(const_in, 16)
            for l in range(layers):
                kind = KINDS[l]
                weights = {"mem": (w_mem, 4 * l), "out": (w_out, 8 * l)}
                body = {0: (w_a, 28 * (l // 3)), 1: (w_b, 0), 2: (w_c, 0)}[kind]
                weights["q"] = body
                weights["gates"] = (body[0], body[1] + 4)
                weights["lora"] = (body[0], 12)
                weights["pairs"] = (body[0], body[1] + (13 if kind == 1 else 12))
                if l == 0:
                    sp.dma_start(memn[:, :, :], mem).then_inc(mem_in, 16)
                    sp.dma_start(xT[:, :, :], x).then_inc(x_in, 16)
                for name, n, tiles in phases(kind):
                    used, chunks, n, tiles, per, free = plan[l, name]
                    src, first = weights[name]
                    width = (KB if name == "out" else KD) * P
                    if name == "pairs" and kind == 0:
                        sp.wait_ge(normed, 8 * (in_norm(l) if l else 0))
                        sp.dma_start(apar[:, :], a_par[l // 3]).then_inc(apar_in, 16)
                    if name == "lora":
                        sp.wait_ge(normed, 8 * in_norm(l) + 8)
                        sp.dma_start(spill, xT[:, :, :]).then_inc(x_spilled, 16)
                        sp.wait_ge(gated[0], 12 * (l + 1))
                        sp.wait_ge(x_spilled, 16)
                        for dst, s in ((bpar[:, :], b_par), (reset[:, :], scan_c), (mask[:, :, :], window_c[1]),
                                       (level[:, :, :, :], level_c)):
                            sp.dma_start(dst, s).then_inc(bpar_in, 16)
                    if name == "pairs" and kind == 2:
                        sp.wait_ge(normed, 8 * in_norm(l))
                        sp.dma_start(na_mask[:, :, :], window_c[0]).then_inc(mask_in, 16)

                    def load(i, first_free=False):
                        for s in range(tiles):
                            before = chunks - per + (s + 1) * per // tiles
                            sp.wait_ge(cols_done, free[s] if first_free else i * per + before)
                            sp.dma_start(ring[:, s, 0:width],
                                         src[bass.ds(first + i * tiles + s, 1), :, :].rearrange("a p c -> (a p) c"))\
                              .then_inc(ring_in[s], 16)
                        if name == "pairs" and kind == 1:
                            sp.wait_ge(up_done, 8 * i)
                            sp.dma_start(up[:, :, :], lora_up[bass.ds(i, 1), :, :, :].rearrange("a p d c -> (a p) d c"))\
                              .then_inc(up_in, 16)
                        if name == "pairs" and kind == 2:
                            sp.wait_ge(bm_ready, i)
                            sp.dma_start(na_bias[:, :, :, :].rearrange("p a h k -> p (a h k)"),
                                         bias[bass.ds(i, 1), :, :].rearrange("a p k -> (a p) k")).then_inc(bias_in, 16)

                    if name == "out" and l + 1 < layers:
                        sp.wait_ge(cols_done, plan[l, "q"][1])
                        if kind == 1:
                            sp.wait_ge(g_done, 40)
                        sp.dma_start(memn[:, :, :], mem).then_inc(mem_in, 16)
                    if name == "out" and kind == 1:
                        sp.wait_ge(bon_done, 16)
                    load(0, True)
                    if name == "out" and kind == 1:
                        sp.wait_ge(g_done, 40)
                        sp.dma_start(xT[:, :, :], spill).then_inc(x_back, 16)
                    if n > 1:
                        with sp.Fori(1, n) as i:
                            load(i)
            sp.wait_ge(normed, 8 * out_norm(layers - 1) + 8)
            sp.dma_start(y, xT[:, :, :]).then_inc(y_out, 16)
            sp.wait_ge(y_out, 16)

        @block.tensor
        def _(pe):
            mm = nc.tensor.matmul

            def project(l, name, i, s, c, src, token_chunks, kd=KD):
                used, chunks, n, tiles, per, _ = plan[l, name]
                pe.wait_ge(ring_in[s], (i + used[s] + 1) * 16)
                for j, (at, w) in enumerate(token_chunks):
                    if l or name != "mem" or i:
                        pe.wait_ge(cols_taken, i * per + chunks + c + j - 1)
                    for k in range(kd):
                        ins = mm(ps[:, (c + j) % 2, 0:w], ring[:, s, k * P:(k + 1) * P], src[:, k, at:at + w],
                                 start=k == 0, stop=k == kd - 1)
                    ins.then_inc(cols_done, 1)

            def project_steps(l, name, iterations, tiles):
                used, chunks, n, _, per, _ = plan[l, name]
                for i in iterations:
                    for s in range(tiles):
                        for j, (at, w) in enumerate(GROUPS):
                            for k in range(KD):
                                if k == 0:
                                    if j == 0:
                                        pe.wait_ge(ring_in[s], i * 16 + (used[s] + 1) * 16)
                                    pe.wait_ge(cols_taken, i * per + (chunks + 2 * s + j - 1))
                                ins = mm(ps[:, j, 0:w], ring[:, s, k * P:(k + 1) * P], xn[:, k, at:at + w],
                                         start=k == 0, stop=k == KD - 1)
                                if k == KD - 1:
                                    ins.then_inc(cols_done, 1)
                                yield

            def sum_squares(q, widths):
                if q:
                    pe.wait_ge(ms_taken, q)
                for k in range(KD):
                    pe.wait_ge(sq_ready, 8 * q + k + 1)
                    for j, (at, w) in enumerate(widths):
                        ins = mm(ps[:, 6 + j, 0:w], ones, sq[:, k % 2, at:at + w], start=k == 0, stop=k == KD - 1)
                    ins.then_inc(sq_used, 1)

            def memory(l):
                pe.wait_ge(normed, 8 * mem_norm(l) + 8)
                for i in range(2):
                    for s in range(2):
                        project(l, "mem", i, s, s, memn, [(0, MEM)])
                pe.wait_ge(cols_taken, plan[l, "q"][1])
                for m in range(4):
                    for c in range(2):
                        ins = nc.tensor.transpose(ps[:, 2 + m // 2, (m % 2) * 256 + c * P:(m % 2) * 256 + (c + 1) * P],
                                                  mvf[:, c, m * P:(m + 1) * P], ident)
                ins.then_inc(mv_turned, 1)

            def attention_units(a, first, n, s_mm, v_of, fill, gaps):
                def score(u):
                    if u >= 2:
                        pe.wait_ge(ex_done[a], (first + (u - 1)) * 2)
                    s_mm(u).then_inc(sc_done[a], 1)

                score(0)
                for u in range(n):
                    if u + 1 < n:
                        score(u + 1)
                    fill(gaps[2 * u])
                    pe.wait_ge(p_done[a], first + (u + 1))
                    for h in range(2):
                        for c in range(2):
                            ins = nc.tensor.transpose(ps[:, 4, (2 * h + c) * P:(2 * h + c + 1) * P],
                                                      exps[:, u % 2, h * 256 + c * P:h * 256 + (c + 1) * P], ident)
                    ins.then_inc(tp_done[a], 1)
                    fill(gaps[2 * u + 1])
                    pe.wait_ge(pt_done[a], first + (u + 1))
                    if u >= 1:
                        pe.wait_ge(gated[a], (first + u) * (2 if a else 1))
                    for h in range(2):
                        for c in range(2):
                            ins = mm(ps[64 * h:64 * h + 64, 5, 0:P], v_of(u, h, c),
                                     probs_t[:, (2 * h + c) * P:(2 * h + c + 1) * P], start=c == 0, stop=c == 1)
                    ins.then_inc(av_done[a], 1)

            def filler(steps):
                def fill(n):
                    for _ in range(n):
                        next(steps, None)
                return fill

            pe.wait_ge(const_in, 32)
            sum_squares(mem_norm(0), [(0, MEM)])
            sum_squares(in_norm(0), GROUPS)
            memory(0)
            for l in range(layers):
                kind = KINDS[l]
                pe.wait_ge(normed, 8 * in_norm(l) + 8)
                for i in range(2):
                    for s in range(2):
                        project(l, "q", i, s, 2 * s, xn, GROUPS)
                if kind == 0:
                    la = l // 3

                    def taps(i):
                        pe.wait_ge(glu_done, 2 * i + (17 * la + 3))
                        pe.wait_ge(diag_done, i * PE_TAPS + (8 * la + 1) * PE_TAPS)
                        for n in range(PE_TAPS):
                            for j in range(2):
                                at = TAPS - PE_TAPS + n + j * CONV_OUT // 2
                                ins = mm(ps[:, 2 + j, 0:CONV_OUT // 2], diag[:, n, :], z_pad[:, at:at + CONV_OUT // 2],
                                         start=n == 0, stop=n == PE_TAPS - 1)
                        ins.then_inc(conv_ps, 1)
                    for s in range(2):
                        project(l, "pairs", 0, s, 2 * s, xn, GROUPS)
                    with pe.Fori(0, 7) as i:
                        for s in range(2):
                            project(l, "pairs", i + 1, s, 2 * s, xn, GROUPS)
                        taps(i)
                    taps(7)
                fill = filler(project_steps(l, "gates", range(4), 2))
                fill(GATES_AHEAD[kind])
                if kind == 0:
                    pe.wait_ge(conv_done, 8 * (l // 3 + 1))
                pe.wait_ge(cols_taken, plan[l, "q"][1] + 8)
                pe.wait_ge(mv_taken, l + 1)

                def mem_scores(u):
                    hp, t = u // 6, u % 6
                    g = int(t >= 2)
                    for h in range(2):
                        r = slice(64 * h, 64 * h + 64)
                        ins = mm(ps[:, score_bank(u) + h, 0:256], mq[r, hp, t * P:(t + 1) * P],
                                 mk[r, hp, g * 256:(g + 1) * 256], start=True, stop=True)
                    return ins

                def mem_v(u, h, c):
                    hp, t = u // 6, u % 6
                    return mv[:, 2 * int(t >= 2) + c, (2 * hp + h) * 64:(2 * hp + h + 1) * 64]

                attention_units(0, 12 * l, 12, mem_scores, mem_v, fill, GATE_GAPS[kind])
                pe.wait_ge(gated[0], 12 * (l + 1))

                if kind == 0:
                    la = l // 3
                    half = CONV_OUT // 2
                    for k in range(KD):
                        for j in range(2):
                            ins = mm(ps[:, 2 + j, 0:half], ones, z_out[:, k, j * half:(j + 1) * half],
                                     start=k == 0, stop=k == KD - 1)
                    ins.then_inc(mean_done, 1)
                    for k in range(KD):
                        pe.wait_ge(lsq_ready, 8 * la + k + 1)
                        for j in range(2):
                            ins = mm(ps[:, 4 + j, 0:half], ones, sq[:, k % 2, j * half:(j + 1) * half],
                                     start=k == 0, stop=k == KD - 1)
                        ins.then_inc(lsq_used, 1)
                    pe.wait_ge(l_gated, 16 * (la + 1))
                elif kind == 2:
                    def pair(i, par, more):
                        pe.wait_ge(cols_taken, i * 6 + (plan[l, "pairs"][1] + 6))
                        for n in range(10):
                            ins = nc.tensor.transpose(ps[:, 2 + n // 4, (n % 4) * P:(n % 4 + 1) * P],
                                                      na_v[:, par, n // 2, (n % 2) * P:(n % 2 + 1) * P], ident)
                        ins.then_inc(vt_turned, 1)
                        pe.wait_ge(vt_taken, i * 3 + 3)

                        def keys(r, u):
                            if u >= 4:
                                return na_k[r, par, 0:256]
                            return na_k[r, par, 256:T].rearrange("p (r c) -> p r c", c=64)[:, :, KEY_START[u]:KEY_START[u] + 32]

                        def na_scores(u):
                            at = 256 + u * P if u < 4 else (u - 4) * P
                            for h in range(2):
                                r = slice(64 * h, 64 * h + 64)
                                ins = mm(ps[:, score_bank(u) + h, 0:256], na_q[r, par, at:at + P], keys(r, u),
                                         start=True, stop=True)
                            return ins

                        def na_values(u, h, c):
                            return na_vt[:, 2 * min(u, 4) + c, h * 64:(h + 1) * 64]

                        steps = project_steps(l, "pairs", [i + 1], 3) if more else iter(())
                        attention_units(1, i * 6, 6, na_scores, na_values, filler(steps), NA_GAPS)
                        pe.wait_ge(gated[1], i * 12 + 12)

                    for s in range(3):
                        project(l, "pairs", 0, s, 2 * s, xn, GROUPS)
                    with pe.Fori(0, 3) as i:
                        pair(i * 2, 0, True)
                        pair(i * 2 + 1, 1, True)
                    pair(6, 0, True)
                    pair(7, 1, False)
                else:
                    project(l, "lora", 0, 0, 0, xn, GROUPS)
                    parts = ((0, 257), (257, 512))

                    def bank(d, n):
                        return 2 + 3 * d + n

                    def prepare(q):
                        for d in range(2):
                            for j, (at, w) in enumerate(parts):
                                if j == 0:
                                    pe.wait_ge(up_in, q * 16 + 16)
                                    if d == 0:
                                        pe.wait_ge(lora_act, 4)
                                        pe.wait_ge(cols_taken, q * 6 + (plan[l, "pairs"][1] + 6))
                                    else:
                                        pe.wait_ge(kk_max, q * 4 + 2)
                                for b in range(2):
                                    if j:
                                        pe.wait_ge(up_act, q * 8 + (4 * d + b + 1))
                                    r = slice(64 * b, 64 * b + 64)
                                    mm(ps[:, b, 0:w], up[r, d, :], tw[r, d, at:at + w], start=True, stop=True)\
                                        .then_inc(up_done, 1)
                                yield
                            pe.wait_ge(up_act, q * 8 + (4 * d + 4))
                            pe.wait_ge(bon_in, q * 4 + (2 * d + 2))
                            for j, (at, w, part) in enumerate(halves):
                                ins = mm(ps[:, j, 0:w], bones, part, start=True, stop=True)
                            ins.then_inc(bon_ps, 1)
                            yield
                            pe.wait_ge(kk_sq, q * 2 + (d + 1))
                            pe.wait_ge(bon_done, q * 2 + (d + 1))
                            for j, (at, w) in enumerate(parts):
                                ins = mm(ps[:, j, 0:w], bones, tmp[:, at:at + w], start=True, stop=True)
                            ins.then_inc(kk_ss, 1)
                            yield

                    def pair(p, more):
                        queue = iter(project_steps(l, "pairs", [p + 1], 3) if more else ())
                        steps = iter(prepare(p + 1) if more else ())

                        for qn in range(3):
                            gaps = iter(PROJECTION_GAPS if qn < 2 else PREPARE_GAPS)

                            def fill():
                                for _ in range(next(gaps)):
                                    next(queue if qn < 2 else steps, None)

                            def at(per, n):
                                return p * (3 * per) + (qn * per + n)

                            def each(b, d, lhs, rhs_, sem_):
                                for c in range(QUAD):
                                    ins = mm(ps[:, bank(d, b), c * P:(c + 1) * P], lhs(c), rhs_(c), start=True, stop=True)
                                if sem_ is not None:
                                    ins.then_inc(sem_, 1)

                            def turn(b, d, src):
                                for c in range(QUAD):
                                    ins = nc.tensor.transpose(ps[:, bank(d, b), c * P:(c + 1) * P], src[:, d, c, :], ident)
                                ins.then_inc(q_turn, 1)

                            for d in range(2):
                                pe.wait_ge(q_dve, at(4, 2 * d + 2))
                                pe.wait_ge(q_act, at(16, 8 * d + 8))
                                if qn:
                                    pe.wait_ge(c_yt, at(2, -1 + d))
                                each(0, d, lambda c: b_bd[:, d, c, :], lambda c: ar[:, d, c, :], q_pairs)
                                each(1, d, lambda c: k_bd[:, d, c, :], lambda c: ar[:, d, c, :], q_pairs)
                                turn(2, d, b_bd)
                            fill()
                            for d in range(2):
                                pe.wait_ge(q_masked, at(4, 2 * d + 1))
                                turn(0, d, k_bd)
                                pe.wait_ge(q_masked, at(4, 2 * d + 2))
                                turn(1, d, v_bd)
                            fill()
                            for d in range(2):
                                pe.wait_ge(q_levels, at(24, 2 * d + 2))
                                pe.wait_ge(q_turned, at(6, d + 1))
                                each(2, d, lambda c: lev[:, d, 0, c, :], lambda c: ident, i_prod)
                            fill()
                            pe.wait_ge(q_turned, at(6, 6))
                            for v in range(1, LEVELS):
                                for d in range(2):
                                    pe.wait_ge(q_levels, at(24, 4 * v + 2 * d + 2))
                                    pe.wait_ge(i_x, at(22, 3 + d if v == 1 else 4 * (v - 1) + 2 * d + 2))
                                    each(0, d, lambda c: lev[:, d, v % 2, c, :], lambda c: inv[:, d, c, :], i_prod)
                                fill()
                                for d in range(2):
                                    pe.wait_ge(i_taken, at(10, 2 * (v - 1) + d + 1))
                                    last = v == LEVELS - 1
                                    each(1, d, lambda c: prod[:, d, c, :], lambda c: inv_t[:, d, c, :], i_next if last else None)
                                    if not last:
                                        each(2, d, lambda c: inv_t[:, d, c, :], lambda c: prod[:, d, c, :], i_next)
                            for m in range(QUAD):
                                def parts_of(d):
                                    c = m if d == 0 else QUAD - 1 - m
                                    return c, state[:, d, m % 2, :]
                                for d in range(2):
                                    c, st = parts_of(d)
                                    if m == 0:
                                        pe.wait_ge(i_x, at(22, 20 + d + 1))
                                        pe.wait_ge(q_akbd, at(4, 2 * d + 2))
                                        ready = d + 1 if qn < 2 else 0
                                    else:
                                        ready = (2 if qn < 2 else 0) + 2 * (m - 1) + d + 1
                                    pe.wait_ge(c_st, p * 28 + (10 * qn + ready))
                                    mm(ps[:, bank(d, 0), 0:P], a_bd[:, d, c, :], st, start=True, stop=False)
                                    mm(ps[:, bank(d, 0), 0:P], ak_bd[:, d, c, :], vt[:, d, c, :], start=False, stop=True)\
                                        .then_inc(c_r, 1)
                                fill()
                                for d in range(2):
                                    c, st = parts_of(d)
                                    pe.wait_ge(c_rt, at(8, 2 * m + d + 1))
                                    mm(ps[:, bank(d, 0), P:2 * P], inv_t[:, d, c, :], rhs[:, d, c, :], start=True, stop=True)\
                                        .then_inc(c_u, 1)
                                fill()
                                for d in range(2):
                                    c, st = parts_of(d)
                                    out = ps[:, bank(d, 0), 2 * P:3 * P]
                                    pe.wait_ge(c_ut, at(8, 2 * m + d + 1))
                                    mm(out, ident, st, start=True, stop=False)
                                    mm(out, kt[:, d, c, :], vt[:, d, c, :], start=False, stop=False)
                                    mm(out, bt[:, d, c, :], unew[:, d, c, :], start=False, stop=True).then_inc(c_s, 1)
                                for d in range(2):
                                    c, st = parts_of(d)
                                    out = ps[:, bank(d, 1), c * P:(c + 1) * P]
                                    mm(out, st, ar[:, d, c, :], start=True, stop=False)
                                    mm(out, vt[:, d, c, :], ak[:, d, c, :], start=False, stop=False)
                                    mm(out, unew[:, d, c, :], ab[:, d, c, :], start=False, stop=True).then_inc(c_y, 1)
                        pe.wait_ge(c_yt, p * 6 + 6)
                        for j, (at_, w) in enumerate(parts):
                            ins = mm(ps[:, 2 + j, 0:w], bones, ysum[:, at_:at_ + w], start=True, stop=True)
                        ins.then_inc(g_mean, 1)
                        for _ in steps:
                            pass
                        pe.wait_ge(g_sq, p + 1)
                        for j, (at_, w) in enumerate(parts):
                            ins = mm(ps[:, 4 + j, 0:w], bones, gn[:, at_:at_ + w], start=True, stop=True)
                        ins.then_inc(g_var, 1)

                    for s in range(3):
                        project(l, "pairs", 0, s, 2 * s, xn, GROUPS)
                    for _ in prepare(0):
                        pass
                    with pe.Fori(0, 7) as p:
                        pair(p, True)
                    pair(7, False)
                    pe.wait_ge(g_done, 40)

                pe.wait_ge(cols_taken, plan[l, "out"][1])
                if l + 1 < layers:
                    sum_squares(mem_norm(l + 1), [(0, MEM)])
                with pe.Fori(0, 4) as i:
                    for s in range(2):
                        project(l, "out", i, s, 2 * s, br, GROUPS, KB)
                sum_squares(out_norm(l), GROUPS)
                if l + 1 < layers:
                    memory(l + 1)
                    sum_squares(in_norm(l + 1), GROUPS)

        @block.scalar
        def _(act):
            a_ = Serial(act)
            f = nc.scalar.activation

            def wait_cols(l, name, i, c):
                used, chunks, n, tiles, per, _ = plan[l, name]
                act.wait_ge(cols_done, i * per + chunks + c + 1)

            def take(l, name, i, c, dst, func, **kw):
                wait_cols(l, name, i, c)
                a_.do(cols_taken, f(dst, ps[:, c % 2, 0:dst.shape[-1]], func, **kw))

            def squares(q, src, w, ready=None):
                for k in range(KD):
                    if ready is not None:
                        ready(k)
                    if 8 * q + k >= 2:
                        act.wait_ge(sq_used, 8 * q + k - 1)
                    a_.go(sq_ready, f(sq[:, k % 2, 0:w], src[:, k, 0:w], ACT.Square))

            def mean_root(q, w):
                act.wait_ge(ms_taken, q + 1)
                a_.go(root, f(rstd[:, 0:w], rstd[:, 0:w], ACT.Sqrt))

            def memory(l):
                for i, dst in enumerate((mk, mvf)):
                    for c in range(2):
                        take(l, "mem", i, c, dst[:, c, :], ACT.Copy)
                act.wait_ge(mv_turned, l + 1)
                a_.go(mv_taken, f(mv[:, :, :].rearrange("p m c -> p (m c)"),
                                  ps[:, 2:4, :].rearrange("p b c -> p (b c)"), ACT.Copy))

            def takes_of(steps_at, takes):
                count = [0, 0]

                def after(n):
                    count[0] += n
                    while count[1] < min(count[0] // KD, len(takes)):
                        takes[count[1]]()
                        count[1] += 1
                after(steps_at)
                return after

            def attention_units(a, first, n, src, after, gaps):
                def exp(u):
                    act.wait_ge(sc_max[a], first + (u + 1))
                    for h in range(2):
                        a_.do(ex_done[a], f(exps[:, u % 2, h * 256:(h + 1) * 256], src(u, h), ACT.Exp,
                                            bias=stat[:, u % 2, h:h + 1], accum_out=stat[:, u % 2, 2 + h:3 + h]))

                exp(0)
                for u in range(n):
                    if u + 1 < n:
                        if u >= 1:
                            act.wait_ge(tp_done[a], first + u)
                        exp(u + 1)
                    after(gaps[2 * u])
                    act.wait_ge(tp_done[a], first + (u + 1))
                    if u >= 1:
                        act.wait_ge(av_done[a], first + u)
                    a_.do(pt_done[a], f(probs_t[:, :], ps[:, 4, :], ACT.Copy))
                    after(gaps[2 * u + 1])

            act.wait_ge(mem_in, 16)
            squares(mem_norm(0), memn, MEM)
            mean_root(mem_norm(0), MEM)
            act.wait_ge(x_in, 16)
            squares(in_norm(0), xT, T)
            memory(0)
            mean_root(in_norm(0), T)
            for l in range(layers):
                kind = KINDS[l]
                for s in range(2):
                    for g in range(2):
                        take(l, "q", 0, 2 * s + g, mq[:, s, tok(g)], ACT.Copy, scale=HEAD_SCALE)
                for s in range(2):
                    for g in range(2):
                        take(l, "q", 1, 2 * s + g, br[:, KD + s, tok(g)], ACT.Silu)
                if kind == 0:
                    la = l // 3

                    def glu(i):
                        act.wait_ge(glu_done, 2 * i + (16 * la + la + 1))
                        for g in range(2):
                            take(l, "pairs", i, g, z_in[:, tok(g)], ACT.Copy)
                        for g in range(2):
                            take(l, "pairs", i, 2 + g, z_gate[:, tok(g)], ACT.Sigmoid)
                    a_.loop(8, [(cols_taken, 4)], glu)

                def take_gate(i, s, g):
                    return lambda: take(l, "gates", i, 2 * s + g, br[:, 2 * i + s, tok(g)], ACT.Silu)
                after = takes_of(GATES_AHEAD[kind], [take_gate(i, s, g) for i in range(4) for s in range(2) for g in range(2)])
                attention_units(0, 12 * l, 12, lambda u, h: ps[:, score_bank(u) + h, 0:256], after, GATE_GAPS[kind])

                if kind == 0:
                    for k in range(KD):
                        act.wait_ge(centred, 8 * la + k + 1)
                        if k >= 2:
                            act.wait_ge(lsq_used, 8 * la + k - 1)
                        a_.do(lsq_ready, f(sq[:, k % 2, 0:CONV_OUT], z_out[:, k, :], ACT.Square))
                    act.wait_ge(l_ms, la + 1)
                    a_.do(l_root, f(rstd[:, 0:CONV_OUT], rstd[:, 0:CONV_OUT], ACT.Sqrt))
                    for k in range(KD):
                        act.wait_ge(l_scaled, 8 * la + k + 1)
                        b = k * APAR + TAPS
                        a_.do(l_silu, f(z_out[:, k, :], z_out[:, k, :], ACT.Silu, scale=apar[:, b + 1:b + 2],
                                        bias=apar[:, b + 2:b + 3]))
                elif kind == 2:
                    def take_q(i, par, g):
                        cols = 16 if g else 32
                        wait_cols(l, "pairs", i, g)
                        a_.do(cols_taken, f(
                            na_q[:, par, tok(g)].rearrange("p (i r c) -> p r i c", c=cols, i=64 // cols),
                            ps[:, g, 0:GROUPS[g][1]].rearrange("p (r i c) -> p r i c", c=cols, i=64 // cols),
                            ACT.Copy, scale=HEAD_SCALE))

                    def take_windows(i, par):
                        wait_cols(l, "pairs", i, 5)
                        for w, start in enumerate(KEY_START):
                            a_.go(v_window if w < 3 else cols_taken, f(
                                na_v[:, par, w, :].rearrange("p (r c) -> p r c", c=32),
                                ps[:, 1, :].rearrange("p (r c) -> p r c", c=64)[:, :, start:start + 32], ACT.Copy))

                    def takes(i, par):
                        return [lambda: take_q(i, par, 0), lambda: take_q(i, par, 1),
                                lambda: take(l, "pairs", i, 2, na_k[:, par, tok(0)], ACT.Copy),
                                lambda: take(l, "pairs", i, 3, na_k[:, par, tok(1)], ACT.Copy),
                                lambda: take(l, "pairs", i, 4, na_v[:, par, 4, :], ACT.Copy),
                                lambda: take_windows(i, par)]

                    def na(i, par, more):
                        act.wait_ge(vt_turned, i + 1)
                        flat = na_vt[:, :, :].rearrange("p w c -> p (w c)")
                        for b, w in ((0, 512), (1, 512), (2, 256)):
                            a_.do(vt_taken, f(flat[:, 512 * b:512 * b + w], ps[:, 2 + b, 0:w], ACT.Copy))
                        after = takes_of(0, takes(i + 1, 1 - par) if more else [])
                        attention_units(1, i * 6, 6, lambda u, h: scores[:, u % 2, h * 256:(h + 1) * 256], after, NA_GAPS)

                    for chunk in takes(0, 0):
                        chunk()

                    def two(i):
                        na(i * 2, 0, True)
                        na(i * 2 + 1, 1, True)
                    a_.loop(3, [(cols_taken, 12), (v_window, 6), (vt_taken, 6), (ex_done[1], 24), (pt_done[1], 12)], two)
                    na(6, 0, True)
                    na(7, 1, False)
                else:
                    act.wait_ge(w_zero, 2)
                    for g in range(2):
                        take(l, "lora", 0, g, lora[:, 1 + WKV_AT[g]:1 + WKV_AT[g] + GROUPS[g][1]], ACT.Copy)
                    for d in range(2):
                        act.wait_ge(lora_mix, 2 * d + 2)
                        a_.do(lora_act, f(tw[0:64, d, :], tw[0:64, d, :], ACT.Tanh))
                        a_.do(lora_act, f(tw[64:128, d, :], tw[64:128, d, :], ACT.Copy))

                    act.wait_ge(lora_mix, 3)

                    def take_pair(p, c):
                        n, g = c // 2, c % 2
                        take(l, "pairs", p, c, h_p[:, n, 1 + WKV_AT[g]:1 + WKV_AT[g] + GROUPS[g][1]], ACT.Copy)

                    def prepare(q, first=False):
                        act.wait_ge(par_ready, q + 1)
                        if not first:
                            act.wait_ge(q_act, q * 48)
                        for d in range(2):
                            if d:
                                act.wait_ge(kk_done, q * 2 + 1)
                            for j, (at, w) in enumerate(((0, 257), (257, 512))):
                                act.wait_ge(up_done, q * 8 + (4 * d + 2 * j + 1))
                                a_.go(up_act, f(sg[:, at:at + w], ps[:, 0, 0:w], ACT.Sigmoid,
                                                bias=par_now[:, W0 + d:W0 + d + 1]))
                                act.wait_ge(up_done, q * 8 + (4 * d + 2 * j + 2))
                                a_.go(up_act, f(av[:, d, at:at + w], ps[:, 1, 0:w], ACT.Sigmoid,
                                                bias=par_now[:, A0 + d:A0 + d + 1]))
                                yield
                            act.wait_ge(less, q * 2 + (d + 1))
                            act.wait_ge(kk_raw, q * 2 + (d + 1))
                            a_.go(kk_sq, f(tmp[:, :], kk[:, :], ACT.Square))
                            a_.go(decays, f(dd[:, :], cum[:, :], ACT.Exp, scale=-DECAY))
                            a_.go(decays, f(dx[:, d, :], dx[:, d, :], ACT.Exp, scale=-DECAY))
                            a_.do(decays, f(cum[:, :], cum[:, :], ACT.Exp, scale=DECAY))
                            yield
                            act.wait_ge(kk_max, q * 4 + (2 * d + 2))
                            a_.do(kk_root, f(tmp[:, :], tmp[:, :], ACT.Sqrt))
                            yield

                    def pair(p, filler):
                        steps = iter(prepare(p + 1) if filler else ())
                        for qn in range(3):
                            def at(per, n):
                                return p * (3 * per) + (qn * per + n)

                            for d in range(2):
                                first = quad_at(d, qn)

                                def quad(buf):
                                    return buf[:, d, first:first + 256].rearrange("p (c t) -> p c t", c=QUAD)
                                if qn == 0:
                                    act.wait_ge(prepared, p * PREPARED + PREPARED)
                                else:
                                    act.wait_ge(c_y, at(8, -2 + d + 1))
                                for dst, src in ((b_bd, av), (k_bd, ke), (v_bd, xv), (a_bd, dx)):
                                    for h in range(2):
                                        r = slice(64 * h, 64 * h + 64)
                                        a_.go(q_act, f(dst[r, d, :, 64 * h:64 * h + 64], quad(src)[r], ACT.Copy))

                            def turned(n, b, d, dst):
                                act.wait_ge(q_turn, at(6, n))
                                a_.go(q_turned, f(dst[:, d, :, :].rearrange("p c t -> p (c t)"), ps[:, 2 + 3 * d + b, :], ACT.Copy))

                            turned(1, 2, 0, bt)
                            turned(2, 2, 1, bt)
                            if qn == 2:
                                next(steps, None)
                            for d in range(2):
                                turned(3 + 2 * d, 0, d, kt)
                                turned(4 + 2 * d, 1, d, vt)
                            for d in range(2):
                                act.wait_ge(q_masked, at(4, 2 * d + 2))
                                for h in range(2):
                                    r = slice(64 * h, 64 * h + 64)
                                    a_.go(q_akbd, f(ak_bd[r, d, :, 64 * h:64 * h + 64], ak[r, d, :, 0:C], ACT.Copy))
                            if qn == 2:
                                next(steps, None)
                            for v in range(1, LEVELS):
                                for d in range(2):
                                    act.wait_ge(i_prod, at(12, 2 * v + d + 1))
                                    a_.go(i_taken, f(prod[:, d, :, :].rearrange("p c t -> p (c t)"), ps[:, 2 + 3 * d, :], ACT.Copy))
                                if qn == 2 and v in (2, 5):
                                    next(steps, None)
                            if filler and qn < 2:
                                take_pair(p + 1, 3 * qn)
                            for m in range(QUAD):
                                for d in range(2):
                                    c = m if d == 0 else QUAD - 1 - m
                                    act.wait_ge(c_r, at(8, 2 * m + d + 1))
                                    a_.go(c_rt, f(rhs[:, d, c, :], ps[:, 2 + 3 * d, 0:P], ACT.Copy))
                                for d in range(2):
                                    c = m if d == 0 else QUAD - 1 - m
                                    act.wait_ge(c_u, at(8, 2 * m + d + 1))
                                    a_.go(c_ut, f(unew[:, d, c, :], ps[:, 2 + 3 * d, P:2 * P], ACT.Copy, scale=-1.0))
                                if qn == 2 and m < 2:
                                    next(steps, None)
                                if filler and qn < 2 and m == 1:
                                    take_pair(p + 1, 3 * qn + 1)
                            if filler and qn < 2:
                                take_pair(p + 1, 3 * qn + 2)
                        next(steps, None)
                        act.wait_ge(g_centred, p * 2 + 2)
                        a_.do(g_sq, f(gn, ysum[:, :], ACT.Square))
                        for _ in steps:
                            pass
                        act.wait_ge(g_eps, p * 2 + 2)
                        a_.do(g_root, f(gn, gn, ACT.Sqrt))

                    for c in range(6):
                        take_pair(0, c)
                    for _ in prepare(0, True):
                        pass
                    counts = [(cols_taken, 6), (up_act, 8), (kk_sq, 2), (kk_root, 2), (decays, 6), (q_act, 48),
                              (q_turned, 18), (q_akbd, 12), (i_taken, 30), (c_rt, 24), (c_ut, 24), (g_sq, 1), (g_root, 1)]
                    a_.loop(7, counts, lambda p: pair(p, True))
                    pair(7, False)

                def outs(i):
                    for s in range(2):
                        for g in range(2):
                            take(l, "out", i, 2 * s + g, xn[:, 2 * i + s, tok(g)], ACT.Copy)
                if l + 1 < layers:
                    act.wait_ge(mem_in, 16 * (l + 2))
                    squares(mem_norm(l + 1), memn, MEM)
                    mean_root(mem_norm(l + 1), MEM)
                for i in range(4):
                    outs(i)
                q = out_norm(l)
                a_.eng.wait_ge(cols_taken, plan[l, "out"][1] + 16)
                squares(q, xn, T)
                mean_root(q, T)
                if l + 1 < layers:
                    memory(l + 1)
                    squares(in_norm(l + 1), xT, T, lambda k: act.wait_ge(normed, 8 * q + k + 1))
                    mean_root(in_norm(l + 1), T)

        @block.gpsimd
        def _(pool):
            g_ = Serial(pool)
            for l in range(layers):
                if KINDS[l] == 2:
                    pool.wait_ge(mask_in, 16)

                    def add_mask(i, first=False):
                        pool.wait_ge(bias_in, i * 16 + 16)
                        if not first:
                            pool.wait_ge(sc_biased[1], i * 6)
                        g_.do(bm_ready, nc.gpsimd.tensor_tensor(
                            na_bm[:, :, :, :], na_bias[:, :, :, :],
                            na_mask[:, :, :].unsqueeze(2).to_broadcast([P, 5, 2, 256]), ALU.add))
                    add_mask(0, True)
                    g_.loop(7, [(bm_ready, 1)], lambda i: add_mask(i + 1))
                elif KINDS[l] == 1:
                    pool.wait_ge(gated[0], 12 * (l + 1))
                    pool.wait_ge(x_spilled, 16)
                    g_.do(w_zero, nc.gpsimd.memset(h_p[:, :, :], 0.0))
                    for dst in (a_bd, b_bd, k_bd, v_bd, ak_bd, lev):
                        ins = nc.gpsimd.memset(dst[tuple(slice(None) for _ in dst.shape)], 0.0)
                        if dst is lev:
                            g_.do(w_zero, ins)
                        else:
                            ins.then_inc(b_start, 1)
                    pool.wait_ge(b_start, 5)
                    pool.wait_ge(cols_taken, plan[l, "pairs"][1])
                    for d in range(2):
                        g_.do(lora_shift, nc.gpsimd.tensor_tensor(
                            tw[:, d, :], lora[:, 2 * d:2 * d + WT], lora[:, 1:1 + WT], ALU.subtract))

                    def prepare(q, first=False):
                        pool.wait_ge(cols_taken, q * 6 + (plan[l, "pairs"][1] + 6))
                        if not first:
                            pool.wait_ge(q_dve, q * 12)
                            pool.wait_ge(q_act, q * 48)
                        for d in range(2):
                            if d:
                                pool.wait_ge(prepared, q * PREPARED + 2)
                            for n, dst in enumerate((xr[:, d, :], xk[:, :], xv[:, d, :])):
                                g_.do(shifted, nc.gpsimd.tensor_tensor(
                                    dst, h_p[:, n, 2 * d:2 * d + WT], h_p[:, n, 1:1 + WT], ALU.subtract))
                            yield
                            pool.wait_ge(summed, q * 2 + (d + 1))
                            g_.do(less, nc.gpsimd.tensor_tensor(dx[:, d, :], cum[:, :], sg[:, :], ALU.subtract))
                            yield

                    def pair(p, more):
                        steps = iter(prepare(p + 1) if more else ())
                        for qn in range(3):
                            def at(per, n):
                                return p * (3 * per) + (qn * per + n)

                            for v in range(LEVELS):
                                for d in range(2):
                                    if v == 0:
                                        pool.wait_ge(q_masked, at(4, 2 * d + 1))
                                    if v >= 2:
                                        pool.wait_ge(i_prod, at(12, 2 * (v - 2) + d + 1))
                                        pool.wait_ge(i_x, at(22, d + 1))
                                    for h in range(2):
                                        r = slice(64 * h, 64 * h + 64)
                                        g_.do(q_levels, nc.gpsimd.tensor_tensor(
                                            lev[r, d, v % 2, :, 64 * h:64 * h + 64], ab[r, d, :, 0:C],
                                            level[r, d, v, :].unsqueeze(1).to_broadcast([64, QUAD, C]), ALU.mult))
                                if qn == 2 and v in (1, 3):
                                    next(steps, None)
                        for _ in steps:
                            pass
                    for _ in prepare(0, True):
                        pass
                    g_.loop(7, [(shifted, 6), (less, 2), (q_levels, 72)], lambda p: pair(p, True))
                    pair(7, False)

        @block.vector
        def _(dve):
            v_ = Serial(dve)
            ve = nc.vector
            stt = ve.scalar_tensor_tensor

            def norm(q, widths, total, k_op):
                dve.wait_ge(sq_used, 8 * q + 8)
                for j, (at, w) in enumerate(widths):
                    ins = ve.tensor_scalar(rstd[:, at:at + w], ps[:, 6 + j, 0:w], 1.0 / D, RMS_EPS, ALU.mult, ALU.add)
                    if j < len(widths) - 1:
                        v_.do(scaled, ins)
                v_.do(ms_taken, ins)
                dve.wait_ge(root, q + 1)
                v_.do(inverse, ve.reciprocal(rstd[:, 0:total], rstd[:, 0:total]))
                for k in range(KD):
                    k_op(k)
                v_.settle(normed)

            def attention_units(a, first, n, bias_of, gate):
                def top(u):
                    dve.wait_ge(sc_done[a], first + (u + 1))
                    src = ps[:, score_bank(u):score_bank(u) + 2, 0:256]
                    if bias_of:
                        out = scores[:, u % 2, :].rearrange("p (h k) -> p h k", h=2)
                        v_.do(sc_biased[a], ve.tensor_tensor(out, src, bias_of(u), ALU.add))
                        src = out
                    v_.go(sc_max[a], ve.tensor_reduce(out=stat[:, u % 2, 0:2], in_=src,
                                                      op=ALU.max, axis=AX_X, negate=True))

                def gate_(u):
                    dve.wait_ge(av_done[a], first + (u + 1))
                    gate(u)

                top(0)
                for u in range(n):
                    if u + 1 < n:
                        top(u + 1)
                    dve.wait_ge(ex_done[a], (first + (u + 1)) * 2)
                    v_.do(p_inv[a], ve.reciprocal(stat[:, u % 2, 4:6], stat[:, u % 2, 2:4]))
                    v_.go(p_done[a], ve.tensor_tensor(
                        exps[:, u % 2, :].rearrange("p (h k) -> p h k", h=2),
                        exps[:, u % 2, :].rearrange("p (h k) -> p h k", h=2),
                        stat[:, u % 2, 4:6].unsqueeze(2).to_broadcast([P, 2, 256]), ALU.mult))
                    if u:
                        gate_(u - 1)
                gate_(n - 1)

            dve.wait_ge(const_in, 32)
            def scale_by(row, src, dst, w):
                def k_op(k):
                    v_.go(normed, stt(dst[:, k, 0:w], src[:, k, 0:w], gain[:, row * KD + k:row * KD + k + 1],
                                      rstd[:, 0:w], ALU.mult, ALU.mult))
                return k_op

            norm(mem_norm(0), [(0, MEM)], MEM, scale_by(8, memn, memn, MEM))
            norm(in_norm(0), GROUPS, T, scale_by(0, xT, xn, T))
            for l in range(layers):
                kind = KINDS[l]
                if kind == 0:
                    la = l // 3
                    dve.wait_ge(apar_in, 16 * (la + 1))
                    v_.do(glu_done, ve.memset(z_pad[:, :], 0.0))

                    def conv_pair(i):
                        dve.wait_ge(cols_taken, i * 4 + plan[l, "pairs"][1] + 4)
                        for g, (first, n) in enumerate(GROUPS):
                            at = HALO + CONV_AT[g]
                            v_.go(glu_done, ve.tensor_tensor(z_pad[:, at:at + n], z_in[:, first:first + n],
                                                             z_gate[:, first:first + n], ALU.mult))

                        def w(c):
                            return apar[:, bass.ds(i * APAR + c, 1)]
                        for n in range(PE_TAPS):
                            v_.go(diag_done, ve.tensor_scalar(diag[:, n, :], ident, w(TAPS - PE_TAPS + n), None, ALU.mult))
                        v_.settle(glu_done)
                        dst = z_out[:, bass.ds(i, 1), :].rearrange("p a t -> p (a t)")
                        v_.go(conv_taps[0], ve.tensor_scalar(dst, z_pad[:, 0:CONV_OUT], w(0), w(TAPS), ALU.mult, ALU.add))
                        v_.go(conv_taps[1], ve.tensor_scalar(z_odd[:, :], z_pad[:, 1:1 + CONV_OUT], w(1), None, ALU.mult))
                        for c in range(2, TAPS - PE_TAPS):
                            to = z_odd[:, :] if c % 2 else dst
                            v_.settle(conv_taps[c % 2])
                            v_.go(conv_taps[c % 2], stt(to, z_pad[:, c:c + CONV_OUT], w(c), to, ALU.mult, ALU.add))
                        v_.settle(conv_taps[0])
                        v_.settle(conv_taps[1])
                        v_.do(conv_taps[0], ve.tensor_tensor(dst, dst, z_odd[:, :], ALU.add))
                        dve.wait_ge(conv_ps, i + (8 * la + 1))
                        dst2 = z_out[:, bass.ds(i, 1), :].rearrange("p a (j t) -> p (a j) t", j=2)
                        v_.do(conv_done, ve.tensor_tensor(dst2, dst2, ps[:, 2:4, 0:CONV_OUT // 2], ALU.add))
                    on_dve = TAPS - PE_TAPS
                    v_.loop(8, [(glu_done, 2), (diag_done, PE_TAPS), (conv_taps[0], (on_dve + 1) // 2 + 1),
                                (conv_taps[1], on_dve // 2), (conv_done, 1)], conv_pair)
                dve.wait_ge(cols_taken, plan[l, "q"][1] + 8)

                def mem_gate(u):
                    hp, t = u // 6, u % 6
                    dst = br[:, KD + hp, t * P:(t + 1) * P]
                    v_.go(gated[0], ve.tensor_tensor(dst, dst, ps[:, 5, 0:P], ALU.mult))
                attention_units(0, 12 * l, 12, None, mem_gate)

                if kind == 0:
                    la = l // 3
                    half = CONV_OUT // 2
                    dve.wait_ge(mean_done, la + 1)
                    for k in range(KD):
                        v = z_out[:, k, :].rearrange("p (j t) -> p j t", j=2)
                        v_.do(centred, stt(v, ps[:, 2:4, 0:half], -1.0 / D, v, ALU.mult, ALU.add))
                    dve.wait_ge(lsq_used, 8 * (la + 1))
                    v_.do(l_ms, ve.tensor_scalar(rstd[:, 0:CONV_OUT].rearrange("p (j t) -> p j t", j=2), ps[:, 4:6, 0:half],
                                                 1.0 / D, LN_EPS, ALU.mult, ALU.add))
                    dve.wait_ge(l_root, la + 1)
                    v_.do(l_inv, ve.reciprocal(rstd[:, 0:CONV_OUT], rstd[:, 0:CONV_OUT]))
                    for k in range(KD):
                        v_.do(l_scaled, ve.tensor_tensor(z_out[:, k, :], z_out[:, k, :], rstd[:, 0:CONV_OUT], ALU.mult))
                    for k in range(KD):
                        dve.wait_ge(l_silu, 8 * la + k + 1)
                        for g, (first, n) in enumerate(GROUPS):
                            dst = br[:, k, first:first + n]
                            v_.do(l_gated, ve.tensor_tensor(dst, dst, z_out[:, k, CONV_AT[g]:CONV_AT[g] + n], ALU.mult))
                elif kind == 2:
                    def na(i):
                        dve.wait_ge(bm_ready, i + 1)

                        def bias_of(u):
                            return na_bm[:, (0, 1, 1, 2, 3, 4)[u], :, :]

                        def gate(u):
                            for h in range(2):
                                r = slice(64 * h, 64 * h + 64)
                                row = br[r, bass.ds(i, 1), :].rearrange("p a t -> p (a t)")
                                if u >= 4:
                                    dst = row[:, 0:256].rearrange("p (r c) -> p r c", c=64)[:, :, 32 * (u - 4):32 * (u - 4) + 32]
                                else:
                                    dst = row[:, 256:T].rearrange("p (r c) -> p r c", c=64)[:, :, 16 * u:16 * u + 16]
                                o = ps[r, 5, 0:P].rearrange("p (r c) -> p r c", c=32 if u >= 4 else 16)
                                v_.go(gated[1], ve.tensor_tensor(dst, dst, o, ALU.mult))
                        attention_units(1, i * 6, 6, bias_of, gate)
                    v_.loop(8, [(sc_biased[1], 6), (sc_max[1], 6), (p_inv[1], 6), (p_done[1], 6), (gated[1], 12)], na)
                else:
                    dve.wait_ge(bpar_in, 64)
                    v_.do(lora_mix, ve.tensor_scalar(
                        one_minus_ka[:, :].unsqueeze(2), bpar[:, 0:8 * BPAR].rearrange("p (k c) -> p k c", c=BPAR)[:, :, KA:KA + 1],
                        -1.0, 1.0, ALU.mult, ALU.add))
                    for d in range(2):
                        dve.wait_ge(lora_shift, d + 1)
                        v_.do(lora_mix, stt(tw[:, d, :], tw[:, d, :], bpar[:, 8 * BPAR + d:8 * BPAR + d + 1],
                                            lora[:, 1:1 + WT], ALU.mult, ALU.add))
                    v_.do(lora_mix, ve.memset(bonus[:, :], 0.0))

                    def par(p, c):
                        return bpar[:, bass.ds(p * BPAR + c, 1)]

                    def rows(part):
                        return part.rearrange("p (a t) -> p a t", t=256) if part.shape[-1] == 512 else part

                    def prepare(q, first=False):
                        for d in range(2):
                            dve.wait_ge(up_act, q * 8 + (4 * d + 4))
                            if d == 0:
                                v_.go(summed, ve.tensor_tensor_scan(out=cum[:, :], data0=reset[:, 0:WT], data1=sg[:, :],
                                                                    initial=0.0, op0=ALU.mult, op1=ALU.add))
                            else:
                                v_.go(summed, ve.tensor_tensor_scan(out=cum[:, ::-1], data0=reset[:, WT:0:-1],
                                                                    data1=sg[:, ::-1], initial=0.0, op0=ALU.mult, op1=ALU.add))

                            def mix(n, dst):
                                dve.wait_ge(shifted, q * 6 + (3 * d + n + 1))
                                v_.do(mixed, stt(dst, dst, par(q, MU + 3 * d + n), h_p[:, n, 1:1 + WT], ALU.mult, ALU.add))
                            mix(0, xr[:, d, :])
                            yield
                            mix(1, xk[:, :])
                            v_.go(kk_raw, ve.tensor_scalar(kk[:, :], xk[:, :], par(q, KG), None, ALU.mult))
                            mix(2, xv[:, d, :])
                            yield
                            if d == 0 and not first:
                                dve.wait_ge(q_act, q * 48)
                            v_.do(prepared, ve.tensor_scalar(ke[:, d, :], av[:, d, :], par(q, KA), one_minus_ka[:, bass.ds(q, 1)],
                                                             ALU.mult, ALU.add))
                            v_.do(prepared, ve.tensor_tensor(ke[:, d, :], ke[:, d, :], xk[:, :], ALU.mult))
                            for at_, w, part in halves:
                                v_.go(bon_in, stt(part, rows(xr[:, d, at_:at_ + w]), par(q, RK), rows(ke[:, d, at_:at_ + w]),
                                                  ALU.mult, ALU.mult))
                            yield
                            dve.wait_ge(bon_ps, q * 2 + (d + 1))
                            for j, (at_, w, part) in enumerate(halves):
                                dst = rows(bonus[:, at_:at_ + w]) if d == 0 else part
                                ins = ve.tensor_tensor(dst, rows(xv[:, d, at_:at_ + w]), rows(ps[:, j, 0:w]), ALU.mult)
                                if j == 0 or d:
                                    v_.do(prepared, ins)
                            if d == 0:
                                v_.do(bon_done, ins)
                            else:
                                for j, (at_, w, part) in enumerate(halves):
                                    ins = ve.tensor_tensor(rows(bonus[:, at_:at_ + w]), rows(bonus[:, at_:at_ + w]), part, ALU.add)
                                    if j == 0:
                                        v_.do(prepared, ins)
                                v_.do(bon_done, ins)
                            yield
                            dve.wait_ge(kk_ss, q * 2 + (d + 1))
                            for j, (at_, w) in enumerate(((0, 257), (257, 512))):
                                v_.go(kk_max, ve.tensor_scalar(tmp[:, at_:at_ + w], ps[:, j, 0:w], 1e-24, None, ALU.max))
                            yield
                            dve.wait_ge(kk_root, q * 2 + (d + 1))
                            v_.do(prepared, ve.reciprocal(tmp[:, :], tmp[:, :]))
                            v_.do(kk_done, ve.tensor_tensor(kk[:, :], kk[:, :], tmp[:, :], ALU.mult))
                            yield
                            dve.wait_ge(decays, q * 6 + (3 * d + 3))
                            v_.go(prepared, ve.tensor_tensor(av[:, d, :], av[:, d, :], cum[:, :], ALU.mult))
                            v_.go(prepared, ve.tensor_tensor(dx[:, d, :], dx[:, d, :], kk[:, :], ALU.mult))
                            v_.go(prepared, ve.tensor_tensor(ke[:, d, :], ke[:, d, :], cum[:, :], ALU.mult))
                            yield
                            v_.do(prepared, ve.tensor_tensor(xr[:, d, :], xr[:, d, :], dd[:, :], ALU.mult))
                            v_.go(prepared, ve.tensor_tensor(av[:, d, :], av[:, d, :], kk[:, :], ALU.mult))
                            e = C - 1 if d == 0 else 0
                            v_.go(prepared, ve.tensor_copy(dend[:, d, 0:4], dd[:, e:e + 3 * C + 1:C]))
                            v_.do(prepared, ve.tensor_copy(dend[:, d, 4:12], dd[:, 257 + e:257 + e + 7 * C + 1:C]))
                            yield

                    def pair(p, more):
                        if more:
                            v_.go(par_ready, ve.tensor_copy(par_now[:, :], bpar[:, bass.ds((p + 1) * BPAR, BPAR)]))
                        v_.go(y_zero, ve.tensor_copy(dend_now[:, :, :], dend[:, :, :]))
                        v_.go(y_zero, ve.tensor_copy(bonus_now[:, :], bonus[:, :]))
                        v_.do(y_zero, ve.memset(ysum[:, :], 0.0))
                        steps = iter(prepare(p + 1) if more else ())
                        for qn in range(3):
                            def at(per, n):
                                return p * (3 * per) + (qn * per + n)

                            def quad(buf, d):
                                first = quad_at(d, qn)
                                return buf[:, first:first + 256].rearrange("p (c t) -> p c t", c=QUAD)

                            def four(bank):
                                return ps[:, bank, :].rearrange("p (c t) -> p c t", c=QUAD)

                            for d in range(2):
                                v_.go(q_dve, ve.tensor_copy(ar[:, d, :, 0:C], quad(dx[:, d, :], d)))
                                v_.go(q_dve, ve.tensor_copy(ar[:, d, :, C:P], quad(xr[:, d, :], d)))
                            for d in range(2):
                                for n, dst in enumerate((ab, ak)):
                                    dve.wait_ge(q_pairs, at(4, 2 * d + n + 1))
                                    v_.go(q_masked, ve.tensor_tensor(dst[:, d, :, :], four(2 + 3 * d + n),
                                                                     mask[:, d, :].unsqueeze(1).to_broadcast([P, QUAD, P]),
                                                                     ALU.mult))
                            eye = ident.unsqueeze(1).to_broadcast([P, QUAD, P])
                            for d in range(2):
                                dve.wait_ge(q_levels, at(24, 2 * d + 2))
                                v_.go(i_x, ve.tensor_tensor(inv_t[:, d, :, :], eye, lev[:, d, 0, :, :], ALU.subtract))
                            for d in range(2):
                                dve.wait_ge(i_prod, at(12, d + 1))
                                v_.go(i_x, ve.tensor_tensor(inv[:, d, :, :], eye, four(4 + 3 * d), ALU.subtract))
                            if qn == 2:
                                next(steps, None)
                            for v in range(1, LEVELS):
                                for d in range(2):
                                    dve.wait_ge(i_next, at(10, 2 * (v - 1) + d + 1))
                                    for b, dst in ((1, inv_t), (2, inv)):
                                        if b == 1 or v < LEVELS - 1:
                                            flat = dst[:, d, :, :].rearrange("p c t -> p (c t)")
                                            v_.go(i_x, ve.tensor_tensor(flat, flat, ps[:, 2 + 3 * d + b, :], ALU.subtract))
                                if qn == 2:
                                    next(steps, None)
                            if qn < 2:
                                for d in range(2):
                                    v_.go(c_st, ve.memset(state[:, d, 0, :], 0.0))
                            for m in range(QUAD):
                                for d in range(2):
                                    c = m if d == 0 else QUAD - 1 - m
                                    dve.wait_ge(c_s, at(8, 2 * m + d + 1))
                                    n = c + {0: 0, 257: 4, 513: 8}[quad_at(d, qn)]
                                    v_.go(c_st, ve.tensor_scalar(state[:, d, (m + 1) % 2, :], ps[:, 2 + 3 * d, 2 * P:3 * P],
                                                                 dend_now[:, d, n:n + 1], None, ALU.mult))
                                if qn == 2:
                                    next(steps, None)
                            for d in range(2):
                                dve.wait_ge(c_y, at(8, 6 + d + 1))
                                v_.do(c_yt, ve.tensor_tensor(quad(ysum, d), quad(ysum, d), four(3 + 3 * d)[:, :, C:P], ALU.add))
                        next(steps, None)
                        dve.wait_ge(g_mean, p + 1)
                        for j, (at_, w) in enumerate(((0, 257), (257, 512))):
                            v_.go(g_centred, stt(ysum[:, at_:at_ + w], ps[:, 2 + j, 0:w], -1.0 / 64, ysum[:, at_:at_ + w],
                                                 ALU.mult, ALU.add))
                        next(steps, None)
                        next(steps, None)
                        dve.wait_ge(g_var, p + 1)
                        for j, (at_, w) in enumerate(((0, 257), (257, 512))):
                            v_.go(g_eps, ve.tensor_scalar(gn[:, at_:at_ + w], ps[:, 4 + j, 0:w], 1.0 / 64, GN_EPS,
                                                          ALU.mult, ALU.add))
                        next(steps, None)
                        dve.wait_ge(g_root, p + 1)
                        v_.do(g_done, ve.reciprocal(gn, gn))
                        for _ in steps:
                            pass
                        v_.do(g_done, stt(ysum[:, :], ysum[:, :], par(p, LNG), gn, ALU.mult, ALU.mult))
                        v_.do(g_done, stt(ysum[:, :], ysum[:, :], par(p, LNB), bonus_now[:, :], ALU.add, ALU.add))
                        for g, (first, n) in enumerate(GROUPS):
                            dst = br[:, bass.ds(p, 1), first:first + n].rearrange("p a t -> p (a t)")
                            v_.do(g_done, ve.tensor_tensor(dst, dst, ysum[:, WKV_AT[g]:WKV_AT[g] + n], ALU.mult))
                    v_.go(par_ready, ve.tensor_copy(par_now[:, :], bpar[:, 0:BPAR]))
                    for _ in prepare(0, True):
                        pass
                    v_.loop(7, [(par_ready, 1), (y_zero, 3), (mixed, 6), (summed, 2), (kk_raw, 2), (kk_max, 4),
                                (prepared, PREPARED), (bon_in, 4), (bon_done, 2), (kk_done, 2), (q_dve, 12), (q_masked, 12),
                                (i_x, 66), (c_st, 28), (c_yt, 6), (g_centred, 2), (g_eps, 2), (g_done, 5)],
                            lambda p: pair(p, True))
                    pair(7, False)
                    dve.wait_ge(x_back, 16)

                if l + 1 < layers:
                    norm(mem_norm(l + 1), [(0, MEM)], MEM, scale_by(9 + l, memn, memn, MEM))

                def residual(k):
                    v_.do(scaled, stt(xn[:, k, :], xn[:, k, :], gain[:, (4 + l) * KD + k:(4 + l) * KD + k + 1], rstd[:, 0:T],
                                      ALU.mult, ALU.mult))
                    v_.go(normed, ve.tensor_tensor(xT[:, k, :], xT[:, k, :], xn[:, k, :], ALU.add))
                norm(out_norm(l), GROUPS, T, residual)
                if l + 1 < layers:
                    norm(in_norm(l + 1), GROUPS, T, scale_by(l + 1, xT, xn, T))


def _tiles(w):
    k, n = w.shape
    return np.ascontiguousarray(w.reshape(k // P, P, n // P, P).transpose(2, 1, 0, 3).reshape(n // P, P, k))


def _features(v):
    return np.ascontiguousarray(v.reshape(-1, KD, P).transpose(2, 0, 1).reshape(P, -1))


def _acts(a, b):
    both = np.concatenate([a[0], b[0]], 0)
    return np.ascontiguousarray(both.T.reshape(KD, P, -1).transpose(1, 0, 2))


def _pairs(w, skip, names):
    t = _tiles(w)
    body = 8 * names
    rest = t[body + skip:]
    mixer = [t[n * 8 + p] for p in range(8) for n in range(names)]
    rest = np.concatenate([rest[0:2], rest[10:12], rest[2:10]], 0)
    return np.ascontiguousarray(np.concatenate([rest, t[body:body + skip], np.stack(mixer)], 0))


def _constants():
    square = np.zeros((P, 3, P), np.float32)
    square[:, 0] = np.eye(P)
    square[:, 1] = 1
    square[:64, 2, :64] = 1
    square[64:, 2, 64:] = 1
    reset = np.ones((P, WT + 1), np.float32)
    for g, at in enumerate(WKV_AT):
        for c in range(GROUPS[g][1] // C):
            reset[:, at + c * C] = 0
    reset[:, 256] = reset[:, WT] = 0
    j, t = np.arange(C)[:, None], np.arange(C)[None, :]
    mask = np.zeros((P, 2, P), np.float32)
    level = np.zeros((P, 2, LEVELS, C), np.float32)
    for d in range(2):
        a, b = (j, t) if d == 0 else (t, j)
        m = np.concatenate([a < b, a <= b], 1)
        mask[:, d] = np.concatenate([m, m], 0)
        for v in range(LEVELS):
            s = 1 << v
            m = (a // (2 * s) == b // (2 * s)) & ((a // s) % 2 == 0) & ((b // s) % 2 == 1)
            level[:, d, v] = np.concatenate([m, m], 0)
    return square, reset, mask, level


def _windows():
    out = []
    for cols, keys in ((range(0, 16), range(0, 32)), (range(16, 32), range(8, 40)), (range(48, 64), range(32, 64))):
        out.append((np.array([(r, c) for r in range(8) for c in cols]), np.array([(r, c) for r in range(8) for c in keys])))
    for i in range(2):
        out.append((np.array([(r, c) for r in range(4) for c in range(32 * i, 32 * i + 32)]),
                    np.array([(r, c) for r in range(4) for c in range(64)])))
    return out


def _bias(rpb):
    bias = np.zeros((8, P, 5, 2, 256), np.float32)
    mask = np.zeros((P, 5, 256), np.float32)
    for n, (q, k) in enumerate(_windows()):
        dr = k[None, :, 0] - q[:, None, 0] + 7
        dc = np.clip(k[None, :, 1] - q[:, None, 1], -15, 15) + 15
        bias[:, :, n] = rpb.reshape(8, 2, 15, 31)[:, :, dr, dc].transpose(0, 2, 1, 3)
        start = np.clip(q[:, 1] - 8, 0, 48)[:, None]
        mask[:, n] = np.where((k[None, :, 1] >= start) & (k[None, :, 1] < start + 16), 0.0, NEG)
    return bias.reshape(8, P, -1), mask


def _inputs(i):
    a = {k: np.asarray(v) for k, v in i.items()}
    out = {"x": _acts(a["x_prompt"], a["x_sample"]), "mem": _acts(a["mem_prompt"], a["mem_sample"])}
    out["w_mem"] = np.concatenate([_tiles(w) for w in a["w_mem_kv"]], 0)
    out["w_a"] = np.concatenate([_pairs(w, 0, 2) for w in a["a_w_in"]], 0)
    out["w_b"] = _pairs(a["b_w_in"][0], 1, 3)
    out["w_c"] = _pairs(a["c_w_in"][0], 0, 3)
    out["w_out"] = np.concatenate([_tiles(w) for w in (a["a_w_out"][0], a["b_w_out"][0], a["c_w_out"][0], a["a_w_out"][1])], 0)
    out["gains"] = np.concatenate([_features(a[n]) for n in ("pre_norm", "post_norm", "mem_norm")], 1)
    par = []
    for j in range(2):
        rows = np.concatenate([a["a_conv_w"][j], a["a_conv_b"][j:j + 1], a["a_ln_g"][j:j + 1], a["a_ln_b"][j:j + 1]], 0)
        par.append(rows.reshape(APAR, KD, P).transpose(2, 1, 0).reshape(P, -1))
    out["a_par"] = np.stack(par)
    mu = a["b_mu"][0]
    rows = [mu[d, n * D:(n + 1) * D] for d in range(2) for n in range(3)]
    rows += [a["b_w0"][0, 0], a["b_w0"][0, 1], a["b_a0"][0, 0], a["b_a0"][0, 1], a["b_k_k"][0], a["b_k_a"][0],
             a["b_r_k"][0].reshape(-1), a["b_ln_g"][0], a["b_ln_b"][0]]
    rows = np.stack(rows).reshape(BPAR, KD, P).transpose(2, 1, 0).reshape(P, -1)
    out["b_par"] = np.concatenate([rows, mu[:, 3 * D:].T], 1)
    up = np.concatenate([a["b_w_up"][0], a["b_a_up"][0]], 1)
    out["lora_up"] = up.reshape(2, P, 8, P).transpose(2, 1, 0, 3)
    square, reset, mask, level = _constants()
    out["bias"], window = _bias(a["c_rpb"][0])
    out["square_c"], out["scan_c"], out["level_c"], out["window_c0"], out["window_c1"] = square, reset, level, window, mask
    return {k: np.ascontiguousarray(v) for k, v in out.items()}


def _declare(nc, arrays, layers=4):
    ap = {n: nc.dram_tensor(f"in_{n}", v.shape, mybir.dt.from_np(v.dtype), kind="ExternalInput").ap()
          for n, v in arrays.items()}
    y = nc.dram_tensor("out_y", (P, KD, T), F32, kind="ExternalOutput").ap()
    trunk_kernel(nc, ap["x"], ap["mem"], ap["w_mem"], ap["w_a"], ap["w_b"], ap["w_c"], ap["w_out"], ap["gains"], ap["a_par"],
                 ap["b_par"], ap["lora_up"], ap["bias"], ap["square_c"], ap["scan_c"], ap["level_c"],
                 (ap["window_c0"], ap["window_c1"]), y, layers)


def _outputs(y):
    out = y.transpose(1, 0, 2).reshape(D, T).T
    return np.ascontiguousarray(out[None, 0:256]), np.ascontiguousarray(out[None, 256:T])


def kernel(**inputs):
    import concourse.bacc as bacc
    from concourse.bass_utils import run_bass_kernel_spmd as run

    arrays = _inputs(inputs)
    nc = bacc.Bacc("TRN2", target_bir_lowering=False, num_devices=1)
    _declare(nc, arrays)
    r = run(nc, [{f"in_{k}": v for k, v in arrays.items()}], core_ids=[0])
    return _outputs(r.results[0]["out_y"])
```
